# Optimizing a Trainium2 kernel written in Bass

```python
import jax, jax.numpy as jnp
from jax import lax
import numpy as np

D_MODEL = 1024
BATCH = 1
SEQ = 256
DEPTH = 1
DEC_BATCH = 1
DEC_SEQ = 2048
PAST_LEN = 512

GRID_W = 64
N_HEADS_GLA = 4
HEAD_DK = 128
HEAD_DV = 256
GLA_KDIM = N_HEADS_GLA * HEAD_DK
GLA_VDIM = N_HEADS_GLA * HEAD_DV
GATE_RANK = 16
GATE_NORM = 16.0
CHUNK = 64
N_FGROUPS = 4
FGROUP_CH = 128
FOURIER_DIM = N_FGROUPS * FGROUP_CH
ROPE_BASE = 10000.0
EPS = 1e-6
IN_DIM = 2 * GLA_KDIM + 2 * GLA_VDIM + 2 * GATE_RANK + 2 * FOURIER_DIM + 2 * D_MODEL

kernel_name = "hybrid_gla_fnet_diffusion_step"

def _rmsnorm(x, g):
    xf = x.astype(jnp.float32)
    xf = xf * lax.rsqrt(jnp.mean(xf * xf, axis=-1, keepdims=True) + EPS)
    return xf.astype(x.dtype) * g

def _grid_rope(n_tokens):
    rows = n_tokens // GRID_W
    r = jnp.repeat(jnp.arange(rows), GRID_W).astype(jnp.float32)
    col = jnp.tile(jnp.arange(GRID_W), rows).astype(jnp.float32)
    n_freq = HEAD_DK // 4
    freqs = ROPE_BASE ** (-jnp.arange(n_freq, dtype=jnp.float32) / n_freq)
    ang = jnp.concatenate([r[:, None] * freqs, col[:, None] * freqs], axis=-1)
    return jnp.cos(ang), jnp.sin(ang)

def _apply_rope(x, cos, sin):
    B, T, H, Dk = x.shape
    nf = Dk // 4
    xr = x.reshape(B, T, H, 2, 2, nf)
    x1, x2 = xr[..., 0, :], xr[..., 1, :]
    c = cos.reshape(T, 2, nf)[None, :, None].astype(x.dtype)
    s = sin.reshape(T, 2, nf)[None, :, None].astype(x.dtype)
    out = jnp.stack([x1 * c - x2 * s, x2 * c + x1 * s], axis=-2)
    return out.reshape(B, T, H, Dk)

def _gla_scan(q, k, v, g, s0):
    B, T, H, Dk = q.shape
    Dv = v.shape[-1]
    n = T // CHUNK
    f32 = jnp.float32
    qc = q.astype(f32).reshape(B, n, CHUNK, H, Dk)
    kc = k.astype(f32).reshape(B, n, CHUNK, H, Dk)
    vc = v.astype(f32).reshape(B, n, CHUNK, H, Dv)
    bc = jnp.cumsum(g.astype(f32).reshape(B, n, CHUNK, H, Dk), axis=2)
    b_last = bc[:, :, -1]
    q_dec = qc * jnp.exp(bc)
    k_inv = kc * jnp.exp(-bc)
    mask = jnp.tril(jnp.ones((CHUNK, CHUNK), dtype=bool))
    scores = jnp.where(mask, jnp.einsum('bnihd,bnjhd->bnhij', q_dec, k_inv), 0.0)
    o_intra = jnp.einsum('bnhij,bnjhe->bnihe', scores, vc)
    k_to_end = kc * jnp.exp(b_last[:, :, None] - bc)
    d_state = jnp.einsum('bnjhd,bnjhe->bnhde', k_to_end, vc)
    decay = jnp.exp(b_last)

    def step(s, inp):
        dec, ds = inp
        return dec[..., None] * s + ds, s

    s_final, s_prev = lax.scan(step, s0.astype(f32),
                               (jnp.moveaxis(decay, 1, 0), jnp.moveaxis(d_state, 1, 0)))
    s_prev = jnp.moveaxis(s_prev, 0, 1)
    o_inter = jnp.einsum('bnihd,bnhde->bnihe', q_dec, s_prev)
    o = (o_intra + o_inter).reshape(B, T, H, Dv)
    return o, s_final

def _layer(x, cond, s_f0, s_b0, rope, w_ada, b_ada, norm_g, w_in, w_af, b_af, w_ab, b_ab,
           gla_norm_g, w_four, w_proj_a, w_proj_b, w_out):
    B, T, _ = x.shape
    ada = jax.nn.silu(cond) @ w_ada + b_ada
    shift, scale, gate = jnp.split(ada, 3, axis=-1)
    h = _rmsnorm(x, norm_g) * (1 + scale[:, None]) + shift[:, None]
    z = h @ w_in
    sizes = (GLA_KDIM, GLA_KDIM, GLA_VDIM, GLA_VDIM, GATE_RANK, GATE_RANK,
             FOURIER_DIM, FOURIER_DIM, D_MODEL, D_MODEL)
    idx = [int(i) for i in np.cumsum(sizes)[:-1]]
    q, k, v, gate_a, r_f, r_b, u, gate_b, mg_a, mg_b = jnp.split(z, idx, axis=-1)

    q = q.reshape(B, T, N_HEADS_GLA, HEAD_DK)
    k = k.reshape(B, T, N_HEADS_GLA, HEAD_DK)
    v = v.reshape(B, T, N_HEADS_GLA, HEAD_DV)
    if rope is not None:
        q = _apply_rope(q, rope[0], rope[1])
        k = _apply_rope(k, rope[0], rope[1])
    q = q * (HEAD_DK ** -0.5)
    g_f = (jax.nn.log_sigmoid((r_f @ w_af + b_af).astype(jnp.float32)) / GATE_NORM).reshape(B, T, N_HEADS_GLA, HEAD_DK)
    g_b = (jax.nn.log_sigmoid((r_b @ w_ab + b_ab).astype(jnp.float32)) / GATE_NORM).reshape(B, T, N_HEADS_GLA, HEAD_DK)
    o_f, s_f = _gla_scan(q, k, v, g_f, s_f0)
    o_b, s_b = _gla_scan(q[:, ::-1], k[:, ::-1], v[:, ::-1], g_b[:, ::-1], s_b0)
    o = (o_f + o_b[:, ::-1]).astype(x.dtype)
    o = _rmsnorm(o, gla_norm_g).reshape(B, T, GLA_VDIM) * jax.nn.silu(gate_a)
    y_a = o @ w_proj_a

    uf = u.reshape(B, T, N_FGROUPS, FGROUP_CH).astype(jnp.float32)
    four = jnp.real(jnp.fft.fft2(uf, axes=(1, 3), norm="ortho")).astype(x.dtype)
    four = jnp.einsum('btgc,gcd->btgd', four, w_four).reshape(B, T, FOURIER_DIM) * jax.nn.silu(gate_b)
    y_b = four @ w_proj_b

    merged = jax.nn.sigmoid(mg_a) * y_a + jax.nn.sigmoid(mg_b) * y_b
    x = x + gate[:, None] * (merged @ w_out)
    return x, s_f, s_b

def setup_inputs(seed: int = 0) -> dict:
    key = jax.random.key(seed)
    ks = jax.random.split(key, 24)
    f32 = jnp.float32
    nrm = lambda k, shape, s: jax.random.normal(k, shape, f32) * s
    st_shape = (DEC_BATCH, DEPTH, N_HEADS_GLA, HEAD_DK, HEAD_DV)
    return {
        "x_prompt": nrm(ks[0], (BATCH, SEQ, D_MODEL), 1.0),
        "x_sample": nrm(ks[1], (DEC_BATCH, DEC_SEQ, D_MODEL), 1.0),
        "state_gla_fwd": nrm(ks[2], st_shape, 1.0),
        "state_gla_bwd": nrm(ks[3], st_shape, 1.0),
        "c": nrm(ks[4], (DEC_BATCH, D_MODEL), 1.0),
        "c_ctx": nrm(ks[5], (D_MODEL,), 1.0),
        "w_ada": nrm(ks[6], (DEPTH, D_MODEL, 3 * D_MODEL), 0.5 * D_MODEL ** -0.5),
        "b_ada": nrm(ks[7], (DEPTH, 3 * D_MODEL), 0.02),
        "norm_g": 1.0 + nrm(ks[8], (DEPTH, D_MODEL), 0.02),
        "w_in": nrm(ks[9], (DEPTH, D_MODEL, IN_DIM), D_MODEL ** -0.5),
        "w_alpha_fwd": nrm(ks[10], (DEPTH, GATE_RANK, GLA_KDIM), GATE_RANK ** -0.5),
        "b_alpha_fwd": nrm(ks[11], (DEPTH, GLA_KDIM), 0.02),
        "w_alpha_bwd": nrm(ks[12], (DEPTH, GATE_RANK, GLA_KDIM), GATE_RANK ** -0.5),
        "b_alpha_bwd": nrm(ks[13], (DEPTH, GLA_KDIM), 0.02),
        "gla_norm_g": 1.0 + nrm(ks[14], (DEPTH, HEAD_DV), 0.02),
        "w_four": nrm(ks[15], (DEPTH, N_FGROUPS, FGROUP_CH, FGROUP_CH), FGROUP_CH ** -0.5),
        "w_proj_a": nrm(ks[16], (DEPTH, GLA_VDIM, D_MODEL), GLA_VDIM ** -0.5),
        "w_proj_b": nrm(ks[17], (DEPTH, FOURIER_DIM, D_MODEL), FOURIER_DIM ** -0.5),
        "w_out": nrm(ks[18], (DEPTH, D_MODEL, D_MODEL), D_MODEL ** -0.5),
        "final_norm_g": 1.0 + nrm(ks[19], (D_MODEL,), 0.02),
    }

def reference(x_prompt, x_sample, state_gla_fwd, state_gla_bwd, c, c_ctx, w_ada, b_ada, norm_g,
              w_in, w_alpha_fwd, b_alpha_fwd, w_alpha_bwd, b_alpha_bwd, gla_norm_g, w_four,
              w_proj_a, w_proj_b, w_out, final_norm_g):
    b_p = x_prompt.shape[0]
    rope = _grid_rope(x_sample.shape[1])
    hp, hs = x_prompt, x_sample
    new_f, new_b = [], []
    for l in range(DEPTH):
        params = (w_ada[l], b_ada[l], norm_g[l], w_in[l], w_alpha_fwd[l], b_alpha_fwd[l],
                  w_alpha_bwd[l], b_alpha_bwd[l], gla_norm_g[l], w_four[l], w_proj_a[l],
                  w_proj_b[l], w_out[l])
        zeros = jnp.zeros((b_p, N_HEADS_GLA, HEAD_DK, HEAD_DV), jnp.float32)
        hp, sf, sb = _layer(hp, c_ctx[None, :], zeros, zeros, None, *params)
        new_f.append(sf.astype(x_prompt.dtype))
        new_b.append(sb.astype(x_prompt.dtype))
        hs, _, _ = _layer(hs, c, state_gla_fwd[:, l], state_gla_bwd[:, l], rope, *params)
    y_prompt = _rmsnorm(hp, final_norm_g)
    y_sample = _rmsnorm(hs, final_norm_g)
    new_state_fwd = jnp.stack(new_f, axis=1)
    new_state_bwd = jnp.stack(new_b, axis=1)
    return (y_prompt, y_sample, new_state_fwd, new_state_bwd)


_drawn_inputs = setup_inputs


def setup_inputs(seed=0):
    import zlib

    import numpy as np

    out = dict(_drawn_inputs(seed))
    spreads = {}
    factors = {'state_gla_fwd': 8.0,
     'state_gla_bwd': 8.0,
     'b_alpha_fwd': 5.591,
     'b_alpha_bwd': 5.597,
     'gla_norm_g': 8.0,
     'final_norm_g': 2.835}
    for name, (base, spread) in spreads.items():
        noise = np.random.default_rng([zlib.crc32(name.encode()), seed]).standard_normal(out[name].shape)
        drawn = base * np.exp(spread * noise) if base else spread * noise
        out[name] = __import__('jax').numpy.asarray(drawn.astype(out[name].dtype))
    for name, factor in factors.items():
        out[name] = (out[name] * factor).astype(out[name].dtype)
    return out
```

```python
from contextlib import ExitStack

import numpy as np

import concourse.bass as bass
from concourse import mybir

F32 = mybir.dt.float32
F32R = mybir.dt.float32r
BF16 = mybir.dt.bfloat16
U32 = mybir.dt.uint32
ALU = mybir.AluOpType
ACT = mybir.ActivationFunctionType

P = 128
D = 1024
KT = D // P
LAT, CTX = 2048, 256
TOK = LAT + CTX
NT = TOK // P
LT = LAT // P
HEADS, DK, DV = 4, 128, 256
BLOCKS = [(0, 512), (512, 512), (1024, 512), (1536, 512), (2048, 256)]
NB = len(BLOCKS)
RANK = 16
GATE_NORM = 16.0
EPS = 1e-6
GROUPS = 4
N1 = 16
KA = KT + GROUPS
MB = 256
NM = TOK // MB
UNITS = 49

C_COND, C_NG, C_BADA, C_GG, C_BAF, C_BAB, C_ALL = 0, 16, 24, 48, 50, 54, 58
K_ID, K_UP, K_DW, K_ONE, K_ALL = 0, 128, 256, 384, 512


def build(nc, io, scratch):
    q_dram = scratch("qk_dram", [8, P, TOK])
    v_dram = scratch("v_dram", [4, P, NT, DV])
    bc_dram = scratch("bc_dram", [4, P, 2, TOK])
    ga_dram = scratch("ga_dram", [8, P, TOK])
    u_dram = scratch("u_dram", [4, P, TOK])
    gb_dram = scratch("gb_dram", [4, P, TOK])
    mg_dram = scratch("mg_dram", [16, P, TOK])
    og_dram = scratch("og_dram", [8, P, TOK])
    me_dram = scratch("me_dram", [8, P, TOK])

    ctx = ExitStack()
    with ctx:
        base = (nc.sbuf_base + 31) // 32 * 32
        end = nc.sbuf_usable_end

        class Region:

            def __init__(self, start):
                self.at = start

            def __call__(self, name, shape, dt=F32):
                size = int(np.prod(shape[1:])) * (2 if dt == BF16 else 4)
                t = nc.alloc_sbuf_tensor_at(name, shape, dt, offset=self.at)
                self.at += (size + 31) // 32 * 32
                assert self.at <= end, (name, self.at, end)
                return t

        def sem(name):
            return ctx.enter_context(nc.semaphore(name))

        bank = [ctx.enter_context(nc.psum_tensor(f"bank{n}", [P, 512], F32)) for n in range(8)]

        keep = Region(base)
        consts = keep("consts", [P, K_ALL])
        ident = consts[:, K_ID:K_ID + P]
        upper = consts[:, K_UP:K_UP + P].bitcast(U32)
        diag2 = consts[:, K_DW:K_DW + P]
        ones = consts[:, K_ONE:K_ONE + P]
        cols = keep("cols", [P, 64])
        silc = keep("silc", [P, 2, KT])
        modu = keep("modu", [P, 2, 2, KT])
        mid = keep("mid", [P, 8, NT])
        last = keep("last", [P, 8, NT])
        pad = keep("pad", [P, 1])
        kept = keep.at

        act_in = Region(kept)
        h_hi = act_in("h_hi", [P, KT, TOK], F32R)
        adarow = Region(act_in.at)("adarow", [2, 2048])
        h_lo = act_in("h_lo", [P, KT, TOK], F32R)
        after_h = act_in.at
        r0 = Region(after_h)
        wada = r0("wada", [P, 2, KT, 512])
        xt = r0("xt", [P, 4, D])
        h32 = r0("h32", [P, 2, 512])
        rows = h32[0:C_ALL, 0, 0:P]
        sq0 = r0("sq0", [P, 4])
        rs0 = r0("rs0", [P, 4])
        junk = r0("junk", [P, D], BF16)

        r1 = Region(after_h)
        w_hi = [r1("w_hi0", [P, KT, 2 * P], F32R)]
        w_lo = [r1("w_lo0", [P, KT, 2 * P], F32R)]
        second = r1.at
        w_hi.append(r1("w_hi1", [P, KT, 2 * P], F32R))
        w_lo.append(r1("w_lo1", [P, KT, 2 * P], F32R))
        w_raw = r1("w_raw", [P, 2, KT, P])
        stage = r1("stage", [P, NB * 512])
        r_t = r1("r_t", [2 * RANK, TOK])
        rg = Region(second)
        walp = rg("walp", [2 * RANK, 8, P])
        walp_now = rg("walp_now", [2 * RANK, 2, P])
        balp_now = rg("balp_now", [P, 2])
        soft = rg("soft", [P, 512])
        logit = rg("logit", [P, 512])
        cum = rg("cum", [P, 512])
        bcs = rg("bcs", [P, 2, 512])
        assert rg.at <= second + 16384

        def stage_b(b):
            return stage[:, 512 * b:512 * b + BLOCKS[b][1]]

        def stage_v(g):
            return stage[:, 768 * g:768 * g + 768].rearrange("p (t c) -> p t c", t=3)

        r2 = Region(kept)
        rope = r2("rope", [P, 2, TOK])
        x_ld = r2("x_ld", [P, 2, 2, 512])
        bc_ld = r2("bc_ld", [P, 2, 2, 512])
        v_ld = r2("v_ld", [P, 2, 4, DV])
        ga_ld = r2("ga_ld", [P, 2, 2, 512])
        kk = r2("kk", [P, 2, TOK])
        pb = r2("pb", [P, NT, DV])
        pf = r2("pf", [P, 2, DV])
        ex = r2("ex", [P, 2, 2, 512])
        rot = r2("rot", [P, 512])
        roped = r2("roped", [P, 2, 512])
        qd = r2("qd", [P, 2, 2, 512])
        kin = r2("kin", [P, 2, P])
        comb = r2("comb", [P, 2, P])
        ds_t = r2("ds_t", [P, 2, DV])
        junk2 = r2("junk2", [P, DV], BF16)
        rms = r2("rms", [P, 2])
        on = r2("on", [P, 2, DV])
        og = r2("og", [P, 2, 2, 512])
        tf = r2("tf", [P, 2, HEADS, NT])
        fac = r2("fac", [P, 2, HEADS, NT])
        mid_e = r2("mid_e", [P, 2, HEADS, NT])
        fac_now = r2("fac_now", [P, 2, NT])
        mid_now = r2("mid_now", [P, 2, NT])
        s0 = r2("s0", [P, 2, DV])
        fin = r2("fin", [P, 2, DV])

        STEPS = [("b", 3), ("b", 2), ("b", 1), ("b", 0), ("b", 4)] + [("f", b) for b in range(NB)]
        tiles_of = lambda b: list(range(BLOCKS[b][0] // P, (BLOCKS[b][0] + BLOCKS[b][1]) // P))
        chunks_of = [tiles_of(b)[::-1] if way == "b" else tiles_of(b) for way, b in STEPS]
        TERMS = [(x, c) for x, (way, b) in enumerate(STEPS) for c in chunks_of[x]
                 if (way, c) not in (("b", 0), ("f", LT - 1))]
        term = {(STEPS[x][0], c): j for j, (x, c) in enumerate(TERMS)}
        NTERM = len(TERMS)
        B_TERMS = sum(STEPS[x][0] == "b" for x, _ in TERMS)

        def terms_through(x):
            return sum(y <= x for y, _ in TERMS)

        def load_value(head, x):
            per = [16 * (7 if way == "b" else 8) for way, _ in STEPS]
            return head * sum(per[x % 2::2]) + sum(per[x % 2:x + 1:2])

        r3 = Region(kept)
        uf = r3("uf", [P, GROUPS, TOK])
        after_uf = r3.at
        zb = r3("zb", [P, NT, 2, 512])
        sb = r3("sb", [P, N1, 2, 512])
        dft = r3("dft", [P, 2, N1, P])
        dft_c = r3("dft_c", [P, 2, CTX // P, CTX])
        chan = r3("chan", [P, 2, P])
        w4 = r3("w4", [P, GROUPS, P])
        cw = r3("cw", [P, GROUPS, 2, P])

        r4 = Region(after_uf)
        pw_hi = r4("pw_hi", [P, KA, D], F32R)
        pw_lo = r4("pw_lo", [P, KA, D], F32R)
        og_ld = r4("og_ld", [P, KT, MB])
        mg_ld = r4("mg_ld", [P, 4, 2, MB])
        me_st = r4("me_st", [P, 4, MB])
        in_hi = r4("in_hi", [P, KA, MB], F32R)
        in_lo = r4("in_lo", [P, KA, MB], F32R)
        pw_raw = Region(r4.at)("pw_raw", [P, 3, D])
        in_hi = [in_hi, r4("in_hi1", [P, KA, MB], F32R)]
        in_lo = [in_lo, r4("in_lo1", [P, KA, MB], F32R)]

        r5 = Region(kept)
        ow_hi = r5("ow_hi", [P, KT, D], F32R)
        ow_lo = r5("ow_lo", [P, KT, D], F32R)
        ow_raw = r5("ow_raw", [P, 3, D])
        me_ld = r5("me_ld", [P, KT, MB])
        me_hi = [r5(f"me_hi{n}", [P, KT, MB], F32R) for n in range(2)]
        me_lo = [r5(f"me_lo{n}", [P, KT, MB], F32R) for n in range(2)]
        x_in = r5("x_in", [P, 2, D])
        yt = r5("yt", [P, 2, D])
        gate_w = r5("gate_w", [P, 2, KT, 512])
        gate_b = r5("gate_b", [P, D])
        res_gate = r5("res_gate", [P, 2, D])
        fng = r5("fng", [P, D])
        silb = r5("silb", [P, 2, KT, P])
        junk3 = r5("junk3", [P, D], BF16)
        rms3 = r5("rms3", [P, 2, 2])

        s_const, s_rows = sem("s_const"), sem("s_rows")
        s_x = [sem(f"s_x{n}") for n in range(4)]
        s_wada = [sem(f"s_wada{n}") for n in range(2)]
        s_rowt, s_cols, s_silc = sem("s_rowt"), sem("s_cols"), sem("s_silc")
        s_ada, s_adar, s_adat, s_mod = sem("s_ada"), sem("s_adar"), sem("s_adat"), sem("s_mod")
        s_ssq, s_root, s_rs, s_xn = sem("s_ssq"), sem("s_root"), sem("s_rs"), sem("s_xn")
        s_xt, s_h32, s_hhi, s_hlo = sem("s_xt"), sem("s_h32"), sem("s_hhi"), sem("s_hlo")
        s_wraw = [sem(f"s_wraw{n}") for n in range(2)]
        s_whi, s_wlo = sem("s_whi"), sem("s_wlo")
        s_mm = sem("s_mm")
        s_ev = sem("s_ev")
        s_st = [sem(f"s_st{n}") for n in range(NB)]
        s_vst = [sem(f"s_vst{n}") for n in range(3)]
        s_wal0, s_wal, s_now = sem("s_wal0"), sem("s_wal"), sem("s_now")
        s_g = sem("s_g")
        s_gabs, s_gexp, s_gln = sem("s_gabs"), sem("s_gexp"), sem("s_gln")
        s_gmin, s_glog, s_gcum, s_bc = sem("s_gmin"), sem("s_glog"), sem("s_gcum"), sem("s_bc")
        s_bst = [sem(f"s_bst{n}") for n in range(2)]

        s_tab, s_s0 = sem("s_tab"), sem("s_s0")
        s_ld = [sem(f"s_ld{n}") for n in range(2)]
        s_tf, s_fac, s_facn, s_p0, s_pz = sem("s_tf"), sem("s_fac"), sem("s_facn"), sem("s_p0"), sem("s_pz")
        s_rot, s_rope, s_ex, s_qd = sem("s_rot"), sem("s_rope"), sem("s_ex"), sem("s_qd")
        s_tr, s_kin, s_ds, s_dt, s_pu = sem("s_tr"), sem("s_kin"), sem("s_ds"), sem("s_dt"), sem("s_pu")
        s_sc, s_cb1, s_cb, s_o = sem("s_sc"), sem("s_cb1"), sem("s_cb"), sem("s_o")
        s_sq2, s_ln2, s_rs2, s_on, s_ot, s_gt = (sem("s_sq2"), sem("s_ln2"), sem("s_rs2"), sem("s_on"), sem("s_ot"),
                                                 sem("s_gt"))
        s_ogst = [sem(f"s_ogst{n}") for n in range(2)]
        s_fst = sem("s_fst")

        s_ftab, s_u, s_gb = sem("s_ftab"), sem("s_u"), sem("s_gb")
        s_cwm, s_cw, s_zm, s_z = sem("s_cwm"), sem("s_cw"), sem("s_zm"), sem("s_z")
        s_l1, s_l2, s_l3, s_l4 = sem("s_l1"), sem("s_l2"), sem("s_l3"), sem("s_l4")
        s_p1, s_p2, s_p3, s_p4 = sem("s_p1"), sem("s_p2"), sem("s_p3"), sem("s_p4")
        s_tw, s_twd, s_cx, s_f, s_fo = sem("s_tw"), sem("s_twd"), sem("s_cx"), sem("s_f"), sem("s_fo")
        s_pwr = [sem(f"s_pwr{n}") for n in range(3)]
        s_pwh, s_pwl = sem("s_pwh"), sem("s_pwl")
        s_og = [sem(f"s_og{n}") for n in range(2)]
        s_mg = [sem(f"s_mg{n}") for n in range(4)]
        s_mest = [sem(f"s_mest{n}") for n in range(4)]
        s_ih, s_il, s_y, s_yg, s_me = sem("s_ih"), sem("s_il"), sem("s_y"), sem("s_yg"), sem("s_me")
        s_owr = [sem(f"s_owr{n}") for n in range(3)]
        s_gw = [sem(f"s_gw{n}") for n in range(2)]
        s_row3 = sem("s_row3")
        s_owh, s_owl, s_silb, s_gm3, s_gate = sem("s_owh"), sem("s_owl"), sem("s_silb"), sem("s_gm3"), sem("s_gate")
        s_mel, s_mh, s_ml, s_out, s_og3 = sem("s_mel"), sem("s_mh"), sem("s_ml"), sem("s_out"), sem("s_og3")
        s_xin = [sem(f"s_xin{n}") for n in range(2)]
        s_yst = [sem(f"s_yst{n}") for n in range(2)]
        s_add, s_sq3, s_ln3, s_rs3, s_yn = sem("s_add"), sem("s_sq3"), sem("s_ln3"), sem("s_rs3"), sem("s_yn")

        A_QK = NB
        A_V = A_QK + 8 * NB
        A_GA = A_V + 4 * NT
        A_END = A_GA + 32 * NB
        SECTIONS = ((ga_dram, ACT.Silu, 0, 4), (u_dram, ACT.Copy, 8, 2), (gb_dram, ACT.Silu, 12, 2),
                    (mg_dram, ACT.Sigmoid, 16, 8))

        Z_ORDER = [4 * a + n for n in range(4) for a in range(4)] + list(range(LT, NT))

        def sums(eng, z, s):
            for n in range(4):
                ins = eng.tensor_tensor(s[n], z[n // 2], z[n // 2 + 2], ALU.subtract if n % 2 else ALU.add)
            return ins

        def turns(eng, s, out):
            eng.tensor_tensor(out[0], s[0], s[2], ALU.add)
            eng.tensor_tensor(out[2], s[0], s[2], ALU.subtract)
            for n, (first, other) in ((1, (ALU.add, ALU.subtract)), (3, (ALU.subtract, ALU.add))):
                eng.tensor_tensor(out[n][:, 0, :], s[1][:, 0, :], s[3][:, 1, :], first)
                ins = eng.tensor_tensor(out[n][:, 1, :], s[1][:, 1, :], s[3][:, 0, :], other)
            return ins

        block = ctx.enter_context(nc.Block())

        @block.sync
        def _(sp):
            sp.dma_start(consts[:, :], io["consts"]).then_inc(s_const, 16)
            at = 0
            for name, n in (("c", 8), ("c_ctx", 8), ("norm_g", 8), ("b_ada", 24), ("gla_norm_g", 2),
                            ("b_alpha_fwd", 4), ("b_alpha_bwd", 4)):
                sp.dma_start(h32[at:at + n, 0, 0:P], io[name]).then_inc(s_rows, 16)
                at += n

            def x_block(b):
                for s in range(BLOCKS[b][1] // P):
                    t = BLOCKS[b][0] // P + s
                    if b:
                        sp.wait_ge(s_xt, KT * b)
                    sp.dma_start(xt[:, s, :], io["x"][t * P:(t + 1) * P, :]).then_inc(s_x[s], 16)

            for n in range(2):
                sp.dma_start(wada[:, n, :, :], io["w_ada"][n]).then_inc(s_wada[n], 16)
            x_block(0)
            for n in range(2, 4):
                sp.wait_ge(s_ada, n - 1)
                sp.dma_start(wada[:, n % 2, :, :], io["w_ada"][n]).then_inc(s_wada[n % 2], 16)
            for b in range(1, NB):
                x_block(b)

            sp.wait_ge(s_xt, KT * NB)
            sp.wait_ge(s_hhi, KT * NB)
            sp.wait_ge(s_hlo, KT * NB)
            for n in range(2):
                sp.dma_start(w_raw[:, (n + 1) % 2, :, :], io["w_in"][n]).then_inc(s_wraw[(n + 1) % 2], 16)
            sp.wait_ge(s_wal0, 1)
            sp.dma_start(walp[0:RANK, 0:4, :], io["w_alpha_fwd"]).then_inc(s_wal, 16)
            sp.dma_start(walp[RANK:2 * RANK, 4:8, :], io["w_alpha_bwd"]).then_inc(s_wal, 16)

            def load_after(slot, n):
                sp.wait_ge(s_wlo, n + 1)
                sp.dma_start(w_raw[:, slot, :, :], io["w_in"][bass.ds(n + 2, 1)].rearrange("o p k c -> p (o k) c")
                             ).then_inc(s_wraw[slot], 16)

            load_after(1, 0)
            for sec in range(2):
                with sp.Fori(0, 2) as i:
                    for u in range(2):
                        head = 2 * i + u
                        unit = 4 * sec + head
                        load_after(u, unit + 1)
                        for b, (t0, n) in enumerate(BLOCKS):
                            sp.wait_ge(s_ev, A_QK + NB * unit + b + 1)
                            sp.dma_start(q_dram[bass.ds(unit, 1), :, t0:t0 + n].rearrange("o p n -> p (o n)"),
                                         stage_b(b)).then_inc(s_st[b], 16)
                            sp.wait_ge(s_bc, NB * unit + b + 1)
                            k = (NB * u + b) % 2
                            sp.dma_start(bc_dram[bass.ds(head, 1), :, sec, t0:t0 + n].rearrange("o p n -> p (o n)"),
                                         bcs[:, k, 0:n]).then_inc(s_bst[k], 16)
            with sp.Fori(0, HEADS) as head:
                for u in range(2):
                    load_after(u, 9 + 2 * head + u)
                for g in range(NT // 3):
                    sp.wait_ge(s_ev, A_V + NT * head + 3 * g + 3)
                    sp.dma_start(v_dram[bass.ds(head, 1), :, 3 * g:3 * g + 3, :].rearrange("o p t c -> p (o t) c"),
                                 stage_v(g % 3)).then_inc(s_vst[g % 3], 16)
            for dst, _, m0, pairs in SECTIONS:
                def store_pair(i, loads):
                    for u in range(2):
                        m = m0 + 2 * i + u
                        if loads:
                            load_after(u, 17 + m)
                        for b, (t0, n) in enumerate(BLOCKS):
                            sp.wait_ge(s_ev, A_GA + NB * m + b + 1)
                            sp.dma_start(dst[bass.ds(2 * i + u, 1), :, t0:t0 + n].rearrange("o p n -> p (o n)"),
                                         stage_b(b)).then_inc(s_st[b], 16)

                final = dst is mg_dram
                with sp.Fori(0, pairs - final) as i:
                    store_pair(i, True)
                if final:
                    store_pair(pairs - 1, False)
            for b in range(NB):
                sp.wait_ge(s_st[b], 16 * 40)
            sp.wait_ge(s_mm, A_END)
            sp.dma_start(rope[:, :, :], io["rope"]).then_inc(s_tab, 16)
            with sp.Fori(0, HEADS) as head:
                sp.wait_ge(s_p0, 3 * head)
                sp.dma_start(s0[:, 0, :], io["state_fwd"][bass.ds(head, 1)].rearrange("o p c -> p (o c)")).then_inc(s_s0, 16)
                sp.dma_start(s0[:, 1, :], io["state_bwd"][bass.ds(head, 1)].rearrange("o p c -> p (o c)")).then_inc(s_s0, 16)

                def load_step(x):
                    way, b = STEPS[x]
                    t0, n = BLOCKS[b]
                    slot, sem_ = x % 2, s_ld[x % 2]
                    if x < 2:
                        sp.wait_ge(s_gt, NT * head)
                    elif x < 7:
                        sp.wait_ge(s_ds, NTERM * head + terms_through(x - 2))
                    else:
                        sp.wait_ge(s_gt, NT * head + chunks_of[x - 2][-1] + 1)
                    src = q_dram[bass.ds(head + (4 if way == "b" else 0), 1)].rearrange("o p n -> p (o n)")
                    for q in range(4):
                        sp.dma_start(x_ld[32 * q:32 * q + 32, slot, 1, 0:n],
                                     src[32 * (q ^ 1):32 * (q ^ 1) + 32, t0:t0 + n]).then_inc(sem_, 16)
                    sp.dma_start(x_ld[:, slot, 0, 0:n], src[:, t0:t0 + n]).then_inc(sem_, 16)
                    sp.dma_start(v_ld[:, slot, 0:n // P, :],
                                 v_dram[bass.ds(head, 1), :, t0 // P:(t0 + n) // P, :].rearrange("o p t c -> p (o t) c")
                                 ).then_inc(sem_, 16)
                    sp.dma_start(bc_ld[:, slot, :, 0:n],
                                 bc_dram[bass.ds(head, 1), :, :, t0:t0 + n].rearrange("o p d n -> p (o d) n")).then_inc(sem_, 16)
                    if way == "f":
                        sp.dma_start(ga_ld[:, slot, :, 0:n],
                                     ga_dram[bass.ds(2 * head, 2), :, t0:t0 + n].rearrange("e p n -> p e n")).then_inc(sem_, 16)

                load_step(0)
                load_step(1)
                for x, (way, b) in enumerate(STEPS):
                    t0, n = BLOCKS[b]
                    if x + 2 < len(STEPS):
                        load_step(x + 2)
                    if way == "f":
                        sp.wait_ge(s_gt, NT * head + chunks_of[x][-1] + 1)
                        sp.dma_start(og_dram[bass.ds(2 * head, 2), :, t0:t0 + n].rearrange("e p n -> p e n"),
                                     og[:, x % 2, :, 0:n]).then_inc(s_ogst[x % 2], 16)
                sp.wait_ge(s_pu, NTERM * head + NTERM)
                sp.dma_start(io["new_fwd"][bass.ds(head, 1)].rearrange("o p c -> p (o c)"), fin[:, 0, :]).then_inc(s_fst, 16)
                sp.dma_start(io["new_bwd"][bass.ds(head, 1)].rearrange("o p c -> p (o c)"), fin[:, 1, :]).then_inc(s_fst, 16)
            sp.wait_ge(s_ogst[0], 16 * 2 * HEADS)
            sp.wait_ge(s_ogst[1], 16 * 3 * HEADS)
            sp.wait_ge(s_fst, 16 * 2 * HEADS)
            sp.wait_ge(s_gt, NT * HEADS)
            sp.dma_start(chan[:, :, :], io["chan"]).then_inc(s_ftab, 16)
            sp.dma_start(w4[:, :, :], io["w_four"]).then_inc(s_ftab, 16)
            for g in range(GROUPS):
                sp.dma_start(uf[:, g, :], u_dram[g]).then_inc(s_u, 16)
            sp.dma_start(dft[:, :, :, :], io["dft"]).then_inc(s_ftab, 16)
            sp.dma_start(dft_c[:, :, :, :], io["dft_c"]).then_inc(s_ftab, 16)
            sp.wait_ge(s_zm, NT)
            for g in range(GROUPS):
                sp.dma_start(uf[:, g, :], gb_dram[g]).then_inc(s_gb, 16)

            sp.wait_ge(s_fo, 17)
            sp.wait_ge(s_f, N1)

            def load_og(b, half):
                k = slice(4 * half, 4 * half + 4)
                t0 = b * MB if isinstance(b, int) else bass.ds(b * MB, MB)
                src = og_dram[k, :, b * MB:b * MB + MB] if isinstance(b, int) else og_dram[k, :, t0]
                sp.dma_start(og_ld[:, k, :], src.rearrange("k p n -> p k n")).then_inc(s_og[half], 16)

            def load_mg(b, j):
                rows = mg_dram[:, :, :].rearrange("(a j) p n -> j p a n", a=2)[j]
                src = rows[:, :, b * MB:b * MB + MB] if isinstance(b, int) else rows[:, :, bass.ds(b * MB, MB)]
                sp.dma_start(mg_ld[:, j % 4, :, :], src).then_inc(s_mg[j % 4], 16)

            for k in range(KA):
                if k >= 3:
                    sp.wait_ge(s_pwl, k - 2)
                sp.dma_start(pw_raw[:, k % 3, :], io["w_proj_a"][k] if k < KT else io["w_proj_b"][k - KT]
                             ).then_inc(s_pwr[k % 3], 16)
                if k == 2:
                    for half in range(2):
                        load_og(0, half)
            for j in range(4):
                load_mg(0, j)

            def merged_block(b, final):
                if not final:
                    for half in range(2):
                        sp.wait_ge(s_il, 3 * b + half + 1)
                        load_og(b + 1, half)
                for j in range(8):
                    sp.wait_ge(s_me, 8 * b + j + 1)
                    sp.dma_start(me_dram[j, :, bass.ds(b * MB, MB)] if not final else me_dram[j, :, b * MB:b * MB + MB],
                                 me_st[:, j % 4, :]).then_inc(s_mest[j % 4], 16)
                    if j < 4:
                        load_mg(b, j + 4)
                    elif not final:
                        load_mg(b + 1, j - 4)

            with sp.Fori(0, NM // 2) as i:
                for u in range(2):
                    merged_block(2 * i + u, False)
            merged_block(NM - 1, True)

            sp.wait_ge(s_y, 8 * NM)
            for k in range(KT):
                if k >= 3:
                    sp.wait_ge(s_owl, k - 2)
                sp.dma_start(ow_raw[:, k % 3, :], io["w_out"][k]).then_inc(s_owr[k % 3], 16)
                if k == 2:
                    sp.wait_ge(s_me, 8 * NM)
                    for n in range(2):
                        sp.dma_start(gate_w[:, n, :, :], io["w_ada"][4 + n]).then_inc(s_gw[n], 16)
                    sp.dma_start(gate_b[:, :], io["b_gate"].to_broadcast([P, D])).then_inc(s_row3, 16)
                    sp.dma_start(fng[:, :], io["final_norm_g"].to_broadcast([P, D])).then_inc(s_row3, 16)
            for j in range(4):
                sp.wait_ge(s_mest[j], 16 * 2 * NM)

            def load_me(b):
                sp.dma_start(me_ld[:, :, :], (me_dram[:, :, 0:MB] if isinstance(b, int) else me_dram[:, :, bass.ds(b * MB, MB)]
                                              ).rearrange("k p n -> p k n")).then_inc(s_mel, 16)

            load_me(0)
            for u in range(2):
                sp.dma_start(x_in[:, u, :], io["x"][u * P:u * P + P, :]).then_inc(s_xin[u], 16)

            def out_block(b, final):
                if not final:
                    sp.wait_ge(s_ml, b + 1)
                    load_me(b + 1)
                for u in range(2):
                    if not final:
                        sp.wait_ge(s_add, 2 * b + u + 1)
                        sp.dma_start(x_in[:, u, :], io["x"][bass.ds((2 * b + u + 2) * P, P), :]).then_inc(s_xin[u], 16)
                for u in range(2):
                    sp.wait_ge(s_yn, 2 * b + u + 1)
                    y = io["y"][bass.ds((2 * b + u) * P, P), :] if not final else io["y"][(2 * b + u) * P:(2 * b + u + 1) * P, :]
                    sp.dma_start(y, yt[:, u, :]).then_inc(s_yst[u], 16)

            with sp.Fori(0, NM // 2) as i:
                for u in range(2):
                    out_block(2 * i + u, False)
            out_block(NM - 1, True)
            for u in range(2):
                sp.wait_ge(s_yst[u], 16 * NM)

        @block.gpsimd
        def _(pool):
            for b, (t0, n) in enumerate(BLOCKS):
                for k in range(KT):
                    e = KT * b + k
                    pool.wait_ge(s_hhi, e + 1)
                    pool.tensor_tensor(h_lo[:, k, t0:t0 + n], h32[:, e % 2, 0:n],
                                       h_hi[:, k, t0:t0 + n].bitcast(F32), ALU.subtract).then_inc(s_hlo, 1)
            pool.wait_ge(s_tab, 16)
            with pool.Fori(0, HEADS) as head:
                for x, (way, b) in enumerate(STEPS):
                    t0, n = BLOCKS[b]
                    slot, step = x % 2, 10 * head + x
                    pool.wait_ge(s_rope, step)
                    pool.wait_ge(s_ld[slot], load_value(head, x))
                    pool.tensor_tensor(rot[:, 0:n], x_ld[:, slot, 1, 0:n], rope[:, 1, t0:t0 + n], ALU.mult).then_inc(s_rot, 1)
                    pool.wait_ge(s_qd, 10 * head + max(x - 1, 0))
                    pool.tensor_tensor(roped[:, slot, 0:n], x_ld[:, slot, 0, 0:n], rope[:, 0, t0:t0 + n],
                                       ALU.mult).then_inc(s_rot, 1)
                    pool.wait_ge(s_rot, 2 * step + 2)
                    pool.tensor_tensor(roped[:, slot, 0:n], roped[:, slot, 0:n], rot[:, 0:n], ALU.add).then_inc(s_rope, 1)
            pool.wait_ge(s_gt, NT * HEADS)
            pool.wait_ge(s_z, 4)
            sums(pool, [zb[:, 4 * a, :, :] for a in range(4)], [sb[:, 4 * a, :, :] for a in range(4)]).then_inc(s_p1, 1)
            pool.wait_ge(s_p1, 1)
            turns(pool, [sb[:, 4 * a, :, :] for a in range(4)], [zb[:, 4 * c, :, :] for c in range(4)]).then_inc(s_p2, 1)
            pool.wait_ge(s_tw, 4)
            pool.wait_ge(s_twd, 3)
            sums(pool, [sb[:, 12 + n, :, :] for n in range(4)], [zb[:, 12 + n, :, :] for n in range(4)]).then_inc(s_p3, 1)
            pool.wait_ge(s_p3, 1)
            turns(pool, [zb[:, 12 + n, :, :] for n in range(4)], [sb[:, 12 + n, :, :] for n in range(4)]).then_inc(s_p4, 1)

            def merge_block(b):
                for j in range(8):
                    pool.wait_ge(s_mest[j % 4], 16 * (2 * b + j // 4))
                    pool.wait_ge(s_yg, 8 + 8 * b + j + 1)
                    pool.tensor_tensor(me_st[:, j % 4, :], mg_ld[:, j % 4, 0, :], mg_ld[:, j % 4, 1, :], ALU.add
                                       ).then_inc(s_me, 1)

            with pool.Fori(0, NM // 2) as i:
                for u in range(2):
                    merge_block(2 * i + u)
            merge_block(NM - 1)

            def add_block(b):
                for u in range(2):
                    pool.wait_ge(s_xin[u], 16 * (b + 1))
                    pool.wait_ge(s_og3, 4 + 2 * b + u + 1)
                    pool.tensor_tensor(yt[:, u, :], yt[:, u, :], x_in[:, u, :], ALU.add).then_inc(s_add, 1)

            with pool.Fori(0, NM // 2) as i:
                for u in range(2):
                    add_block(2 * i + u)
            add_block(NM - 1)

        @block.scalar
        def _(act):
            act.wait_ge(s_cols, 1)
            act.activation(silc[:, :, :], cols[:, C_COND:C_COND + 2 * KT].rearrange("p (s k) -> p s k", s=2),
                           ACT.Silu).then_inc(s_silc, 1)

            def squares(b):
                for s in range(BLOCKS[b][1] // P):
                    act.wait_ge(s_x[s], 16 * (b + 1))
                    if b:
                        act.wait_ge(s_rs, b)
                    act.wait_ge(s_ssq, BLOCKS[b][0] // P + s)
                    act.activation(junk[:, :], xt[:, s, :], ACT.Square, accum_out=sq0[:, s:s + 1]).then_inc(s_ssq, 1)
                tiles = BLOCKS[b][1] // P
                act.wait_ge(s_ssq, BLOCKS[b][0] // P + tiles)
                act.activation(sq0[:, 0:tiles], sq0[:, 0:tiles], ACT.Sqrt, scale=1.0 / D, bias=EPS).then_inc(s_root, 1)

            squares(0)
            for b, (t0, n) in enumerate(BLOCKS):
                for k in range(KT):
                    e = KT * b + k
                    act.wait_ge(s_h32, e + 1)
                    act.activation(h_hi[:, k, t0:t0 + n], h32[:, e % 2, 0:n], ACT.Copy).then_inc(s_hhi, 1)
                if b + 1 < NB:
                    squares(b + 1)

            for b, (t0, n) in enumerate(BLOCKS):
                act.wait_ge(s_mm, b + 1)
                act.activation(r_t[:, t0:t0 + n], bank[b][0:2 * RANK, 0:n], ACT.Copy).then_inc(s_ev, 1)
            act.preload_act_table_set("natural_log_exp_and_others")
            for sec in range(2):
                with act.Fori(0, 2) as i:
                    for u in range(2):
                        unit = 4 * sec + 2 * i + u
                        for b, (t0, n) in enumerate(BLOCKS):
                            e = NB * unit + b
                            act.wait_ge(s_st[b], 16 * unit)
                            act.wait_ge(s_mm, A_QK + e + 1)
                            act.activation(stage_b(b), bank[b][:, 0:n], ACT.Copy,
                                           scale=DK ** -0.5 if sec == 0 else 1.0).then_inc(s_ev, 1)
                            act.wait_ge(s_now, 2 * sec + i + 1)
                            act.wait_ge(s_glog, e)
                            act.wait_ge(s_g, e + 1)
                            act.activation(soft[:, 0:n], bank[5 + (NB * u + b) % 2][:, 0:n], ACT.Abs,
                                           bias=balp_now[:, u:u + 1]).then_inc(s_gabs, 1)
                            act.wait_ge(s_gabs, e + 1)
                            act.activation(soft[:, 0:n], soft[:, 0:n], ACT.Exp, scale=-1.0).then_inc(s_gexp, 1)
                            act.wait_ge(s_gexp, e + 1)
                            act.activation(soft[:, 0:n], soft[:, 0:n], ACT.Ln, bias=1.0).then_inc(s_gln, 1)
            for b in range(NB):
                act.wait_ge(s_st[b], 16 * 8)
            with act.Fori(0, HEADS) as head:
                for t in range(NT):
                    if t % 3 == 0:
                        act.wait_ge(s_vst[t // 3 % 3], 16 * (2 * head + t // 9))
                    act.wait_ge(s_mm, A_V + NT * head + t + 1)
                    act.activation(stage_v(t // 3 % 3)[:, t % 3, :], bank[5 + t % 3][:, 0:DV], ACT.Copy).then_inc(s_ev, 1)
            for g in range(3):
                act.wait_ge(s_vst[g], 16 * 2 * HEADS)
            for _, func, m0, pairs in SECTIONS:
                with act.Fori(0, pairs) as i:
                    for u in range(2):
                        m = m0 + 2 * i + u
                        for b, (t0, n) in enumerate(BLOCKS):
                            act.wait_ge(s_st[b], 16 * (8 + m))
                            act.wait_ge(s_mm, A_GA + NB * m + b + 1)
                            act.activation(stage_b(b), bank[b][:, 0:n], func).then_inc(s_ev, 1)
            act.preload_act_table_set("natural_log_exp_and_others")
            act.wait_ge(s_tf, 3)
            act.activation(fac[:, :, :, :], tf[:, :, :, :], ACT.Exp, scale=1.0 / GATE_NORM).then_inc(s_fac, 1)
            act.activation(mid_e[:, :, :, :].rearrange("p d h c -> p (d h) c"), mid[:, :, :], ACT.Exp, scale=1.0 / GATE_NORM).then_inc(s_fac, 1)
            with act.Fori(0, HEADS) as head:
                def decays(x):
                    way, b = STEPS[x]
                    n, slot = BLOCKS[b][1], x % 2
                    act.wait_ge(s_ld[slot], load_value(head, x))
                    act.wait_ge(s_qd, 10 * head + max(x - 1, 0))
                    act.activation(ex[:, slot, :, 0:n], bc_ld[:, slot, :, 0:n], ACT.Exp,
                                   scale=(-1.0 if way == "b" else 1.0) / GATE_NORM).then_inc(s_ex, 1)

                def k_out(j):
                    act.wait_ge(s_ds, NTERM * head + max(j - 1, 0))
                    act.wait_ge(s_tr, NTERM * head + j + 1)
                    act.activation(kin[:, j % 2, :], bank[6 + (j % 2 if j < B_TERMS else 0)][:, 0:P], ACT.Copy).then_inc(s_kin, 1)

                def term_out(j):
                    x, c = TERMS[j]
                    act.wait_ge(s_pu, NTERM * head + max(j - 1, 0))
                    act.wait_ge(s_ds, NTERM * head + j + 1)
                    act.activation(ds_t[:, j % 2, :], bank[4 + j % 2][:, 0:DV], ACT.Copy,
                                   scale=fac_now[:, 0 if STEPS[x][0] == "f" else 1, c:c + 1]).then_inc(s_dt, 1)

                act.wait_ge(s_facn, head + 1)
                decays(0)
                k_out(0)
                for j in range(B_TERMS):
                    x, c = TERMS[j]
                    if c == chunks_of[x][-2]:
                        decays(x + 1)
                    if j + 1 < B_TERMS:
                        k_out(j + 1)
                    term_out(j)
                k_out(term["f", 0])
                for c in range(NT):
                    x = next(x for x in range(5, 10) if c in chunks_of[x])
                    if c == chunks_of[x][-2] and x + 1 < len(STEPS):
                        decays(x + 1)
                    if ("f", c + 1) in term:
                        k_out(term["f", c + 1])
                    if ("f", c) in term:
                        term_out(term["f", c])
                    e, o = NT * head + c, bank[2 + c % 2][:, 0:DV]
                    act.wait_ge(s_on, e)
                    act.wait_ge(s_o, e + 1)
                    act.activation(junk2[:, :], o, ACT.Square, accum_out=rms[:, 0:1]).then_inc(s_sq2, 1)
                    act.wait_ge(s_sq2, e + 1)
                    act.activation(rms[:, 1:2], rms[:, 0:1], ACT.Ln, scale=1.0 / DV, bias=EPS).then_inc(s_ln2, 1)
                    act.wait_ge(s_ln2, e + 1)
                    act.activation(rms[:, 1:2], rms[:, 1:2], ACT.Exp, scale=-0.5).then_inc(s_rs2, 1)
                    act.wait_ge(s_ot, NT * head + max(c - 1, 0))
                    act.wait_ge(s_rs2, e + 1)
                    act.activation(on[:, c % 2, :], o, ACT.Copy, scale=rms[:, 1:2]).then_inc(s_on, 1)
            act.wait_ge(s_gt, NT * HEADS)
            for n in range(2):
                act.wait_ge(s_cwm, n + 1)
                act.activation(cw[:, 2 * n:2 * n + 2, :, :], bank[n][:, :].rearrange("p (g r c) -> p g r c", g=2, r=2),
                               ACT.Copy).then_inc(s_cw, 1)
            for m, t in enumerate(Z_ORDER):
                act.wait_ge(s_zm, m + 1)
                for h in range(2):
                    ins = act.activation(zb[:, t, :, 256 * h:256 * h + 256].rearrange("p r (g c) -> p g r c", g=2),
                                         bank[2 * (m % 3) + h][:, :].rearrange("p (g r c) -> p g r c", g=2, r=2), ACT.Copy)
                ins.then_inc(s_z, 1)
            for n in (1, 2, 0, 3):
                if n:
                    act.wait_ge(s_l2, n)
                else:
                    act.wait_ge(s_p2, 1)
                for c in range(4):
                    ins = act.activation(sb[:, 4 * c + n, :, :], zb[:, 4 * c + n, :, :], ACT.Copy,
                                         scale=float(np.cos(2 * np.pi * n * c / N1)))
                ins.then_inc(s_tw, 1)

            def high(slot, out, src, value, done):
                act.wait_ge(slot, value)
                act.activation(out, src, ACT.Copy).then_inc(done, 1)

            for k in range(KA):
                high(s_pwr[k % 3], pw_hi[:, k, :], pw_raw[:, k % 3, :], 16 * (k // 3 + 1), s_pwh)

            def high_block(b, slot):
                if not isinstance(b, int):
                    act.wait_ge(s_y, 8 * (b - 1))
                for half in range(2):
                    k = slice(4 * half, 4 * half + 4)
                    high(s_og[half], in_hi[slot][:, k, :], og_ld[:, k, :], 16 * (b + 1), s_ih)
                act.activation(in_hi[slot][:, KT:KA, :], uf[:, :, bass.ds(b * MB, MB)], ACT.Copy).then_inc(s_ih, 1)

            act.wait_ge(s_fo, 17)
            high_block(0, 0)
            act.wait_ge(s_pwl, KA)
            with act.Fori(0, NM // 2) as i:
                for u in range(2):
                    high_block(2 * i + u + 1, 1 - u)

            act.wait_ge(s_me, 8 * NM)
            for k in range(KT):
                high(s_owr[k % 3], ow_hi[:, k, :], ow_raw[:, k % 3, :], 16 * (k // 3 + 1), s_owh)
            high(s_mel, me_hi[0][:, :, :], me_ld[:, :, :], 16, s_mh)

            def root_block(b, slot, final):
                if not final:
                    act.wait_ge(s_out, 2 * b)
                    high(s_mel, me_hi[1 - slot][:, :, :], me_ld[:, :, :], 16 * (b + 2), s_mh)
                for u in range(2):
                    e = 2 * b + u
                    act.wait_ge(s_add, e + 1)
                    act.wait_ge(s_sq3, e)
                    act.wait_ge(s_yn, 2 * b)
                    act.activation(junk3[:, :], yt[:, u, :], ACT.Square, accum_out=rms3[:, u, 0:1]).then_inc(s_sq3, 1)
                    act.wait_ge(s_sq3, e + 1)
                    act.activation(rms3[:, u, 1:2], rms3[:, u, 0:1], ACT.Ln, scale=1.0 / D, bias=EPS).then_inc(s_ln3, 1)
                    act.wait_ge(s_ln3, e + 1)
                    act.activation(rms3[:, u, 1:2], rms3[:, u, 1:2], ACT.Exp, scale=-0.5).then_inc(s_rs3, 1)

            with act.Fori(0, NM // 2) as i:
                for u in range(2):
                    root_block(2 * i + u, u, False)
            root_block(NM - 1, 0, True)

        @block.vector
        def _(dve):
            dve.wait_ge(s_rowt, 1)
            dve.tensor_copy(cols[:, 0:C_ALL], bank[7][:, 0:C_ALL]).then_inc(s_cols, 1)

            def normalise(b):
                tiles = BLOCKS[b][1] // P
                dve.wait_ge(s_root, b + 1)
                dve.wait_ge(s_xn, BLOCKS[b][0] // P)
                dve.reciprocal(rs0[:, 0:tiles], sq0[:, 0:tiles]).then_inc(s_rs, 1)
                dve.wait_ge(s_rs, b + 1)
                for s in range(tiles):
                    dve.tensor_scalar(xt[:, s, :], xt[:, s, :], rs0[:, s:s + 1], None, ALU.mult).then_inc(s_xn, 1)

            normalise(0)
            for n in range(4):
                dve.wait_ge(s_ada, n + 1)
                dve.tensor_copy(adarow[:, n * 512:(n + 1) * 512], bank[n][0:2, :]).then_inc(s_adar, 1)
            dve.wait_ge(s_adat, 1)
            dve.wait_ge(s_cols, 1)
            ada = bank[6][:, 0:32].rearrange("p (j k s) -> p j s k", j=2, s=2)
            bada = cols[:, C_BADA:C_BADA + 16].rearrange("p (j k) -> p j k", j=2)
            for s in range(2):
                dve.tensor_tensor(modu[:, 1, s, :], ada[:, 0, s, :], bada[:, 0, :], ALU.add)
                ins = dve.scalar_tensor_tensor(modu[:, 0, s, :], ada[:, 1, s, :], 1.0, bada[:, 1, :], ALU.add, ALU.add)
            ins.then_inc(s_mod, 1)
            dve.wait_ge(s_mod, 1)
            dve.tensor_tensor(modu[:, 0, :, :], modu[:, 0, :, :],
                              cols[:, C_NG:C_NG + KT].unsqueeze(1).to_broadcast([P, 2, KT]), ALU.mult).then_inc(s_mod, 1)
            dve.wait_ge(s_mod, 2)
            for b, (t0, n) in enumerate(BLOCKS):
                s = 0 if t0 < LAT else 1
                for k in range(KT):
                    e = KT * b + k
                    if e >= 2:
                        dve.wait_ge(s_hhi, e - 1)
                        dve.wait_ge(s_hlo, e - 1)
                    dve.wait_ge(s_xt, e + 1)
                    dve.tensor_scalar(h32[:, e % 2, 0:n], bank[k][:, 0:n], modu[:, 0, s, k:k + 1],
                                      modu[:, 1, s, k:k + 1], ALU.mult, ALU.add).then_inc(s_h32, 1)
                if b + 1 < NB:
                    normalise(b + 1)

            def split(slot, n, landed, pair=0):
                sl = slice(P * slot, P * slot + P)
                dve.wait_ge(s_wraw[slot], 16 * landed)
                dve.tensor_copy(w_hi[pair][:, :, sl], w_raw[:, slot, :, :]).then_inc(s_whi, 1)
                dve.wait_ge(s_whi, n + 1)
                dve.tensor_tensor(w_lo[pair][:, :, sl], w_raw[:, slot, :, :], w_hi[pair][:, :, sl].bitcast(F32),
                                  ALU.subtract).then_inc(s_wlo, 1)

            dve.wait_ge(s_hhi, KT * NB)
            dve.wait_ge(s_hlo, KT * NB)
            dve.memset(walp[:, :, :], 0.0).then_inc(s_wal0, 1)
            split(1, 0, 1)
            split(0, 1, 1)
            dve.wait_ge(s_wal, 32)
            for sec in range(2):
                with dve.Fori(0, 2) as i:
                    for u in range(2):
                        unit = 4 * sec + 2 * i + u
                        dve.wait_ge(s_mm, A_QK + NB * unit)
                        split(1 - u, unit + 2, 2 * sec + i + 2)
                        if u == 0:
                            dve.wait_ge(s_g, NB * unit)
                            dve.wait_ge(s_gabs, NB * unit)
                            dve.tensor_copy(walp_now[:, :, :], walp[:, bass.ds(unit, 2), :])
                            dve.tensor_copy(balp_now[:, :], cols[:, bass.ds(C_BAF + unit, 2)]).then_inc(s_now, 1)
                            dve.wait_ge(s_now, 2 * sec + i + 1)
                        for b, (t0, n) in enumerate(BLOCKS):
                            e = NB * unit + b
                            par, chunks, t = NB * u + b, n // P, t0 // P
                            dve.wait_ge(s_gabs, e + 1)
                            dve.tensor_scalar(logit[:, 0:n], bank[5 + par % 2][:, 0:n], balp_now[:, u:u + 1], 0.0,
                                              ALU.add, ALU.min).then_inc(s_gmin, 1)
                            dve.wait_ge(s_gmin, e + 1)
                            dve.wait_ge(s_gln, e + 1)
                            dve.tensor_tensor(logit[:, 0:n], logit[:, 0:n], soft[:, 0:n], ALU.subtract).then_inc(s_glog, 1)
                            dve.wait_ge(s_glog, e + 1)
                            for c in range(chunks):
                                x, y = logit[:, c * P:c * P + P], cum[:, c * P:c * P + P]
                                if sec:
                                    x, y = x[:, ::-1], y[:, ::-1]
                                ins = dve.tensor_tensor_scan(y, ones, x, 0.0, ALU.mult, ALU.add)
                            ins.then_inc(s_gcum, 1)
                            dve.wait_ge(s_gcum, e + 1)
                            cc = cum[:, 0:n].rearrange("p (c t) -> p c t", t=P)
                            mt, lt = (64, 0) if sec else (63, 127)
                            dve.tensor_copy(mid[:, bass.ds(unit, 1), t:t + chunks].rearrange("p o c -> p (o c)"), cc[:, :, mt])
                            dve.tensor_copy(last[:, bass.ds(unit, 1), t:t + chunks].rearrange("p o c -> p (o c)"), cc[:, :, lt])
                            dve.wait_ge(s_bst[par % 2], 16 * (NB * (2 * sec + i) + par // 2))
                            dve.tensor_tensor(bcs[:, par % 2, 0:n].rearrange("p (c t) -> p c t", t=P), cc,
                                              cc[:, :, mt:mt + 1].to_broadcast([P, chunks, P]),
                                              ALU.subtract).then_inc(s_bc, 1)
            dve.wait_ge(s_mm, A_V)
            split(1, 10, 6)
            for k in range(2):
                dve.wait_ge(s_bst[k], 16 * 4 * NB)
            for h in range(1, HEADS):
                if h > 1:
                    dve.wait_ge(s_mm, A_V + NT * (h - 1))
                for u in range(2):
                    split(u, 9 + 2 * h + u, 5 + h + u, pair=h % 2)
            dve.wait_ge(s_mm, A_GA - NB)
            split(0, 17, 9)
            for _, _, m0, pairs in SECTIONS:
                def split_pair(i, final):
                    for u in range(2):
                        m = m0 + 2 * i + u
                        if final and u:
                            continue
                        dve.wait_ge(s_mm, A_GA + NB * m)
                        split(1 - u, 18 + m, 10 + m0 // 2 + i)

                final = m0 == 16
                with dve.Fori(0, pairs - final) as i:
                    split_pair(i, False)
                if final:
                    split_pair(pairs - 1, True)
            dve.wait_ge(s_mm, A_END)
            dve.wait_ge(s_ev, A_END)
            md = mid[:, :, :].rearrange("p (d h) c -> p d h c", d=2)
            dve.tensor_tensor(tf[:, :, :, :].rearrange("p d h c -> p (d h) c"), last[:, :, :], mid[:, :, :],
                              ALU.subtract).then_inc(s_tf, 1)
            dve.wait_ge(s_tf, 1)
            for n, (d, a, z) in enumerate(((0, 0, LT - 1), (0, LT, NT - 1), (1, 1, LT), (1, LT + 1, NT))):
                step = 1 if d == 0 else -1
                ins = dve.tensor_tensor(tf[:, d, :, a:z], tf[:, d, :, a:z], md[:, d, :, a + step:z + step], ALU.add)
            ins.then_inc(s_tf, 2)
            dve.wait_ge(s_fac, 2)
            with dve.Fori(0, HEADS) as head:
                def prepare(x):
                    way, b = STEPS[x]
                    t0, n = BLOCKS[b]
                    slot, step = x % 2, 10 * head + x
                    if way == "b":
                        out = kk[:, :, t0:t0 + n]
                    else:
                        out = qd[:, slot, :, 0:n]
                        dve.wait_ge(s_o, NT * head + sum(len(chunks_of[y]) for y in range(5, x - 1)))
                    dve.wait_ge(s_ex, step + 1)
                    dve.wait_ge(s_rope, step + 1)
                    dve.tensor_tensor(out, ex[:, slot, :, 0:n], roped[:, slot, 0:n].unsqueeze(1).to_broadcast([P, 2, n]),
                                      ALU.mult).then_inc(s_qd, 1)

                def update(j):
                    x, c = TERMS[j]
                    if STEPS[x][0] == "b":
                        old = pb[:, c, :]
                        new = fin[:, 1, :] if c == LT else pb[:, c - 1, :]
                        d = 1
                    else:
                        old = pf[:, c % 2, :]
                        new = fin[:, 0, :] if c == NT - 1 else pf[:, (c + 1) % 2, :]
                        d = 0
                        dve.wait_ge(s_o, NT * head + max(c, 0))
                    dve.wait_ge(s_pu, NTERM * head + j)
                    dve.wait_ge(s_dt, NTERM * head + j + 1)
                    dve.scalar_tensor_tensor(new, old, fac_now[:, d, c:c + 1], ds_t[:, j % 2, :],
                                             ALU.mult, ALU.add).then_inc(s_pu, 1)

                def combine_backward(c):
                    dve.wait_ge(s_o, NT * head + max(c - 1, 0))
                    dve.wait_ge(s_sc, NT * head + c + 1)
                    dve.tensor_tensor(comb[:, c % 2, :], bank[c % 2][:, P:2 * P], diag2, ALU.mult).then_inc(s_cb1, 1)

                def backward_in_place(c):
                    dve.wait_ge(s_cb1, NT * head + c + 1)

                def combine_forward(c):
                    dve.copy_predicated(comb[:, c % 2, :], upper, bank[c % 2][:, 0:P]).then_inc(s_cb, 1)

                def gate(c):
                    x = next(x for x in range(5, 10) if c in chunks_of[x])
                    at = (c - chunks_of[x][0]) * P
                    if at == 0:
                        dve.wait_ge(s_ogst[x % 2], 16 * ((3 if x % 2 else 2) * head + (x - 5) // 2))
                    dve.wait_ge(s_ot, NT * head + c + 1)
                    for e in range(2):
                        ins = dve.scalar_tensor_tensor(og[:, x % 2, e, at:at + P], bank[7][:, e * P:e * P + P],
                                                       cols[:, C_GG + e:C_GG + e + 1], ga_ld[:, x % 2, e, at:at + P],
                                                       ALU.mult, ALU.mult)
                    ins.then_inc(s_gt, 1)

                dve.wait_ge(s_o, NT * head)
                dve.wait_ge(s_pu, NTERM * head)
                dve.tensor_copy(fac_now[:, :, :], fac[:, :, bass.ds(head, 1), :].rearrange("p d o c -> p (d o) c"))
                dve.tensor_copy(mid_now[:, :, :], mid_e[:, :, bass.ds(head, 1), :].rearrange("p d o c -> p (d o) c")).then_inc(s_facn, 1)
                dve.wait_ge(s_facn, head + 1)
                dve.wait_ge(s_s0, 32 * head + 32)
                dve.tensor_scalar(pb[:, LT - 1, :], s0[:, 1, :], mid_now[:, 1, LT - 1:LT], None, ALU.mult).then_inc(s_p0, 1)
                dve.tensor_scalar(pf[:, 0, :], s0[:, 0, :], mid_now[:, 0, 0:1], None, ALU.mult).then_inc(s_p0, 1)
                dve.memset(pb[:, NT - 1, :], 0.0).then_inc(s_p0, 1)
                dve.wait_ge(s_fst, 32 * head)
                dve.wait_ge(s_p0, 3 * head + 3)
                prepare(0)
                for j in range(B_TERMS):
                    x, c = TERMS[j]
                    if c == chunks_of[x][-2]:
                        prepare(x + 1)
                    update(j)
                combine_backward(0)
                backward_in_place(0)
                dve.memset(pad[:, :], 0.0)
                combine_forward(0)
                for c in range(NT):
                    x = next(x for x in range(5, 10) if c in chunks_of[x])
                    if c == chunks_of[x][-2] and x + 1 < len(STEPS):
                        prepare(x + 1)
                    if c + 1 < NT:
                        combine_backward(c + 1)
                        backward_in_place(c + 1)
                    if ("f", c) in term:
                        update(term["f", c])
                    else:
                        dve.wait_ge(s_o, NT * head + c)
                        dve.memset(pf[:, (c + 1) % 2, :], 0.0).then_inc(s_pz, 1)
                    if c + 1 < NT:
                        combine_forward(c + 1)
                    if c:
                        gate(c - 1)
                gate(NT - 1)
            def butterfly(n):
                dve.wait_ge(s_z, 4 * n + 4)
                sums(dve, [zb[:, 4 * a + n, :, :] for a in range(4)], [sb[:, 4 * a + n, :, :] for a in range(4)]).then_inc(s_l1, 1)
                dve.wait_ge(s_l1, n)
                turns(dve, [sb[:, 4 * a + n, :, :] for a in range(4)], [zb[:, 4 * c + n, :, :] for c in range(4)]).then_inc(s_l2, 1)

            def twiddle(n):
                dve.wait_ge(s_tw, (0, 1, 2, 4)[n])
                for c in range(1, 4):
                    sn = float(np.sin(2 * np.pi * n * c / N1))
                    z, o = zb[:, 4 * c + n, :, :], sb[:, 4 * c + n, :, :]
                    dve.scalar_tensor_tensor(o[:, 0, :], z[:, 1, :], sn, o[:, 0, :], ALU.mult, ALU.add)
                    ins = dve.scalar_tensor_tensor(o[:, 1, :], z[:, 0, :], -sn, o[:, 1, :], ALU.mult, ALU.add)
                ins.then_inc(s_twd, 1)

            def second(c):
                sums(dve, [sb[:, 4 * c + n, :, :] for n in range(4)], [zb[:, 4 * c + n, :, :] for n in range(4)]).then_inc(s_l3, 1)
                dve.wait_ge(s_l3, c + 1)
                turns(dve, [zb[:, 4 * c + n, :, :] for n in range(4)], [sb[:, 4 * c + d, :, :] for d in range(4)]).then_inc(s_l4, 1)

            def gate_latents(c):
                for d in range(4):
                    dve.wait_ge(s_f, 4 * c + d + 1)
                    y = uf[:, :, 0:LAT].rearrange("p g (k s) -> p g s k", s=N1)[:, :, c + 4 * d, :]
                    dve.tensor_tensor(y, bank[4 * (c % 2) + d][:, :].rearrange("p (g k) -> p g k", g=4), y, ALU.mult).then_inc(s_fo, 1)

            butterfly(1)
            butterfly(2)
            twiddle(1)
            butterfly(3)
            twiddle(2)
            twiddle(3)
            dve.wait_ge(s_twd, 3)
            dve.wait_ge(s_tw, 4)
            second(0)
            dve.wait_ge(s_gb, 16 * GROUPS)
            dve.wait_ge(s_cx, 1)
            for h in range(2):
                y = uf[:, 2 * h:2 * h + 2, LAT:TOK]
                ins = dve.tensor_tensor(y, bank[6 + h][:, :].rearrange("p (g k) -> p g k", g=2), y, ALU.mult)
            ins.then_inc(s_fo, 1)
            second(1)
            gate_latents(0)
            second(2)
            for c in range(1, 4):
                gate_latents(c)

            def low(out, raw, hi, count, value, done):
                dve.wait_ge(count, value)
                return dve.tensor_tensor(out, raw, hi.bitcast(F32), ALU.subtract).then_inc(done, 1)

            for k in range(KA):
                low(pw_lo[:, k, :], pw_raw[:, k % 3, :], pw_hi[:, k, :], s_pwh, k + 1, s_pwl)

            def low_block(b, slot):
                for half in range(2):
                    k = slice(4 * half, 4 * half + 4)
                    low(in_lo[slot][:, k, :], og_ld[:, k, :], in_hi[slot][:, k, :], s_ih, 3 * b + half + 1, s_il)
                low(in_lo[slot][:, KT:KA, :], uf[:, :, bass.ds(b * MB, MB)], in_hi[slot][:, KT:KA, :], s_ih, 3 * b + 3, s_il)

            def gate_block(b):
                for j in range(8):
                    dve.wait_ge(s_mg[j % 4], 16 * (2 * b + j // 4 + 1))
                    dve.wait_ge(s_y, 8 * b + j + 1)
                    m = mg_ld[:, j % 4, :, :].rearrange("p a n -> p (a n)")
                    dve.tensor_tensor(m, bank[j][:, :], m, ALU.mult).then_inc(s_yg, 1)

            dve.wait_ge(s_fo, 17)
            dve.wait_ge(s_pwl, KA)
            dve.memset(pad[:, :], 0.0).then_inc(s_yg, 8)
            low_block(0, 0)
            with dve.Fori(0, NM // 2) as i:
                for u in range(2):
                    low_block(2 * i + u + 1, 1 - u)
                    gate_block(2 * i + u)
            gate_block(NM - 1)

            dve.wait_ge(s_me, 8 * NM)
            dve.tensor_copy(silb[:, :, :, :], silc[:, :, :].unsqueeze(3).to_broadcast([P, 2, KT, P])).then_inc(s_silb, 1)
            for k in range(KT):
                low(ow_lo[:, k, :], ow_raw[:, k % 3, :], ow_hi[:, k, :], s_owh, k + 1, s_owl)
            dve.wait_ge(s_row3, 32)
            for n in range(4):
                s, h = n // 2, n % 2
                dve.wait_ge(s_gm3, n + 1)
                dve.tensor_tensor(res_gate[:, s, 512 * h:512 * h + 512], bank[n][:, :], gate_b[:, 512 * h:512 * h + 512],
                                  ALU.add).then_inc(s_gate, 1)
            dve.wait_ge(s_gate, 4)
            dve.memset(pad[:, :], 0.0).then_inc(s_og3, 4)
            low(me_lo[0][:, :, :], me_ld[:, :, :], me_hi[0][:, :, :], s_mh, 1, s_ml)

            def finish_block(b, slot, final):
                if not final:
                    low(me_lo[1 - slot][:, :, :], me_ld[:, :, :], me_hi[1 - slot][:, :, :], s_mh, b + 2, s_ml)
                for u in range(2):
                    dve.wait_ge(s_yst[u], 16 * b)
                    dve.wait_ge(s_out, 2 * b + u + 1)
                    for h in range(2):
                        sl = slice(512 * h, 512 * h + 512)
                        ins = dve.tensor_tensor(yt[:, u, sl], bank[4 * slot + 2 * u + h][:, :], res_gate[:, int(final), sl], ALU.mult)
                    ins.then_inc(s_og3, 1)
                for u in range(2):
                    dve.wait_ge(s_rs3, 2 * b + u + 1)
                    dve.scalar_tensor_tensor(yt[:, u, :], yt[:, u, :], rms3[:, u, 1:2], fng[:, :], ALU.mult, ALU.mult
                                             ).then_inc(s_yn, 1)

            with dve.Fori(0, NM // 2) as i:
                for u in range(2):
                    finish_block(2 * i + u, u, False)
            finish_block(NM - 1, 0, True)

        @block.tensor
        def _(pe):
            pe.wait_ge(s_const, 16)
            pe.wait_ge(s_rows, 16 * 7)
            pe.transpose(bank[7][:, 0:C_ALL], rows, ident[0:C_ALL, 0:C_ALL]).then_inc(s_rowt, 1)
            pe.wait_ge(s_silc, 1)
            for n in range(4):
                pe.wait_ge(s_wada[n % 2], 16 * (n // 2 + 1))
                for k in range(KT):
                    ins = pe.matmul(bank[n][0:2, :], silc[:, :, k], wada[:, n % 2, k, :], start=(k == 0), stop=(k == KT - 1))
                ins.then_inc(s_ada, 1)
            pe.wait_ge(s_adar, 4)
            for j in range(16):
                ins = pe.transpose(bank[6][:, 2 * j:2 * j + 2], adarow[:, j * P:(j + 1) * P], ident[0:2, 0:2])
            ins.then_inc(s_adat, 1)
            for b, (t0, n) in enumerate(BLOCKS):
                tiles = n // P
                for k in range(KT):
                    if k == 0:
                        pe.wait_ge(s_xn, t0 // P + tiles)
                    if b:
                        pe.wait_ge(s_h32, KT * (b - 1) + k + 1)
                    elif k == 6:
                        pe.wait_ge(s_mod, 2)
                    for s in range(tiles):
                        ins = pe.transpose(bank[k][:, s * P:(s + 1) * P], xt[:, s, k * P:(k + 1) * P], ident)
                    ins.then_inc(s_xt, 1)

            def unit_block(slot, b, a):
                t0, n = BLOCKS[b]
                sl = slice(P * slot, P * slot + P)
                pe.wait_ge(s_ev, a - (NB - 1))
                for k in range(KT):
                    for w, h in ((w_hi, h_hi), (w_hi, h_lo), (w_lo, h_hi)):
                        ins = pe.matmul(bank[b][:, 0:n], w[0][:, k, sl], h[:, k, t0:t0 + n],
                                        start=(k == 0 and w is w_hi and h is h_hi), stop=(k == KT - 1 and w is w_lo))
                ins.then_inc(s_mm, 1)

            pe.wait_ge(s_wlo, 1)
            for b in range(NB):
                pe.wait_ge(s_h32, KT * (NB - 1) + b + 1)
                pe.wait_ge(s_hlo, KT * (b + 1))
                unit_block(1, b, NB - 1)
            pe.wait_ge(s_h32, KT * NB)
            for sec in range(2):
                with pe.Fori(0, 2) as i:
                    for u in range(2):
                        unit = 4 * sec + 2 * i + u
                        pe.wait_ge(s_wlo, unit + 2)
                        for b, (t0, n) in enumerate(BLOCKS):
                            e = NB * unit + b
                            unit_block(u, b, A_QK + e)
                            pe.wait_ge(s_now, 2 * sec + i + 1)
                            lag = 0 if (sec, u, b) == (0, 0, 0) else 1
                            pe.wait_ge(s_gabs, e - lag)
                            pe.wait_ge(s_gmin, e - lag)
                            pe.matmul(bank[5 + (NB * u + b) % 2][:, 0:n], walp_now[:, u, :], r_t[:, t0:t0 + n],
                                      start=True, stop=True).then_inc(s_g, 1)
            pe.wait_ge(s_gabs, 8 * NB)
            pe.wait_ge(s_gmin, 8 * NB)
            with pe.Fori(0, 2) as i:
                for pair in range(2):
                    head = 2 * i + pair
                    pe.wait_ge(s_wlo, 11 + 2 * head)
                    for t in range(NT):
                        pe.wait_ge(s_ev, A_V + NT * head + t - 2)
                        for k in range(KT):
                            for h, w in ((h_hi, w_hi), (h_hi, w_lo), (h_lo, w_hi)):
                                ins = pe.matmul(bank[5 + t % 3][:, 0:DV], h[:, k, t * P:t * P + P], w[pair][:, k, :],
                                                start=(k == 0 and h is h_hi and w is w_hi), stop=(k == KT - 1 and h is h_lo))
                        ins.then_inc(s_mm, 1)
            with pe.Fori(0, 16) as i:
                for u in range(2):
                    m = 2 * i + u
                    pe.wait_ge(s_wlo, 18 + m)
                    for b in range(NB):
                        unit_block(u, b, A_GA + NB * m + b)
            pe.wait_ge(s_ev, A_END)
            with pe.Fori(0, HEADS) as head:
                def turn(j):
                    x, c = TERMS[j]
                    way = STEPS[x][0]
                    if way == "b":
                        pe.wait_ge(s_qd, 10 * head + x + 1)
                        pe.wait_ge(s_kin, NTERM * head + max(j - 1, 0))
                    else:
                        pe.wait_ge(s_kin, NTERM * head + j)
                    pe.transpose(bank[6 + (j % 2 if way == "b" else 0)][:, 0:P], kk[:, 1 if way == "b" else 0, c * P:c * P + P],
                                 ident).then_inc(s_tr, 1)

                def state_term(j):
                    x, c = TERMS[j]
                    pe.wait_ge(s_ld[x % 2], load_value(head, x))
                    pe.wait_ge(s_dt, NTERM * head + max(j - 1, 0))
                    pe.wait_ge(s_kin, NTERM * head + j + 1)
                    pe.matmul(bank[4 + j % 2][:, 0:DV], kin[:, j % 2, :], v_of(x, c), start=True, stop=True).then_inc(s_ds, 1)

                def v_of(x, c):
                    return v_ld[:, x % 2, c - min(chunks_of[x]), :]

                def scores(c):
                    x = next(x for x in range(5, 10) if c in chunks_of[x])
                    at = (c - chunks_of[x][0]) * P
                    pe.wait_ge(s_cb, NT * head + max(c - 1, 0))
                    pe.wait_ge(s_qd, 10 * head + x + 1)
                    for d in range(2):
                        ins = pe.matmul(bank[c % 2][:, d * P:d * P + P], kk[:, d, c * P:c * P + P],
                                        qd[:, x % 2, d, at:at + P], start=True, stop=True)
                    ins.then_inc(s_sc, 1)

                def output(c):
                    x = next(x for x in range(5, 10) if c in chunks_of[x])
                    at = (c - chunks_of[x][0]) * P
                    out = bank[2 + c % 2][:, 0:DV]
                    pe.wait_ge(s_on, NT * head + max(c - 1, 0))
                    pe.wait_ge(s_ld[x % 2], load_value(head, x))
                    pe.wait_ge(s_pu, NTERM * head + (term["f", c - 1] + 1 if ("f", c - 1) in term else
                                                     term["f", c - 2] + 1 if c else B_TERMS))
                    if c == 0:
                        pe.wait_ge(s_p0, 3 * head + 3)
                    if c == LT:
                        pe.wait_ge(s_pz, head + 1)
                    pe.wait_ge(s_cb, NT * head + c + 1)
                    pe.matmul(out, comb[:, c % 2, :], v_of(x, c), start=True, stop=False)
                    pe.matmul(out, qd[:, x % 2, 0, at:at + P], pf[:, c % 2, :], start=False, stop=False)
                    pe.matmul(out, qd[:, x % 2, 1, at:at + P], pb[:, c, :], start=False, stop=True).then_inc(s_o, 1)

                def turn_output(c):
                    pe.wait_ge(s_gt, NT * head + c)
                    pe.wait_ge(s_on, NT * head + c + 1)
                    for e in range(2):
                        ins = pe.transpose(bank[7][:, e * P:e * P + P], on[:, c % 2, e * P:e * P + P], ident)
                    ins.then_inc(s_ot, 1)

                pe.wait_ge(s_gt, NT * head)
                turn(0)
                for j in range(B_TERMS):
                    if j + 1 < B_TERMS:
                        turn(j + 1)
                    state_term(j)
                turn(term["f", 0])
                scores(0)
                for c in range(NT):
                    if ("f", c + 1) in term:
                        turn(term["f", c + 1])
                    if c + 1 < NT:
                        scores(c + 1)
                    if ("f", c) in term:
                        state_term(term["f", c])
                    output(c)
                    if c:
                        turn_output(c - 1)
                turn_output(NT - 1)
            pe.wait_ge(s_gt, NT * HEADS)
            pe.wait_ge(s_ftab, 64)
            for g in range(GROUPS):
                for r in range(2):
                    ins = pe.matmul(bank[g // 2][:, 256 * (g % 2) + P * r:256 * (g % 2) + P * r + P], chan[:, r, :], w4[:, g, :],
                                    start=True, stop=True)
                if g % 2:
                    ins.then_inc(s_cwm, 1)
            pe.wait_ge(s_u, 16 * GROUPS)
            pe.wait_ge(s_cw, 2)
            for m, t in enumerate(Z_ORDER):
                if m >= 3:
                    pe.wait_ge(s_z, m - 2)
                for g in range(GROUPS):
                    ins = pe.matmul(bank[2 * (m % 3) + g // 2][:, 256 * (g % 2):256 * (g % 2) + 256], uf[:, g, t * P:t * P + P],
                                    cw[:, g, :, :].rearrange("p r c -> p (r c)"), start=True, stop=True)
                ins.then_inc(s_zm, 1)
            pe.wait_ge(s_z, NT)
            for g in range(GROUPS):
                for n in range(4):
                    t, r = n // 2, n % 2
                    ins = pe.matmul(bank[6 + g // 2][:, 256 * (g % 2):256 * (g % 2) + 256], zb[:, LT + t, r, g * P:g * P + P],
                                    dft_c[:, r, t, :], start=(n == 0), stop=(n == 3))
            ins.then_inc(s_cx, 1)
            for c in range(4):
                if c < 3:
                    pe.wait_ge(s_l4, c + 1)
                else:
                    pe.wait_ge(s_p4, 1)
                if c:
                    pe.wait_ge(s_fo, 1 if c == 1 else 1 + 4 * (c - 1))
                for d in range(4):
                    for g in range(GROUPS):
                        for r in range(2):
                            ins = pe.matmul(bank[4 * (c % 2) + d][:, g * P:g * P + P], sb[:, 4 * c + d, r, g * P:g * P + P],
                                            dft[:, r, c + 4 * d, :], start=(r == 0), stop=(r == 1))
                    ins.then_inc(s_f, 1)

            def split_product(out, pairs, count):
                for k, (st, mv) in enumerate(pairs):
                    for p, (a, b) in enumerate(((0, 0), (0, 1), (1, 0))):
                        ins = pe.matmul(out, st[a], mv[b], start=(k == 0 and p == 0), stop=(k == count - 1 and p == 2))
                return ins

            def branch_block(b, slot):
                pe.wait_ge(s_il, 3 * b + 3)
                for j in range(8):
                    pe.wait_ge(s_yg, 8 * b + j + 1)
                    for a, ks in enumerate((range(0, KT), range(KT, KA))):
                        ins = split_product(bank[j][:, a * MB:a * MB + MB],
                                            [((pw_hi[:, k, j * P:j * P + P], pw_lo[:, k, j * P:j * P + P]),
                                              (in_hi[slot][:, k, :], in_lo[slot][:, k, :])) for k in ks], len(ks))
                    ins.then_inc(s_y, 1)

            with pe.Fori(0, NM // 2) as i:
                for u in range(2):
                    branch_block(2 * i + u, u)
            branch_block(NM - 1, 0)

            pe.wait_ge(s_silb, 1)
            pe.wait_ge(s_yg, 8 + 8 * NM)
            for n in range(4):
                s, h = n // 2, n % 2
                pe.wait_ge(s_gw[h], 16)
                for k in range(KT):
                    ins = pe.matmul(bank[n][:, :], silb[:, s, k, :], gate_w[:, h, k, :], start=(k == 0), stop=(k == KT - 1))
                ins.then_inc(s_gm3, 1)
            pe.wait_ge(s_owl, KT)

            def out_tiles(b, slot):
                pe.wait_ge(s_ml, b + 1)
                for u in range(2):
                    pe.wait_ge(s_og3, 2 * b + u + 1)
                    for h in range(2):
                        ins = split_product(bank[4 * slot + 2 * u + h][:, :],
                                            [((me_hi[slot][:, k, u * P:u * P + P], me_lo[slot][:, k, u * P:u * P + P]),
                                              (ow_hi[:, k, 512 * h:512 * h + 512], ow_lo[:, k, 512 * h:512 * h + 512]))
                                             for k in range(KT)], KT)
                    ins.then_inc(s_out, 1)

            with pe.Fori(0, NM // 2) as i:
                for u in range(2):
                    out_tiles(2 * i + u, u)
            out_tiles(NM - 1, 0)
    return nc


def constants():
    c = np.zeros((P, K_ALL), np.float32)
    c[:, K_ID:K_ID + P] = np.eye(P)
    c[:, K_UP:K_UP + P] = np.triu(np.ones((P, P)), 1)
    c[:, K_DW:K_DW + P] = 1 + np.eye(P)
    c[:, K_ONE:K_ONE + P] = 1
    return c


def rope_tables():
    f = DK // 4
    freqs = np.float32(10000.0) ** (-np.arange(f, dtype=np.float32) / f)
    t = np.arange(LAT)
    out = np.zeros((P, 2, TOK), np.float32)
    out[:, 0, LAT:] = 1
    for a, at in enumerate((t // 64, t % 64)):
        ang = freqs[:, None] * at[None].astype(np.float32)
        for half in range(2):
            rows = slice(64 * a + 32 * half, 64 * a + 32 * half + 32)
            out[rows, 0, :LAT] = np.cos(ang)
            out[rows, 1, :LAT] = np.sin(ang) * (1 if half else -1)
    return out


def fourier_tables():
    n = np.arange(P)
    ang = 2 * np.pi * np.outer(n, n) / P
    chan = np.stack([np.cos(ang), -np.sin(ang)], 1)
    k = N1 * n[None, :] + np.arange(N1)[:, None]
    ang = 2 * np.pi * (n[:, None, None] * k[None] % LAT) / LAT
    dft = np.stack([np.cos(ang), np.sin(ang)], 1) / np.sqrt(LAT * P)
    t = np.arange(CTX).reshape(CTX // P, P).T
    ang = 2 * np.pi * (t[:, :, None] * np.arange(CTX) % CTX) / CTX
    dft_c = np.stack([np.cos(ang), np.sin(ang)], 1) / np.sqrt(CTX * P)
    return {"chan": chan.astype(np.float32), "dft": dft.astype(np.float32), "dft_c": dft_c.astype(np.float32)}


def layout(a):
    w_in = a["w_in"][0]
    ranks = 2 * HEADS * DK + 2 * HEADS * DV
    order = np.concatenate([np.arange(ranks, ranks + P), np.arange(ranks), np.arange(ranks + 2 * RANK, w_in.shape[1])])
    tiles = lambda w, c: w.reshape(w.shape[0] // P, P, -1, c).transpose(2, 1, 0, 3)
    return {
        "consts": constants(), "rope": rope_tables(), **fourier_tables(),
        "w_four": a["w_four"][0].transpose(1, 0, 2), "b_gate": a["b_ada"][:, 2 * D:], "final_norm_g": a["final_norm_g"][None],
        "w_proj_a": a["w_proj_a"][0].reshape(KT, P, D), "w_proj_b": a["w_proj_b"][0].reshape(GROUPS, P, D),
        "w_out": a["w_out"][0].reshape(KT, P, D),
        "state_fwd": a["state_gla_fwd"][0, 0], "state_bwd": a["state_gla_bwd"][0, 0],
        "x": np.concatenate([a["x_sample"][0], a["x_prompt"][0]]),
        "c": a["c"].reshape(8, P), "c_ctx": a["c_ctx"].reshape(8, P), "norm_g": a["norm_g"].reshape(8, P),
        "b_ada": a["b_ada"].reshape(24, P), "gla_norm_g": a["gla_norm_g"].reshape(2, P),
        "b_alpha_fwd": a["b_alpha_fwd"].reshape(4, P), "b_alpha_bwd": a["b_alpha_bwd"].reshape(4, P),
        "w_ada": tiles(a["w_ada"][0], 512),
        "w_in": tiles(w_in[:, order], P),
        "w_alpha_fwd": a["w_alpha_fwd"].reshape(RANK, 4, P), "w_alpha_bwd": a["w_alpha_bwd"].reshape(RANK, 4, P),
    }


OUTS = {"y": (TOK, D), "new_fwd": (HEADS, DK, DV), "new_bwd": (HEADS, DK, DV)}


def kernel(**inputs):
    import concourse.bacc as bacc
    from concourse.bass_utils import run_bass_kernel_spmd

    nc = bacc.Bacc("TRN2", target_bir_lowering=False, num_devices=1)
    arrays = {"in_" + k: np.ascontiguousarray(v) for k, v in layout({k: np.asarray(v) for k, v in inputs.items()}).items()}
    io = {k[3:]: nc.dram_tensor(k, v.shape, mybir.dt.from_np(v.dtype), kind="ExternalInput").ap() for k, v in arrays.items()}
    for k, shape in OUTS.items():
        io[k] = nc.dram_tensor(k, shape, F32, kind="ExternalOutput").ap()
    build(nc, io, lambda name, shape: nc.dram_tensor(name, shape, F32, kind="Internal").ap())
    out = run_bass_kernel_spmd(nc, [arrays], core_ids=[0]).results[0]
    y = out["y"]
    return (y[LAT:][None], y[:LAT][None], out["new_fwd"][None, None], out["new_bwd"][None, None])
```

```python
from contextlib import ExitStack

import numpy as np

import concourse.bass as bass
from concourse import mybir

F32 = mybir.dt.float32
F32R = mybir.dt.float32r
BF16 = mybir.dt.bfloat16
U32 = mybir.dt.uint32
ALU = mybir.AluOpType
ACT = mybir.ActivationFunctionType

P = 128
D = 1024
KT = D // P
LAT, CTX = 2048, 256
TOK = LAT + CTX
NT = TOK // P
LT = LAT // P
HEADS, DK, DV = 4, 128, 256
BLOCKS = [(0, 512), (512, 512), (1024, 512), (1536, 512), (2048, 256)]
NB = len(BLOCKS)
RANK = 16
GATE_NORM = 16.0
EPS = 1e-6
GROUPS = 4
N1 = 16
RB = 384
KA = KT + GROUPS
MB = 256
NM = TOK // MB
UNITS = 49

C_COND, C_NG, C_BADA, C_GG, C_BAF, C_BAB, C_ALL = 0, 16, 24, 48, 50, 54, 58
K_ID, K_UP, K_DW, K_ONE, K_ALL = 0, 128, 256, 384, 512


def build(nc, io, scratch):
    q_dram = scratch("qk_dram", [8, P, TOK])
    v_dram = scratch("v_dram", [4, P, NT, DV])
    e_dram = scratch("e_dram", [4, P, 2, 2, TOK])
    qk_dec = scratch("qk_dec", [8, P, 2, TOK])
    ga_dram = scratch("ga_dram", [8, P, TOK])
    u_dram = scratch("u_dram", [4, P, TOK])
    gb_dram = scratch("gb_dram", [4, P, TOK])
    mg_dram = scratch("mg_dram", [16, P, TOK])
    og_dram = scratch("og_dram", [8, P, TOK])
    me_dram = scratch("me_dram", [8, P, TOK])

    ctx = ExitStack()
    with ctx:
        base = (nc.sbuf_base + 31) // 32 * 32
        end = nc.sbuf_usable_end

        class Region:

            def __init__(self, start):
                self.at = start

            def __call__(self, name, shape, dt=F32):
                size = int(np.prod(shape[1:])) * (2 if dt == BF16 else 4)
                t = nc.alloc_sbuf_tensor_at(name, shape, dt, offset=self.at)
                self.at += (size + 31) // 32 * 32
                assert self.at <= end, (name, self.at, end)
                return t

        def sem(name):
            return ctx.enter_context(nc.semaphore(name))

        bank = [ctx.enter_context(nc.psum_tensor(f"bank{n}", [P, 512], F32)) for n in range(8)]

        keep = Region(base)
        consts = keep("consts", [P, K_ALL])
        ident = consts[:, K_ID:K_ID + P]
        upper = consts[:, K_UP:K_UP + P].bitcast(U32)
        diag2 = consts[:, K_DW:K_DW + P]
        ones = consts[:, K_ONE:K_ONE + P]
        cols = keep("cols", [P, 64])
        silc = keep("silc", [P, 2, KT])
        modu = keep("modu", [P, 2, 2, KT])
        mid = keep("mid", [P, 8, NT])
        last = keep("last", [P, 8, NT])
        pad = keep("pad", [P, 1])
        kept = keep.at

        act_in = Region(kept)
        h_hi = act_in("h_hi", [P, KT, TOK], F32R)
        adarow = Region(act_in.at)("adarow", [2, 2048])
        h_lo = act_in("h_lo", [P, KT, TOK], F32R)
        after_h = act_in.at
        r0 = Region(after_h)
        wada = r0("wada", [P, 2, KT, 512])
        xt = r0("xt", [P, 4, D])
        h32 = r0("h32", [P, 2, 512])
        rows = h32[0:C_ALL, 0, 0:P]
        sq0 = r0("sq0", [P, 4])
        rs0 = r0("rs0", [P, 4])
        junk = r0("junk", [P, D], BF16)

        r1 = Region(after_h)
        w_hi = [r1("w_hi0", [P, KT, 2 * P], F32R)]
        w_lo = [r1("w_lo0", [P, KT, 2 * P], F32R)]
        second = r1.at
        w_hi.append(r1("w_hi1", [P, KT, 2 * P], F32R))
        w_lo.append(r1("w_lo1", [P, KT, 2 * P], F32R))
        r1.at += 1056
        r_t = r1("r_t", [2 * RANK, TOK])
        w_raw = r1("w_raw", [P, 2, KT, P])
        stage = r1("stage", [P, NB * 512])
        rg = Region(second)
        walp = rg("walp", [2 * RANK, 8, P])
        walp_now = rg("walp_now", [2 * RANK, 2, P])
        balp_now = rg("balp_now", [P, 2])
        soft = rg("soft", [P, 512])
        logit = rg("logit", [P, 512])
        cum = rg("cum", [P, 512])
        bcs = rg("bcs", [P, 512])
        decs = rg("decs", [P, 2, 512])
        assert rg.at <= second + 17440
        rp = Region(second)
        x_rot = rp("x_rot", [P, 2, 2, RB])
        rope = rp("rope", [P, 2, 2, RB])
        dec_in = rp("dec_in", [P, 2, 2, RB])

        def stage_b(b):
            return stage[:, 512 * b:512 * b + BLOCKS[b][1]]

        def stage_v(g):
            return stage[:, 768 * g:768 * g + 768].rearrange("p (t c) -> p t c", t=3)

        r2 = Region(kept)
        v_ld = r2("v_ld", [P, 2, NT, DV])
        ga_ld = r2("ga_ld", [P, 2, 2, TOK])
        qd = [r2("qd0", [P, 2, TOK]), r2("qd1", [P, 2, TOK])]
        kk = [None, r2("kk1", [P, 2, TOK])]
        pb = r2("pb", [P, NT, DV])
        pf = r2("pf", [P, 2, DV])
        kin = r2("kin", [P, 2, P])
        comb = r2("comb", [P, 2, P])
        ds_t = r2("ds_t", [P, 2, DV])
        junk2 = r2("junk2", [P, DV], BF16)
        rms = r2("rms", [P, 2])
        on = r2("on", [P, 2, DV])
        tf = r2("tf", [P, 2, HEADS, NT])
        fac = r2("fac", [P, 2, HEADS, NT])
        mid_e = r2("mid_e", [P, 2, HEADS, NT])
        fac_now = r2("fac_now", [P, 2, 2, NT])
        mid_now = r2("mid_now", [P, 2, 2, NT])
        assert r2.at <= second, (r2.at, second)
        r2.at = second
        kk[0] = r2("kk0", [P, 2, TOK])
        og = r2("og", [P, 2, 2, 512])
        s0 = r2("s0", [P, 2, HEADS, DV])
        first = r2("first", [P, 2, 2, DV])
        fin = r2("fin", [P, 2, 2, DV])

        TERMS = [("b", c) for c in [*range(LT - 1, 0, -1), NT - 1, LT]] + [("f", c) for c in range(NT) if c != LT - 1]
        term = {t: j for j, t in enumerate(TERMS)}
        NTERM = len(TERMS)
        B_TERMS = LT + 1

        r3 = Region(kept)
        uf = r3("uf", [P, GROUPS, TOK])
        after_uf = r3.at
        zb = r3("zb", [P, NT, 2, 512])
        sb = r3("sb", [P, N1, 2, 512])
        dft = r3("dft", [P, 2, N1, P])
        dft_c = r3("dft_c", [P, 2, CTX // P, CTX])
        chan = r3("chan", [P, 2, P])
        w4 = r3("w4", [P, GROUPS, P])
        cw = r3("cw", [P, GROUPS, 2, P])

        r4 = Region(after_uf)
        pw_hi = r4("pw_hi", [P, KA, D], F32R)
        pw_lo = r4("pw_lo", [P, KA, D], F32R)
        og_ld = r4("og_ld", [P, KT, MB])
        mg_ld = r4("mg_ld", [P, 4, 2, MB])
        me_st = r4("me_st", [P, 4, MB])
        in_hi = r4("in_hi", [P, KA, MB], F32R)
        in_lo = r4("in_lo", [P, KA, MB], F32R)
        pw_raw = Region(r4.at)("pw_raw", [P, 3, D])
        in_hi = [in_hi, r4("in_hi1", [P, KA, MB], F32R)]
        in_lo = [in_lo, r4("in_lo1", [P, KA, MB], F32R)]

        r5 = Region(kept)
        ow_hi = r5("ow_hi", [P, KT, D], F32R)
        ow_lo = r5("ow_lo", [P, KT, D], F32R)
        ow_raw = r5("ow_raw", [P, 3, D])
        me_ld = r5("me_ld", [P, KT, MB])
        me_hi = [r5(f"me_hi{n}", [P, KT, MB], F32R) for n in range(2)]
        me_lo = [r5(f"me_lo{n}", [P, KT, MB], F32R) for n in range(2)]
        x_in = r5("x_in", [P, 2, D])
        yt = r5("yt", [P, 2, D])
        gate_w = r5("gate_w", [P, 2, KT, 512])
        gate_b = r5("gate_b", [P, D])
        res_gate = r5("res_gate", [P, 2, D])
        fng = r5("fng", [P, D])
        silb = r5("silb", [P, 2, KT, P])
        junk3 = r5("junk3", [P, D], BF16)
        rms3 = r5("rms3", [P, 2, 2])

        s_const, s_rows = sem("s_const"), sem("s_rows")
        s_x = [sem(f"s_x{n}") for n in range(4)]
        s_wada = [sem(f"s_wada{n}") for n in range(2)]
        s_rowt, s_cols, s_silc = sem("s_rowt"), sem("s_cols"), sem("s_silc")
        s_ada, s_adar, s_adat, s_mod = sem("s_ada"), sem("s_adar"), sem("s_adat"), sem("s_mod")
        s_ssq, s_root, s_rs, s_xn = sem("s_ssq"), sem("s_root"), sem("s_rs"), sem("s_xn")
        s_xt, s_h32, s_hhi, s_hlo = sem("s_xt"), sem("s_h32"), sem("s_hhi"), sem("s_hlo")
        s_wraw = [sem(f"s_wraw{n}") for n in range(2)]
        s_whi, s_wlo = sem("s_whi"), sem("s_wlo")
        s_mm = sem("s_mm")
        s_ev = sem("s_ev")
        s_st = [sem(f"s_st{n}") for n in range(NB)]
        s_vst = [sem(f"s_vst{n}") for n in range(3)]
        s_wal0, s_wal, s_now = sem("s_wal0"), sem("s_wal"), sem("s_now")
        s_g = sem("s_g")
        s_gabs, s_gexp, s_gln = sem("s_gabs"), sem("s_gexp"), sem("s_gln")
        s_gmin, s_glog, s_gcum, s_bc = sem("s_gmin"), sem("s_glog"), sem("s_gcum"), sem("s_bc")
        s_dec, s_est = sem("s_dec"), sem("s_est")
        s_rld = [sem(f"s_rld{n}") for n in range(2)]
        s_rm, s_rotd, s_rprod = sem("s_rm"), sem("s_rotd"), sem("s_rprod")
        s_rst = [sem(f"s_rst{n}") for n in range(2)]

        s_s0 = sem("s_s0")
        s_kl, s_vl, s_ql, s_gl = ([sem(f"{name}{n}") for n in range(2)] for name in ("s_kl", "s_vl", "s_ql", "s_gl"))
        s_tf, s_fac, s_facn, s_p0 = sem("s_tf"), sem("s_fac"), sem("s_facn"), sem("s_p0")
        s_tr, s_kin, s_ds, s_dt, s_pu = sem("s_tr"), sem("s_kin"), sem("s_ds"), sem("s_dt"), sem("s_pu")
        s_sc, s_cb1, s_cb, s_o = sem("s_sc"), sem("s_cb1"), sem("s_cb"), sem("s_o")
        s_sq2, s_ln2, s_rs2, s_on, s_ot, s_gt = (sem("s_sq2"), sem("s_ln2"), sem("s_rs2"), sem("s_on"), sem("s_ot"),
                                                 sem("s_gt"))
        s_ogst = [sem(f"s_ogst{n}") for n in range(2)]
        s_fst = sem("s_fst")

        s_ftab, s_u, s_gb = sem("s_ftab"), sem("s_u"), sem("s_gb")
        s_cwm, s_cw, s_zm, s_z = sem("s_cwm"), sem("s_cw"), sem("s_zm"), sem("s_z")
        s_l1, s_l2, s_l3, s_l4 = sem("s_l1"), sem("s_l2"), sem("s_l3"), sem("s_l4")
        s_p1, s_p2, s_p3, s_p4 = sem("s_p1"), sem("s_p2"), sem("s_p3"), sem("s_p4")
        s_tw, s_twd, s_cx, s_f, s_fo = sem("s_tw"), sem("s_twd"), sem("s_cx"), sem("s_f"), sem("s_fo")
        s_pwr = [sem(f"s_pwr{n}") for n in range(3)]
        s_pwh, s_pwl = sem("s_pwh"), sem("s_pwl")
        s_og = [sem(f"s_og{n}") for n in range(2)]
        s_mg = [sem(f"s_mg{n}") for n in range(4)]
        s_mest = [sem(f"s_mest{n}") for n in range(4)]
        s_ih, s_il, s_y, s_yg, s_me = sem("s_ih"), sem("s_il"), sem("s_y"), sem("s_yg"), sem("s_me")
        s_owr = [sem(f"s_owr{n}") for n in range(3)]
        s_gw = [sem(f"s_gw{n}") for n in range(2)]
        s_row3 = sem("s_row3")
        s_owh, s_owl, s_silb, s_gm3, s_gate = sem("s_owh"), sem("s_owl"), sem("s_silb"), sem("s_gm3"), sem("s_gate")
        s_mel, s_mh, s_ml, s_out, s_og3 = sem("s_mel"), sem("s_mh"), sem("s_ml"), sem("s_out"), sem("s_og3")
        s_xin = [sem(f"s_xin{n}") for n in range(2)]
        s_yst = [sem(f"s_yst{n}") for n in range(2)]
        s_add, s_sq3, s_ln3, s_rs3, s_yn = sem("s_add"), sem("s_sq3"), sem("s_ln3"), sem("s_rs3"), sem("s_yn")

        A_QK = NB
        A_V = A_QK + 8 * NB
        A_GA = A_V + 4 * NT
        A_END = A_GA + 32 * NB
        SECTIONS = ((ga_dram, ACT.Silu, 0, 4), (u_dram, ACT.Copy, 8, 2), (gb_dram, ACT.Silu, 12, 2),
                    (mg_dram, ACT.Sigmoid, 16, 8))

        def state_f(n, c):
            return first[:, n, 0, :] if c == 0 else pb[:, NT - 1, :] if c == LT else pf[:, c % 2, :]

        def state_b(n, c):
            return first[:, n, 1, :] if c == LT - 1 else pb[:, c, :]

        def turn_bank(j):
            return 0 if j < B_TERMS and j % 2 else 6

        Z_ORDER = [4 * a + n for n in range(4) for a in range(4)] + list(range(LT, NT))

        def sums(eng, z, s):
            for n in range(4):
                ins = eng.tensor_tensor(s[n], z[n // 2], z[n // 2 + 2], ALU.subtract if n % 2 else ALU.add)
            return ins

        def turns(eng, s, out):
            eng.tensor_tensor(out[0], s[0], s[2], ALU.add)
            eng.tensor_tensor(out[2], s[0], s[2], ALU.subtract)
            for n, (first, other) in ((1, (ALU.add, ALU.subtract)), (3, (ALU.subtract, ALU.add))):
                eng.tensor_tensor(out[n][:, 0, :], s[1][:, 0, :], s[3][:, 1, :], first)
                ins = eng.tensor_tensor(out[n][:, 1, :], s[1][:, 1, :], s[3][:, 0, :], other)
            return ins

        block = ctx.enter_context(nc.Block())

        @block.sync
        def _(sp):
            sp.dma_start(consts[:, :], io["consts"]).then_inc(s_const, 16)
            at = 0
            for name, n in (("c", 8), ("c_ctx", 8), ("norm_g", 8), ("b_ada", 24), ("gla_norm_g", 2),
                            ("b_alpha_fwd", 4), ("b_alpha_bwd", 4)):
                sp.dma_start(h32[at:at + n, 0, 0:P], io[name]).then_inc(s_rows, 16)
                at += n

            def x_block(b):
                for s in range(BLOCKS[b][1] // P):
                    t = BLOCKS[b][0] // P + s
                    if b:
                        sp.wait_ge(s_xt, KT * b)
                    sp.dma_start(xt[:, s, :], io["x"][t * P:(t + 1) * P, :]).then_inc(s_x[s], 16)

            for n in range(2):
                sp.dma_start(wada[:, n, :, :], io["w_ada"][n]).then_inc(s_wada[n], 16)
            x_block(0)
            for n in range(2, 4):
                sp.wait_ge(s_ada, n - 1)
                sp.dma_start(wada[:, n % 2, :, :], io["w_ada"][n]).then_inc(s_wada[n % 2], 16)
            for b in range(1, NB):
                x_block(b)

            sp.wait_ge(s_xt, KT * NB)
            sp.wait_ge(s_hhi, KT * NB)
            sp.wait_ge(s_hlo, KT * NB)
            for n in range(2):
                sp.dma_start(w_raw[:, (n + 1) % 2, :, :], io["w_in"][n]).then_inc(s_wraw[(n + 1) % 2], 16)
            sp.wait_ge(s_wal0, 1)
            sp.dma_start(walp[0:RANK, 0:4, :], io["w_alpha_fwd"]).then_inc(s_wal, 16)
            sp.dma_start(walp[RANK:2 * RANK, 4:8, :], io["w_alpha_bwd"]).then_inc(s_wal, 16)

            def load_after(slot, n):
                sp.wait_ge(s_wlo, n + 1)
                sp.dma_start(w_raw[:, slot, :, :], io["w_in"][bass.ds(n + 2, 1)].rearrange("o p k c -> p (o k) c")
                             ).then_inc(s_wraw[slot], 16)

            load_after(1, 0)
            for sec in range(2):
                with sp.Fori(0, 2) as i:
                    for u in range(2):
                        head = 2 * i + u
                        unit = 4 * sec + head
                        load_after(u, unit + 1)
                        for b, (t0, n) in enumerate(BLOCKS):
                            sp.wait_ge(s_ev, A_QK + NB * unit + b + 1)
                            sp.dma_start(q_dram[bass.ds(unit, 1), :, t0:t0 + n].rearrange("o p n -> p (o n)"),
                                         stage_b(b)).then_inc(s_st[b], 16)
                            sp.wait_ge(s_dec, 2 * (NB * unit + b) + 2)
                            sp.dma_start(e_dram[bass.ds(head, 1), :, :, sec, t0:t0 + n].rearrange("o p s n -> p (o s) n"),
                                         decs[:, :, 0:n]).then_inc(s_est, 16)
            with sp.Fori(0, HEADS) as head:
                for u in range(2):
                    load_after(u, 9 + 2 * head + u)
                for g in range(NT // 3):
                    sp.wait_ge(s_ev, A_V + NT * head + 3 * g + 3)
                    sp.dma_start(v_dram[bass.ds(head, 1), :, 3 * g:3 * g + 3, :].rearrange("o p t c -> p (o t) c"),
                                 stage_v(g % 3)).then_inc(s_vst[g % 3], 16)
            sp.wait_ge(s_est, 16 * 8 * NB)
            for b in range(NB):
                sp.wait_ge(s_st[b], 16 * 8)
            for dst, _, m0, pairs in SECTIONS:
                if dst is mg_dram:
                    for n in range(2):
                        sp.wait_ge(s_rst[n], 16 * 24)
                    sp.dma_start(kk[0][:, :, :], qk_dec[4]).then_inc(s_kl[0], 16)

                def rotate(i, at):
                    pair = m0 // 2 + i
                    sign, heads0 = (0, 0) if m0 == 0 else (1, m0 // 2 - 4)
                    load, store = {0: (0, None), 1: (1, None), 2: (2, 0), 3: (3, 1), 5: (4, 2), 6: (5, 3), 8: (None, 4),
                                   9: (None, 5)}.get(at, (None, None))
                    if store is not None:
                        t0 = store * RB
                        sp.wait_ge(s_rprod, 6 * pair + store + 1)
                        sp.dma_start(qk_dec[bass.ds(pair, 1), :, :, t0:t0 + RB].rearrange("o p d n -> p (o d) n"),
                                     dec_in[:, store % 2, :, :]).then_inc(s_rst[store % 2], 16)
                    if load is not None:
                        t0, slot, got = load * RB, load % 2, s_rld[load % 2]
                        src = q_dram[bass.ds(pair, 1), :, t0:t0 + RB].rearrange("o p n -> p (o n)")
                        sp.wait_ge(s_rst[slot], 16 * (3 * pair + load // 2))
                        for q in range(4):
                            sp.dma_start(x_rot[32 * q:32 * q + 32, slot, 1, :], src[32 * (q ^ 1):32 * (q ^ 1) + 32, :]
                                         ).then_inc(got, 16)
                        sp.dma_start(x_rot[:, slot, 0, :], src).then_inc(got, 16)
                        sp.dma_start(dec_in[:, slot, :, :], e_dram[bass.ds(heads0 + i, 1), :, sign, :, t0:t0 + RB]
                                     .rearrange("o p d n -> p (o d) n")).then_inc(got, 16)
                        sp.dma_start(rope[:, slot, :, :], io["rope"][:, :, t0:t0 + RB]).then_inc(got, 16)

                def store_pair(i, loads):
                    for u in range(2):
                        m = m0 + 2 * i + u
                        if loads:
                            load_after(u, 17 + m)
                        for b, (t0, n) in enumerate(BLOCKS):
                            sp.wait_ge(s_ev, A_GA + NB * m + b + 1)
                            sp.dma_start(dst[bass.ds(2 * i + u, 1), :, t0:t0 + n].rearrange("o p n -> p (o n)"),
                                         stage_b(b)).then_inc(s_st[b], 16)
                            if dst is not mg_dram:
                                rotate(i, NB * u + b)

                final = dst is mg_dram
                with sp.Fori(0, pairs - final) as i:
                    store_pair(i, True)
                if final:
                    store_pair(pairs - 1, False)
            for b in range(NB):
                sp.wait_ge(s_st[b], 16 * 40)
            sp.wait_ge(s_mm, A_END)
            for g in range(3):
                sp.wait_ge(s_vst[g], 16 * 2 * HEADS)

            def load_head(head):
                n = head % 2
                if head:
                    sp.dma_start(kk[n][:, :, :], qk_dec[4 + head]).then_inc(s_kl[n], 16)
                sp.dma_start(v_ld[:, n, :, :], v_dram[head]).then_inc(s_vl[n], 16)
                if head == 0:
                    for d, name in enumerate(("state_fwd", "state_bwd")):
                        sp.dma_start(s0[:, d, :, :], io[name].rearrange("h p c -> p h c")).then_inc(s_s0, 16)
                sp.dma_start(qd[n][:, :, :], qk_dec[head]).then_inc(s_ql[n], 16)
                sp.dma_start(ga_ld[:, n, :, :], ga_dram[2 * head:2 * head + 2].rearrange("e p n -> p e n")).then_inc(s_gl[n], 16)

            load_head(0)
            for head in range(HEADS):
                if head + 1 < HEADS:
                    if head:
                        sp.wait_ge(s_gt, NT * head)
                    load_head(head + 1)
                for b, (t0, n) in enumerate(BLOCKS):
                    sp.wait_ge(s_gt, NT * head + (t0 + n) // P)
                    sp.dma_start(og_dram[2 * head:2 * head + 2, :, t0:t0 + n].rearrange("e p n -> p e n"),
                                 og[:, b % 2, :, 0:n]).then_inc(s_ogst[b % 2], 16)
                sp.wait_ge(s_pu, NTERM * head + NTERM)
                sp.dma_start(io["new_fwd"][head], fin[:, head % 2, 0, :]).then_inc(s_fst, 16)
                sp.dma_start(io["new_bwd"][head], fin[:, head % 2, 1, :]).then_inc(s_fst, 16)
            sp.wait_ge(s_ogst[0], 16 * 3 * HEADS)
            sp.wait_ge(s_ogst[1], 16 * 2 * HEADS)
            sp.wait_ge(s_fst, 16 * 2 * HEADS)
            sp.wait_ge(s_gt, NT * HEADS)
            sp.dma_start(chan[:, :, :], io["chan"]).then_inc(s_ftab, 16)
            sp.dma_start(w4[:, :, :], io["w_four"]).then_inc(s_ftab, 16)
            for g in range(GROUPS):
                sp.dma_start(uf[:, g, :], u_dram[g]).then_inc(s_u, 16)
            sp.dma_start(dft[:, :, :, :], io["dft"]).then_inc(s_ftab, 16)
            sp.dma_start(dft_c[:, :, :, :], io["dft_c"]).then_inc(s_ftab, 16)
            sp.wait_ge(s_zm, NT)
            for g in range(GROUPS):
                sp.dma_start(uf[:, g, :], gb_dram[g]).then_inc(s_gb, 16)

            sp.wait_ge(s_fo, 17)
            sp.wait_ge(s_f, N1)

            def load_og(b, half):
                k = slice(4 * half, 4 * half + 4)
                t0 = b * MB if isinstance(b, int) else bass.ds(b * MB, MB)
                src = og_dram[k, :, b * MB:b * MB + MB] if isinstance(b, int) else og_dram[k, :, t0]
                sp.dma_start(og_ld[:, k, :], src.rearrange("k p n -> p k n")).then_inc(s_og[half], 16)

            def load_mg(b, j):
                rows = mg_dram[:, :, :].rearrange("(a j) p n -> j p a n", a=2)[j]
                src = rows[:, :, b * MB:b * MB + MB] if isinstance(b, int) else rows[:, :, bass.ds(b * MB, MB)]
                sp.dma_start(mg_ld[:, j % 4, :, :], src).then_inc(s_mg[j % 4], 16)

            for k in range(KA):
                if k >= 3:
                    sp.wait_ge(s_pwl, k - 2)
                sp.dma_start(pw_raw[:, k % 3, :], io["w_proj_a"][k] if k < KT else io["w_proj_b"][k - KT]
                             ).then_inc(s_pwr[k % 3], 16)
                if k == 2:
                    for half in range(2):
                        load_og(0, half)
            for j in range(4):
                load_mg(0, j)

            def merged_block(b, final):
                if not final:
                    for half in range(2):
                        sp.wait_ge(s_il, 3 * b + half + 1)
                        load_og(b + 1, half)
                for j in range(8):
                    sp.wait_ge(s_me, 8 * b + j + 1)
                    sp.dma_start(me_dram[j, :, bass.ds(b * MB, MB)] if not final else me_dram[j, :, b * MB:b * MB + MB],
                                 me_st[:, j % 4, :]).then_inc(s_mest[j % 4], 16)
                    if j < 4:
                        load_mg(b, j + 4)
                    elif not final:
                        load_mg(b + 1, j - 4)

            with sp.Fori(0, NM // 2) as i:
                for u in range(2):
                    merged_block(2 * i + u, False)
            merged_block(NM - 1, True)

            sp.wait_ge(s_y, 8 * NM)
            for k in range(KT):
                if k >= 3:
                    sp.wait_ge(s_owl, k - 2)
                sp.dma_start(ow_raw[:, k % 3, :], io["w_out"][k]).then_inc(s_owr[k % 3], 16)
                if k == 2:
                    sp.wait_ge(s_me, 8 * NM)
                    for n in range(2):
                        sp.dma_start(gate_w[:, n, :, :], io["w_ada"][4 + n]).then_inc(s_gw[n], 16)
                    sp.dma_start(gate_b[:, :], io["b_gate"].to_broadcast([P, D])).then_inc(s_row3, 16)
                    sp.dma_start(fng[:, :], io["final_norm_g"].to_broadcast([P, D])).then_inc(s_row3, 16)
            for j in range(4):
                sp.wait_ge(s_mest[j], 16 * 2 * NM)

            def load_me(b):
                sp.dma_start(me_ld[:, :, :], (me_dram[:, :, 0:MB] if isinstance(b, int) else me_dram[:, :, bass.ds(b * MB, MB)]
                                              ).rearrange("k p n -> p k n")).then_inc(s_mel, 16)

            load_me(0)
            for u in range(2):
                sp.dma_start(x_in[:, u, :], io["x"][u * P:u * P + P, :]).then_inc(s_xin[u], 16)

            def out_block(b, final):
                if not final:
                    sp.wait_ge(s_ml, b + 1)
                    load_me(b + 1)
                for u in range(2):
                    if not final:
                        sp.wait_ge(s_add, 2 * b + u + 1)
                        sp.dma_start(x_in[:, u, :], io["x"][bass.ds((2 * b + u + 2) * P, P), :]).then_inc(s_xin[u], 16)
                for u in range(2):
                    sp.wait_ge(s_yn, 2 * b + u + 1)
                    y = io["y"][bass.ds((2 * b + u) * P, P), :] if not final else io["y"][(2 * b + u) * P:(2 * b + u + 1) * P, :]
                    sp.dma_start(y, yt[:, u, :]).then_inc(s_yst[u], 16)

            with sp.Fori(0, NM // 2) as i:
                for u in range(2):
                    out_block(2 * i + u, False)
            out_block(NM - 1, True)
            for u in range(2):
                sp.wait_ge(s_yst[u], 16 * NM)

        @block.gpsimd
        def _(pool):
            for b, (t0, n) in enumerate(BLOCKS):
                for k in range(KT):
                    e = KT * b + k
                    pool.wait_ge(s_hhi, e + 1)
                    pool.tensor_tensor(h_lo[:, k, t0:t0 + n], h32[:, e % 2, 0:n],
                                       h_hi[:, k, t0:t0 + n].bitcast(F32), ALU.subtract).then_inc(s_hlo, 1)
            with pool.Fori(0, 8) as pair:
                for x in range(6):
                    slot, step = x % 2, 6 * pair + x
                    a, b = x_rot[:, slot, 0, :], x_rot[:, slot, 1, :]
                    pool.wait_ge(s_rld[slot], 16 * 7 * (3 * pair + x // 2 + 1))
                    pool.tensor_tensor(a, a, rope[:, slot, 0, :], ALU.mult)
                    pool.tensor_tensor(b, b, rope[:, slot, 1, :], ALU.mult).then_inc(s_rm, 1)
                    pool.wait_ge(s_rm, step + 1)
                    pool.tensor_tensor(a, a, b, ALU.add).then_inc(s_rotd, 1)
                    pool.wait_ge(s_rotd, step + 1)
                    d = dec_in[:, slot, :, :]
                    pool.tensor_tensor(d, d, a.unsqueeze(1).to_broadcast([P, 2, RB]), ALU.mult).then_inc(s_rprod, 1)
            pool.wait_ge(s_gt, NT * HEADS)
            pool.wait_ge(s_z, 4)
            sums(pool, [zb[:, 4 * a, :, :] for a in range(4)], [sb[:, 4 * a, :, :] for a in range(4)]).then_inc(s_p1, 1)
            pool.wait_ge(s_p1, 1)
            turns(pool, [sb[:, 4 * a, :, :] for a in range(4)], [zb[:, 4 * c, :, :] for c in range(4)]).then_inc(s_p2, 1)
            pool.wait_ge(s_tw, 4)
            pool.wait_ge(s_twd, 3)
            sums(pool, [sb[:, 12 + n, :, :] for n in range(4)], [zb[:, 12 + n, :, :] for n in range(4)]).then_inc(s_p3, 1)
            pool.wait_ge(s_p3, 1)
            turns(pool, [zb[:, 12 + n, :, :] for n in range(4)], [sb[:, 12 + n, :, :] for n in range(4)]).then_inc(s_p4, 1)

            def merge_block(b):
                for j in range(8):
                    pool.wait_ge(s_mest[j % 4], 16 * (2 * b + j // 4))
                    pool.wait_ge(s_yg, 8 + 8 * b + j + 1)
                    pool.tensor_tensor(me_st[:, j % 4, :], mg_ld[:, j % 4, 0, :], mg_ld[:, j % 4, 1, :], ALU.add
                                       ).then_inc(s_me, 1)

            with pool.Fori(0, NM // 2) as i:
                for u in range(2):
                    merge_block(2 * i + u)
            merge_block(NM - 1)

            def add_block(b):
                for u in range(2):
                    pool.wait_ge(s_xin[u], 16 * (b + 1))
                    pool.wait_ge(s_og3, 4 + 2 * b + u + 1)
                    pool.tensor_tensor(yt[:, u, :], yt[:, u, :], x_in[:, u, :], ALU.add).then_inc(s_add, 1)

            with pool.Fori(0, NM // 2) as i:
                for u in range(2):
                    add_block(2 * i + u)
            add_block(NM - 1)

        @block.scalar
        def _(act):
            act.wait_ge(s_cols, 1)
            act.activation(silc[:, :, :], cols[:, C_COND:C_COND + 2 * KT].rearrange("p (s k) -> p s k", s=2),
                           ACT.Silu).then_inc(s_silc, 1)

            def squares(b):
                for s in range(BLOCKS[b][1] // P):
                    act.wait_ge(s_x[s], 16 * (b + 1))
                    if b:
                        act.wait_ge(s_rs, b)
                    act.wait_ge(s_ssq, BLOCKS[b][0] // P + s)
                    act.activation(junk[:, :], xt[:, s, :], ACT.Square, accum_out=sq0[:, s:s + 1]).then_inc(s_ssq, 1)
                tiles = BLOCKS[b][1] // P
                act.wait_ge(s_ssq, BLOCKS[b][0] // P + tiles)
                act.activation(sq0[:, 0:tiles], sq0[:, 0:tiles], ACT.Sqrt, scale=1.0 / D, bias=EPS).then_inc(s_root, 1)

            squares(0)
            for b, (t0, n) in enumerate(BLOCKS):
                for k in range(KT):
                    e = KT * b + k
                    act.wait_ge(s_h32, e + 1)
                    act.activation(h_hi[:, k, t0:t0 + n], h32[:, e % 2, 0:n], ACT.Copy).then_inc(s_hhi, 1)
                if b + 1 < NB:
                    squares(b + 1)

            for b, (t0, n) in enumerate(BLOCKS):
                act.wait_ge(s_mm, b + 1)
                act.activation(r_t[:, t0:t0 + n], bank[b][0:2 * RANK, 0:n], ACT.Copy).then_inc(s_ev, 1)
            act.preload_act_table_set("natural_log_exp_and_others")
            for sec in range(2):
                with act.Fori(0, 2) as i:
                    for u in range(2):
                        unit = 4 * sec + 2 * i + u
                        for b, (t0, n) in enumerate(BLOCKS):
                            e = NB * unit + b
                            act.wait_ge(s_now, 2 * sec + i + 1)
                            act.wait_ge(s_glog, e)
                            act.wait_ge(s_g, e + 1)
                            act.activation(soft[:, 0:n], bank[5 + (NB * u + b) % 2][:, 0:n], ACT.Abs,
                                           bias=balp_now[:, u:u + 1]).then_inc(s_gabs, 1)
                            act.wait_ge(s_gabs, e + 1)
                            act.activation(soft[:, 0:n], soft[:, 0:n], ACT.Exp, scale=-1.0).then_inc(s_gexp, 1)
                            act.wait_ge(s_gexp, e + 1)
                            act.activation(soft[:, 0:n], soft[:, 0:n], ACT.Ln, bias=1.0).then_inc(s_gln, 1)
                            act.wait_ge(s_st[b], 16 * unit)
                            act.wait_ge(s_mm, A_QK + e + 1)
                            act.activation(stage_b(b), bank[b][:, 0:n], ACT.Copy,
                                           scale=DK ** -0.5 if sec == 0 else 1.0).then_inc(s_ev, 1)
                            act.wait_ge(s_est, 16 * e)
                            act.wait_ge(s_bc, e + 1)
                            for sign in range(2):
                                act.activation(decs[:, sign, 0:n], bcs[:, 0:n], ACT.Exp,
                                               scale=(1.0, -1.0)[sign] / GATE_NORM).then_inc(s_dec, 1)
            for b in range(NB):
                act.wait_ge(s_st[b], 16 * 8)
            with act.Fori(0, HEADS) as head:
                for t in range(NT):
                    if t % 3 == 0:
                        act.wait_ge(s_vst[t // 3 % 3], 16 * (2 * head + t // 9))
                    act.wait_ge(s_mm, A_V + NT * head + t + 1)
                    act.activation(stage_v(t // 3 % 3)[:, t % 3, :], bank[5 + t % 3][:, 0:DV], ACT.Copy).then_inc(s_ev, 1)
            for g in range(3):
                act.wait_ge(s_vst[g], 16 * 2 * HEADS)
            for _, func, m0, pairs in SECTIONS:
                with act.Fori(0, pairs) as i:
                    for u in range(2):
                        m = m0 + 2 * i + u
                        for b, (t0, n) in enumerate(BLOCKS):
                            act.wait_ge(s_st[b], 16 * (8 + m))
                            act.wait_ge(s_mm, A_GA + NB * m + b + 1)
                            act.activation(stage_b(b), bank[b][:, 0:n], func).then_inc(s_ev, 1)
            act.preload_act_table_set("natural_log_exp_and_others")
            act.wait_ge(s_tf, 3)
            act.activation(fac[:, :, :, :], tf[:, :, :, :], ACT.Exp, scale=1.0 / GATE_NORM).then_inc(s_fac, 1)
            act.activation(mid_e[:, :, :, :].rearrange("p d h c -> p (d h) c"), mid[:, :, :], ACT.Exp, scale=1.0 / GATE_NORM).then_inc(s_fac, 1)

            def act_head(head, n, i):
                def k_out(j):
                    act.wait_ge(s_ds, NTERM * head + max(j - 1, 0))
                    act.wait_ge(s_tr, NTERM * head + j + 1)
                    act.activation(kin[:, j % 2, :], bank[turn_bank(j)][:, 0:P], ACT.Copy).then_inc(s_kin, 1)

                def term_out(j):
                    way, c = TERMS[j]
                    act.wait_ge(s_pu, NTERM * head + max(j - 1, 0))
                    act.wait_ge(s_ds, NTERM * head + j + 1)
                    act.activation(ds_t[:, j % 2, :], bank[4 + j % 2][:, 0:DV], ACT.Copy,
                                   scale=fac_now[:, 0 if way == "f" else 1, n, c:c + 1]).then_inc(s_dt, 1)

                act.wait_ge(s_facn, i + 1)
                k_out(0)
                for j in range(B_TERMS):
                    if j + 1 < B_TERMS:
                        k_out(j + 1)
                    term_out(j)
                k_out(term["f", 0])
                for c in range(NT):
                    if ("f", c + 1) in term:
                        k_out(term["f", c + 1])
                    if ("f", c) in term:
                        term_out(term["f", c])
                    e, o = NT * head + c, bank[2 + c % 2][:, 0:DV]
                    act.wait_ge(s_on, e)
                    act.wait_ge(s_o, e + 1)
                    act.activation(junk2[:, :], o, ACT.Square, accum_out=rms[:, 0:1]).then_inc(s_sq2, 1)
                    act.wait_ge(s_sq2, e + 1)
                    act.activation(rms[:, 1:2], rms[:, 0:1], ACT.Ln, scale=1.0 / DV, bias=EPS).then_inc(s_ln2, 1)
                    act.wait_ge(s_ln2, e + 1)
                    act.activation(rms[:, 1:2], rms[:, 1:2], ACT.Exp, scale=-0.5).then_inc(s_rs2, 1)
                    act.wait_ge(s_ot, NT * head + max(c - 1, 0))
                    act.wait_ge(s_rs2, e + 1)
                    act.activation(on[:, c % 2, :], o, ACT.Copy, scale=rms[:, 1:2]).then_inc(s_on, 1)

            with act.Fori(0, HEADS // 2) as i:
                for n in range(2):
                    act_head(2 * i + n, n, i)
            act.wait_ge(s_gt, NT * HEADS)
            for n in range(2):
                act.wait_ge(s_cwm, n + 1)
                act.activation(cw[:, 2 * n:2 * n + 2, :, :], bank[n][:, :].rearrange("p (g r c) -> p g r c", g=2, r=2),
                               ACT.Copy).then_inc(s_cw, 1)
            for m, t in enumerate(Z_ORDER):
                act.wait_ge(s_zm, m + 1)
                for h in range(2):
                    ins = act.activation(zb[:, t, :, 256 * h:256 * h + 256].rearrange("p r (g c) -> p g r c", g=2),
                                         bank[2 * (m % 3) + h][:, :].rearrange("p (g r c) -> p g r c", g=2, r=2), ACT.Copy)
                ins.then_inc(s_z, 1)
            for n in (1, 2, 0, 3):
                if n:
                    act.wait_ge(s_l2, n)
                else:
                    act.wait_ge(s_p2, 1)
                for c in range(4):
                    ins = act.activation(sb[:, 4 * c + n, :, :], zb[:, 4 * c + n, :, :], ACT.Copy,
                                         scale=float(np.cos(2 * np.pi * n * c / N1)))
                ins.then_inc(s_tw, 1)

            def high(slot, out, src, value, done):
                act.wait_ge(slot, value)
                act.activation(out, src, ACT.Copy).then_inc(done, 1)

            for k in range(KA):
                high(s_pwr[k % 3], pw_hi[:, k, :], pw_raw[:, k % 3, :], 16 * (k // 3 + 1), s_pwh)

            def high_block(b, slot):
                if not isinstance(b, int):
                    act.wait_ge(s_y, 8 * (b - 1))
                for half in range(2):
                    k = slice(4 * half, 4 * half + 4)
                    high(s_og[half], in_hi[slot][:, k, :], og_ld[:, k, :], 16 * (b + 1), s_ih)
                act.activation(in_hi[slot][:, KT:KA, :], uf[:, :, bass.ds(b * MB, MB)], ACT.Copy).then_inc(s_ih, 1)

            act.wait_ge(s_fo, 17)
            high_block(0, 0)
            act.wait_ge(s_pwl, KA)
            with act.Fori(0, NM // 2) as i:
                for u in range(2):
                    high_block(2 * i + u + 1, 1 - u)

            act.wait_ge(s_me, 8 * NM)
            for k in range(KT):
                high(s_owr[k % 3], ow_hi[:, k, :], ow_raw[:, k % 3, :], 16 * (k // 3 + 1), s_owh)
            high(s_mel, me_hi[0][:, :, :], me_ld[:, :, :], 16, s_mh)

            def root_block(b, slot, final):
                if not final:
                    act.wait_ge(s_out, 2 * b)
                    high(s_mel, me_hi[1 - slot][:, :, :], me_ld[:, :, :], 16 * (b + 2), s_mh)
                for u in range(2):
                    e = 2 * b + u
                    act.wait_ge(s_add, e + 1)
                    act.wait_ge(s_sq3, e)
                    act.wait_ge(s_yn, 2 * b)
                    act.activation(junk3[:, :], yt[:, u, :], ACT.Square, accum_out=rms3[:, u, 0:1]).then_inc(s_sq3, 1)
                    act.wait_ge(s_sq3, e + 1)
                    act.activation(rms3[:, u, 1:2], rms3[:, u, 0:1], ACT.Ln, scale=1.0 / D, bias=EPS).then_inc(s_ln3, 1)
                    act.wait_ge(s_ln3, e + 1)
                    act.activation(rms3[:, u, 1:2], rms3[:, u, 1:2], ACT.Exp, scale=-0.5).then_inc(s_rs3, 1)

            with act.Fori(0, NM // 2) as i:
                for u in range(2):
                    root_block(2 * i + u, u, False)
            root_block(NM - 1, 0, True)

        @block.vector
        def _(dve):
            dve.wait_ge(s_rowt, 1)
            dve.tensor_copy(cols[:, 0:C_ALL], bank[7][:, 0:C_ALL]).then_inc(s_cols, 1)

            def normalise(b):
                tiles = BLOCKS[b][1] // P
                dve.wait_ge(s_root, b + 1)
                dve.wait_ge(s_xn, BLOCKS[b][0] // P)
                dve.reciprocal(rs0[:, 0:tiles], sq0[:, 0:tiles]).then_inc(s_rs, 1)
                dve.wait_ge(s_rs, b + 1)
                for s in range(tiles):
                    dve.tensor_scalar(xt[:, s, :], xt[:, s, :], rs0[:, s:s + 1], None, ALU.mult).then_inc(s_xn, 1)

            normalise(0)
            for n in range(4):
                dve.wait_ge(s_ada, n + 1)
                dve.tensor_copy(adarow[:, n * 512:(n + 1) * 512], bank[n][0:2, :]).then_inc(s_adar, 1)
            dve.wait_ge(s_adat, 1)
            dve.wait_ge(s_cols, 1)
            ada = bank[6][:, 0:32].rearrange("p (j k s) -> p j s k", j=2, s=2)
            bada = cols[:, C_BADA:C_BADA + 16].rearrange("p (j k) -> p j k", j=2)
            for s in range(2):
                dve.tensor_tensor(modu[:, 1, s, :], ada[:, 0, s, :], bada[:, 0, :], ALU.add)
                ins = dve.scalar_tensor_tensor(modu[:, 0, s, :], ada[:, 1, s, :], 1.0, bada[:, 1, :], ALU.add, ALU.add)
            ins.then_inc(s_mod, 1)
            dve.wait_ge(s_mod, 1)
            dve.tensor_tensor(modu[:, 0, :, :], modu[:, 0, :, :],
                              cols[:, C_NG:C_NG + KT].unsqueeze(1).to_broadcast([P, 2, KT]), ALU.mult).then_inc(s_mod, 1)
            dve.wait_ge(s_mod, 2)
            for b, (t0, n) in enumerate(BLOCKS):
                s = 0 if t0 < LAT else 1
                for k in range(KT):
                    e = KT * b + k
                    if e >= 2:
                        dve.wait_ge(s_hhi, e - 1)
                        dve.wait_ge(s_hlo, e - 1)
                    dve.wait_ge(s_xt, e + 1)
                    dve.tensor_scalar(h32[:, e % 2, 0:n], bank[k][:, 0:n], modu[:, 0, s, k:k + 1],
                                      modu[:, 1, s, k:k + 1], ALU.mult, ALU.add).then_inc(s_h32, 1)
                if b + 1 < NB:
                    normalise(b + 1)

            def split(slot, n, landed, pair=0):
                sl = slice(P * slot, P * slot + P)
                dve.wait_ge(s_wraw[slot], 16 * landed)
                dve.tensor_copy(w_hi[pair][:, :, sl], w_raw[:, slot, :, :]).then_inc(s_whi, 1)
                dve.wait_ge(s_whi, n + 1)
                dve.tensor_tensor(w_lo[pair][:, :, sl], w_raw[:, slot, :, :], w_hi[pair][:, :, sl].bitcast(F32),
                                  ALU.subtract).then_inc(s_wlo, 1)

            dve.wait_ge(s_hhi, KT * NB)
            dve.wait_ge(s_hlo, KT * NB)
            dve.memset(walp[:, :, :], 0.0).then_inc(s_wal0, 1)
            split(1, 0, 1)
            split(0, 1, 1)
            dve.wait_ge(s_wal, 32)
            for sec in range(2):
                with dve.Fori(0, 2) as i:
                    for u in range(2):
                        unit = 4 * sec + 2 * i + u
                        if u == 0:
                            dve.wait_ge(s_g, NB * unit)
                            dve.wait_ge(s_gabs, NB * unit)
                            dve.tensor_copy(walp_now[:, :, :], walp[:, bass.ds(unit, 2), :])
                            dve.tensor_copy(balp_now[:, :], cols[:, bass.ds(C_BAF + unit, 2)]).then_inc(s_now, 1)
                            dve.wait_ge(s_now, 2 * sec + i + 1)
                        dve.wait_ge(s_mm, A_QK + NB * unit)
                        split(1 - u, unit + 2, 2 * sec + i + 2)
                        for b, (t0, n) in enumerate(BLOCKS):
                            e = NB * unit + b
                            par, chunks, t = NB * u + b, n // P, t0 // P
                            dve.wait_ge(s_gabs, e + 1)
                            dve.tensor_scalar(logit[:, 0:n], bank[5 + par % 2][:, 0:n], balp_now[:, u:u + 1], 0.0,
                                              ALU.add, ALU.min).then_inc(s_gmin, 1)
                            dve.wait_ge(s_gmin, e + 1)
                            dve.wait_ge(s_gln, e + 1)
                            dve.tensor_tensor(logit[:, 0:n], logit[:, 0:n], soft[:, 0:n], ALU.subtract).then_inc(s_glog, 1)
                            dve.wait_ge(s_glog, e + 1)
                            for c in range(chunks):
                                x, y = logit[:, c * P:c * P + P], cum[:, c * P:c * P + P]
                                if sec:
                                    x, y = x[:, ::-1], y[:, ::-1]
                                ins = dve.tensor_tensor_scan(y, ones, x, 0.0, ALU.mult, ALU.add)
                            ins.then_inc(s_gcum, 1)
                            dve.wait_ge(s_gcum, e + 1)
                            cc = cum[:, 0:n].rearrange("p (c t) -> p c t", t=P)
                            mt, lt = (64, 0) if sec else (63, 127)
                            dve.tensor_copy(mid[:, bass.ds(unit, 1), t:t + chunks].rearrange("p o c -> p (o c)"), cc[:, :, mt])
                            dve.tensor_copy(last[:, bass.ds(unit, 1), t:t + chunks].rearrange("p o c -> p (o c)"), cc[:, :, lt])
                            dve.wait_ge(s_dec, 2 * e)
                            dve.tensor_tensor(bcs[:, 0:n].rearrange("p (c t) -> p c t", t=P), cc,
                                              cc[:, :, mt:mt + 1].to_broadcast([P, chunks, P]),
                                              ALU.subtract).then_inc(s_bc, 1)
            dve.wait_ge(s_mm, A_V)
            split(1, 10, 6)
            dve.wait_ge(s_est, 16 * 8 * NB)
            for h in range(1, HEADS):
                if h > 1:
                    dve.wait_ge(s_mm, A_V + NT * (h - 1))
                for u in range(2):
                    split(u, 9 + 2 * h + u, 5 + h + u, pair=h % 2)
            dve.wait_ge(s_mm, A_GA - NB)
            split(0, 17, 9)
            for _, _, m0, pairs in SECTIONS:
                def split_pair(i, final):
                    for u in range(2):
                        m = m0 + 2 * i + u
                        if final and u:
                            continue
                        dve.wait_ge(s_mm, A_GA + NB * m)
                        split(1 - u, 18 + m, 10 + m0 // 2 + i)

                final = m0 == 16
                with dve.Fori(0, pairs - final) as i:
                    split_pair(i, False)
                if final:
                    split_pair(pairs - 1, True)
            dve.wait_ge(s_mm, A_END)
            dve.wait_ge(s_ev, A_END)
            md = mid[:, :, :].rearrange("p (d h) c -> p d h c", d=2)
            dve.tensor_tensor(tf[:, :, :, :].rearrange("p d h c -> p (d h) c"), last[:, :, :], mid[:, :, :],
                              ALU.subtract).then_inc(s_tf, 1)
            dve.memset(pb[:, NT - 1, :], 0.0)
            dve.wait_ge(s_tf, 1)
            for n, (d, a, z) in enumerate(((0, 0, LT - 1), (0, LT, NT - 1), (1, 1, LT), (1, LT + 1, NT))):
                step = 1 if d == 0 else -1
                ins = dve.tensor_tensor(tf[:, d, :, a:z], tf[:, d, :, a:z], md[:, d, :, a + step:z + step], ALU.add)
            ins.then_inc(s_tf, 2)
            dve.wait_ge(s_fac, 2)
            dve.wait_ge(s_s0, 32)

            def dve_head(head, n):
                def update(j):
                    way, c = TERMS[j]
                    if way == "b":
                        old, d = state_b(n, c), 1
                        new = fin[:, n, 1, :] if c == LT else pb[:, c - 1, :]
                        if 0 < c < LT:
                            dve.wait_ge(s_o, NT * head)
                    else:
                        old, d = state_f(n, c), 0
                        new = fin[:, n, 0, :] if c == NT - 1 else pf[:, (c + 1) % 2, :]
                        dve.wait_ge(s_o, NT * head + c)
                    dve.wait_ge(s_pu, NTERM * head + j)
                    dve.wait_ge(s_dt, NTERM * head + j + 1)
                    dve.scalar_tensor_tensor(new, old, fac_now[:, d, n, c:c + 1], ds_t[:, j % 2, :],
                                             ALU.mult, ALU.add).then_inc(s_pu, 1)

                def combine_backward(c):
                    dve.wait_ge(s_o, NT * head + max(c - 1, 0))
                    dve.wait_ge(s_sc, NT * head + c + 1)
                    dve.tensor_tensor(comb[:, c % 2, :], bank[c % 2][:, P:2 * P], diag2, ALU.mult).then_inc(s_cb1, 1)

                def backward_in_place(c):
                    dve.wait_ge(s_cb1, NT * head + c + 1)

                def combine_forward(c):
                    dve.copy_predicated(comb[:, c % 2, :], upper, bank[c % 2][:, 0:P]).then_inc(s_cb, 1)

                def gate(c):
                    b = min(c // 4, NB - 1)
                    at = c * P - BLOCKS[b][0]
                    if at == 0:
                        dve.wait_ge(s_ogst[b % 2], 16 * ((2 if b % 2 else 3) * head + b // 2))
                    dve.wait_ge(s_ot, NT * head + c + 1)
                    for e in range(2):
                        ins = dve.scalar_tensor_tensor(og[:, b % 2, e, at:at + P], bank[7][:, e * P:e * P + P],
                                                       cols[:, C_GG + e:C_GG + e + 1], ga_ld[:, n, e, c * P:c * P + P],
                                                       ALU.mult, ALU.mult)
                    ins.then_inc(s_gt, 1)

                for j in range(B_TERMS):
                    update(j)
                combine_backward(0)
                backward_in_place(0)
                dve.memset(pad[:, :], 0.0)
                combine_forward(0)
                for c in range(NT):
                    if c + 1 < NT:
                        combine_backward(c + 1)
                        backward_in_place(c + 1)
                    if ("f", c) in term:
                        update(term["f", c])
                    else:
                        dve.memset(pad[:, :], 0.0)
                    if c + 1 < NT:
                        combine_forward(c + 1)
                    if c == 1:
                        dve.wait_ge(s_gl[n], gate_loads)
                    if c:
                        gate(c - 1)
                gate(NT - 1)

            with dve.Fori(0, HEADS // 2) as i:
                gate_loads = 16 * (i + 1)
                dve.wait_ge(s_o, 2 * NT * i)
                dve.wait_ge(s_pu, 2 * NTERM * i)
                dve.wait_ge(s_fst, 64 * i)
                dve.tensor_copy(fac_now[:, :, :, :], fac[:, :, bass.ds(2 * i, 2), :])
                dve.tensor_copy(mid_now[:, :, :, :], mid_e[:, :, bass.ds(2 * i, 2), :])
                dve.tensor_copy(first[:, :, :, :].rearrange("p n d c -> p d n c"), s0[:, :, bass.ds(2 * i, 2), :]
                                ).then_inc(s_facn, 1)
                dve.wait_ge(s_facn, i + 1)
                for n in range(2):
                    for d, c in ((0, 0), (1, LT - 1)):
                        ins = dve.tensor_scalar(first[:, n, d, :], first[:, n, d, :], mid_now[:, d, n, c:c + 1], None, ALU.mult)
                ins.then_inc(s_p0, 1)
                dve.wait_ge(s_p0, i + 1)
                for n in range(2):
                    dve_head(2 * i + n, n)
            def butterfly(n):
                dve.wait_ge(s_z, 4 * n + 4)
                sums(dve, [zb[:, 4 * a + n, :, :] for a in range(4)], [sb[:, 4 * a + n, :, :] for a in range(4)]).then_inc(s_l1, 1)
                dve.wait_ge(s_l1, n)
                turns(dve, [sb[:, 4 * a + n, :, :] for a in range(4)], [zb[:, 4 * c + n, :, :] for c in range(4)]).then_inc(s_l2, 1)

            def twiddle(n):
                dve.wait_ge(s_tw, (0, 1, 2, 4)[n])
                for c in range(1, 4):
                    sn = float(np.sin(2 * np.pi * n * c / N1))
                    z, o = zb[:, 4 * c + n, :, :], sb[:, 4 * c + n, :, :]
                    dve.scalar_tensor_tensor(o[:, 0, :], z[:, 1, :], sn, o[:, 0, :], ALU.mult, ALU.add)
                    ins = dve.scalar_tensor_tensor(o[:, 1, :], z[:, 0, :], -sn, o[:, 1, :], ALU.mult, ALU.add)
                ins.then_inc(s_twd, 1)

            def second(c):
                sums(dve, [sb[:, 4 * c + n, :, :] for n in range(4)], [zb[:, 4 * c + n, :, :] for n in range(4)]).then_inc(s_l3, 1)
                dve.wait_ge(s_l3, c + 1)
                turns(dve, [zb[:, 4 * c + n, :, :] for n in range(4)], [sb[:, 4 * c + d, :, :] for d in range(4)]).then_inc(s_l4, 1)

            def gate_latents(c):
                for d in range(4):
                    dve.wait_ge(s_f, 4 * c + d + 1)
                    y = uf[:, :, 0:LAT].rearrange("p g (k s) -> p g s k", s=N1)[:, :, c + 4 * d, :]
                    dve.tensor_tensor(y, bank[4 * (c % 2) + d][:, :].rearrange("p (g k) -> p g k", g=4), y, ALU.mult).then_inc(s_fo, 1)

            butterfly(1)
            butterfly(2)
            twiddle(1)
            butterfly(3)
            twiddle(2)
            twiddle(3)
            dve.wait_ge(s_twd, 3)
            dve.wait_ge(s_tw, 4)
            second(0)
            dve.wait_ge(s_gb, 16 * GROUPS)
            dve.wait_ge(s_cx, 1)
            for h in range(2):
                y = uf[:, 2 * h:2 * h + 2, LAT:TOK]
                ins = dve.tensor_tensor(y, bank[6 + h][:, :].rearrange("p (g k) -> p g k", g=2), y, ALU.mult)
            ins.then_inc(s_fo, 1)
            second(1)
            gate_latents(0)
            second(2)
            for c in range(1, 4):
                gate_latents(c)

            def low(out, raw, hi, count, value, done):
                dve.wait_ge(count, value)
                return dve.tensor_tensor(out, raw, hi.bitcast(F32), ALU.subtract).then_inc(done, 1)

            for k in range(KA):
                low(pw_lo[:, k, :], pw_raw[:, k % 3, :], pw_hi[:, k, :], s_pwh, k + 1, s_pwl)

            def low_block(b, slot):
                for half in range(2):
                    k = slice(4 * half, 4 * half + 4)
                    low(in_lo[slot][:, k, :], og_ld[:, k, :], in_hi[slot][:, k, :], s_ih, 3 * b + half + 1, s_il)
                low(in_lo[slot][:, KT:KA, :], uf[:, :, bass.ds(b * MB, MB)], in_hi[slot][:, KT:KA, :], s_ih, 3 * b + 3, s_il)

            def gate_block(b):
                for j in range(8):
                    dve.wait_ge(s_mg[j % 4], 16 * (2 * b + j // 4 + 1))
                    dve.wait_ge(s_y, 8 * b + j + 1)
                    m = mg_ld[:, j % 4, :, :].rearrange("p a n -> p (a n)")
                    dve.tensor_tensor(m, bank[j][:, :], m, ALU.mult).then_inc(s_yg, 1)

            dve.wait_ge(s_fo, 17)
            dve.wait_ge(s_pwl, KA)
            dve.memset(pad[:, :], 0.0).then_inc(s_yg, 8)
            low_block(0, 0)
            with dve.Fori(0, NM // 2) as i:
                for u in range(2):
                    low_block(2 * i + u + 1, 1 - u)
                    gate_block(2 * i + u)
            gate_block(NM - 1)

            dve.wait_ge(s_me, 8 * NM)
            dve.tensor_copy(silb[:, :, :, :], silc[:, :, :].unsqueeze(3).to_broadcast([P, 2, KT, P])).then_inc(s_silb, 1)
            for k in range(KT):
                low(ow_lo[:, k, :], ow_raw[:, k % 3, :], ow_hi[:, k, :], s_owh, k + 1, s_owl)
            dve.wait_ge(s_row3, 32)
            for n in range(4):
                s, h = n // 2, n % 2
                dve.wait_ge(s_gm3, n + 1)
                dve.tensor_tensor(res_gate[:, s, 512 * h:512 * h + 512], bank[n][:, :], gate_b[:, 512 * h:512 * h + 512],
                                  ALU.add).then_inc(s_gate, 1)
            dve.wait_ge(s_gate, 4)
            dve.memset(pad[:, :], 0.0).then_inc(s_og3, 4)
            low(me_lo[0][:, :, :], me_ld[:, :, :], me_hi[0][:, :, :], s_mh, 1, s_ml)

            def finish_block(b, slot, final):
                if not final:
                    low(me_lo[1 - slot][:, :, :], me_ld[:, :, :], me_hi[1 - slot][:, :, :], s_mh, b + 2, s_ml)
                for u in range(2):
                    dve.wait_ge(s_yst[u], 16 * b)
                    dve.wait_ge(s_out, 2 * b + u + 1)
                    for h in range(2):
                        sl = slice(512 * h, 512 * h + 512)
                        ins = dve.tensor_tensor(yt[:, u, sl], bank[4 * slot + 2 * u + h][:, :], res_gate[:, int(final), sl], ALU.mult)
                    ins.then_inc(s_og3, 1)
                for u in range(2):
                    dve.wait_ge(s_rs3, 2 * b + u + 1)
                    dve.scalar_tensor_tensor(yt[:, u, :], yt[:, u, :], rms3[:, u, 1:2], fng[:, :], ALU.mult, ALU.mult
                                             ).then_inc(s_yn, 1)

            with dve.Fori(0, NM // 2) as i:
                for u in range(2):
                    finish_block(2 * i + u, u, False)
            finish_block(NM - 1, 0, True)

        @block.tensor
        def _(pe):
            pe.wait_ge(s_const, 16)
            pe.wait_ge(s_rows, 16 * 7)
            pe.transpose(bank[7][:, 0:C_ALL], rows, ident[0:C_ALL, 0:C_ALL]).then_inc(s_rowt, 1)
            pe.wait_ge(s_silc, 1)
            for n in range(4):
                pe.wait_ge(s_wada[n % 2], 16 * (n // 2 + 1))
                for k in range(KT):
                    ins = pe.matmul(bank[n][0:2, :], silc[:, :, k], wada[:, n % 2, k, :], start=(k == 0), stop=(k == KT - 1))
                ins.then_inc(s_ada, 1)
            pe.wait_ge(s_adar, 4)
            for j in range(16):
                ins = pe.transpose(bank[6][:, 2 * j:2 * j + 2], adarow[:, j * P:(j + 1) * P], ident[0:2, 0:2])
            ins.then_inc(s_adat, 1)
            for b, (t0, n) in enumerate(BLOCKS):
                tiles = n // P
                for k in range(KT):
                    if k == 0:
                        pe.wait_ge(s_xn, t0 // P + tiles)
                    if b:
                        pe.wait_ge(s_h32, KT * (b - 1) + k + 1)
                    elif k == 6:
                        pe.wait_ge(s_mod, 2)
                    for s in range(tiles):
                        ins = pe.transpose(bank[k][:, s * P:(s + 1) * P], xt[:, s, k * P:(k + 1) * P], ident)
                    ins.then_inc(s_xt, 1)

            def unit_block(slot, b, a):
                t0, n = BLOCKS[b]
                sl = slice(P * slot, P * slot + P)
                pe.wait_ge(s_ev, a - (NB - 1))
                for k in range(KT):
                    for w, h in ((w_hi, h_hi), (w_hi, h_lo), (w_lo, h_hi)):
                        ins = pe.matmul(bank[b][:, 0:n], w[0][:, k, sl], h[:, k, t0:t0 + n],
                                        start=(k == 0 and w is w_hi and h is h_hi), stop=(k == KT - 1 and w is w_lo))
                ins.then_inc(s_mm, 1)

            pe.wait_ge(s_wlo, 1)
            for b in range(NB):
                pe.wait_ge(s_h32, KT * (NB - 1) + b + 1)
                pe.wait_ge(s_hlo, KT * (b + 1))
                unit_block(1, b, NB - 1)
            pe.wait_ge(s_h32, KT * NB)
            for sec in range(2):
                with pe.Fori(0, 2) as i:
                    for u in range(2):
                        unit = 4 * sec + 2 * i + u
                        for b, (t0, n) in enumerate(BLOCKS):
                            e = NB * unit + b
                            pe.wait_ge(s_now, 2 * sec + i + 1)
                            lag = 0 if (sec, u, b) == (0, 0, 0) else 1
                            pe.wait_ge(s_gabs, e - lag)
                            pe.wait_ge(s_gmin, e - lag)
                            if (sec, u, b) == (0, 0, 0):
                                pe.wait_ge(s_ev, NB)
                            pe.matmul(bank[5 + (NB * u + b) % 2][:, 0:n], walp_now[:, u, :], r_t[:, t0:t0 + n],
                                      start=True, stop=True).then_inc(s_g, 1)
                            if b == 0:
                                pe.wait_ge(s_wlo, unit + 2)
                            unit_block(u, b, A_QK + e)
            pe.wait_ge(s_gabs, 8 * NB)
            pe.wait_ge(s_gmin, 8 * NB)
            with pe.Fori(0, 2) as i:
                for pair in range(2):
                    head = 2 * i + pair
                    pe.wait_ge(s_wlo, 11 + 2 * head)
                    for t in range(NT):
                        pe.wait_ge(s_ev, A_V + NT * head + t - 2)
                        for k in range(KT):
                            for h, w in ((h_hi, w_hi), (h_hi, w_lo), (h_lo, w_hi)):
                                ins = pe.matmul(bank[5 + t % 3][:, 0:DV], h[:, k, t * P:t * P + P], w[pair][:, k, :],
                                                start=(k == 0 and h is h_hi and w is w_hi), stop=(k == KT - 1 and h is h_lo))
                        ins.then_inc(s_mm, 1)
            with pe.Fori(0, 16) as i:
                for u in range(2):
                    m = 2 * i + u
                    pe.wait_ge(s_wlo, 18 + m)
                    for b in range(NB):
                        unit_block(u, b, A_GA + NB * m + b)
            pe.wait_ge(s_ev, A_END)

            def pe_head(head, n, i):
                landed = 16 * (i + 1)

                def turn(j):
                    way, c = TERMS[j]
                    pe.wait_ge(s_kin, NTERM * head + (max(j - 1, 0) if way == "b" else j))
                    pe.transpose(bank[turn_bank(j)][:, 0:P], kk[n][:, 1 if way == "b" else 0, c * P:c * P + P],
                                 ident).then_inc(s_tr, 1)

                def state_term(j):
                    pe.wait_ge(s_dt, NTERM * head + max(j - 1, 0))
                    pe.wait_ge(s_kin, NTERM * head + j + 1)
                    pe.matmul(bank[4 + j % 2][:, 0:DV], kin[:, j % 2, :], v_ld[:, n, TERMS[j][1], :], start=True, stop=True
                              ).then_inc(s_ds, 1)

                def scores(c):
                    pe.wait_ge(s_cb, NT * head + max(c - 1, 0))
                    for d in range(2):
                        ins = pe.matmul(bank[c % 2][:, d * P:d * P + P], kk[n][:, d, c * P:c * P + P],
                                        qd[n][:, d, c * P:c * P + P], start=True, stop=True)
                    ins.then_inc(s_sc, 1)

                def output(c):
                    out = bank[2 + c % 2][:, 0:DV]
                    pe.wait_ge(s_on, NT * head + max(c - 1, 0))
                    pe.wait_ge(s_pu, NTERM * head + (term["f", c - 1] + 1 if ("f", c - 1) in term else
                                                     term["f", c - 2] + 1 if c else B_TERMS))
                    pe.wait_ge(s_cb, NT * head + c + 1)
                    pe.matmul(out, comb[:, c % 2, :], v_ld[:, n, c, :], start=True, stop=False)
                    pe.matmul(out, qd[n][:, 0, c * P:c * P + P], state_f(n, c), start=False, stop=False)
                    pe.matmul(out, qd[n][:, 1, c * P:c * P + P], state_b(n, c), start=False, stop=True).then_inc(s_o, 1)

                def turn_output(c):
                    pe.wait_ge(s_gt, NT * head + c)
                    pe.wait_ge(s_on, NT * head + c + 1)
                    for e in range(2):
                        ins = pe.transpose(bank[7][:, e * P:e * P + P], on[:, c % 2, e * P:e * P + P], ident)
                    ins.then_inc(s_ot, 1)

                pe.wait_ge(s_cb, NT * head)
                pe.wait_ge(s_kl[n], landed)
                turn(0)
                pe.wait_ge(s_vl[n], landed)
                pe.wait_ge(s_p0, i + 1)
                for j in range(B_TERMS):
                    if j + 1 < B_TERMS:
                        turn(j + 1)
                    state_term(j)
                turn(term["f", 0])
                pe.wait_ge(s_ql[n], landed)
                scores(0)
                for c in range(NT):
                    if ("f", c + 1) in term:
                        turn(term["f", c + 1])
                    if c + 1 < NT:
                        scores(c + 1)
                    if ("f", c) in term:
                        state_term(term["f", c])
                    output(c)
                    if c:
                        turn_output(c - 1)
                turn_output(NT - 1)

            with pe.Fori(0, HEADS // 2) as i:
                for n in range(2):
                    pe_head(2 * i + n, n, i)
            pe.wait_ge(s_gt, NT * HEADS)
            pe.wait_ge(s_ftab, 64)
            for g in range(GROUPS):
                for r in range(2):
                    ins = pe.matmul(bank[g // 2][:, 256 * (g % 2) + P * r:256 * (g % 2) + P * r + P], chan[:, r, :], w4[:, g, :],
                                    start=True, stop=True)
                if g % 2:
                    ins.then_inc(s_cwm, 1)
            pe.wait_ge(s_u, 16 * GROUPS)
            pe.wait_ge(s_cw, 2)
            for m, t in enumerate(Z_ORDER):
                if m >= 3:
                    pe.wait_ge(s_z, m - 2)
                for g in range(GROUPS):
                    ins = pe.matmul(bank[2 * (m % 3) + g // 2][:, 256 * (g % 2):256 * (g % 2) + 256], uf[:, g, t * P:t * P + P],
                                    cw[:, g, :, :].rearrange("p r c -> p (r c)"), start=True, stop=True)
                ins.then_inc(s_zm, 1)
            pe.wait_ge(s_z, NT)
            for g in range(GROUPS):
                for n in range(4):
                    t, r = n // 2, n % 2
                    ins = pe.matmul(bank[6 + g // 2][:, 256 * (g % 2):256 * (g % 2) + 256], zb[:, LT + t, r, g * P:g * P + P],
                                    dft_c[:, r, t, :], start=(n == 0), stop=(n == 3))
            ins.then_inc(s_cx, 1)
            for c in range(4):
                if c < 3:
                    pe.wait_ge(s_l4, c + 1)
                else:
                    pe.wait_ge(s_p4, 1)
                if c:
                    pe.wait_ge(s_fo, 1 if c == 1 else 1 + 4 * (c - 1))
                for d in range(4):
                    for g in range(GROUPS):
                        for r in range(2):
                            ins = pe.matmul(bank[4 * (c % 2) + d][:, g * P:g * P + P], sb[:, 4 * c + d, r, g * P:g * P + P],
                                            dft[:, r, c + 4 * d, :], start=(r == 0), stop=(r == 1))
                    ins.then_inc(s_f, 1)

            def split_product(out, pairs, count):
                for k, (st, mv) in enumerate(pairs):
                    for p, (a, b) in enumerate(((0, 0), (0, 1), (1, 0))):
                        ins = pe.matmul(out, st[a], mv[b], start=(k == 0 and p == 0), stop=(k == count - 1 and p == 2))
                return ins

            def branch_block(b, slot):
                pe.wait_ge(s_il, 3 * b + 3)
                for j in range(8):
                    pe.wait_ge(s_yg, 8 * b + j + 1)
                    for a, ks in enumerate((range(0, KT), range(KT, KA))):
                        ins = split_product(bank[j][:, a * MB:a * MB + MB],
                                            [((pw_hi[:, k, j * P:j * P + P], pw_lo[:, k, j * P:j * P + P]),
                                              (in_hi[slot][:, k, :], in_lo[slot][:, k, :])) for k in ks], len(ks))
                    ins.then_inc(s_y, 1)

            with pe.Fori(0, NM // 2) as i:
                for u in range(2):
                    branch_block(2 * i + u, u)
            branch_block(NM - 1, 0)

            pe.wait_ge(s_silb, 1)
            pe.wait_ge(s_yg, 8 + 8 * NM)
            for n in range(4):
                s, h = n // 2, n % 2
                pe.wait_ge(s_gw[h], 16)
                for k in range(KT):
                    ins = pe.matmul(bank[n][:, :], silb[:, s, k, :], gate_w[:, h, k, :], start=(k == 0), stop=(k == KT - 1))
                ins.then_inc(s_gm3, 1)
            pe.wait_ge(s_owl, KT)

            def out_tiles(b, slot):
                pe.wait_ge(s_ml, b + 1)
                for u in range(2):
                    pe.wait_ge(s_og3, 2 * b + u + 1)
                    for h in range(2):
                        ins = split_product(bank[4 * slot + 2 * u + h][:, :],
                                            [((me_hi[slot][:, k, u * P:u * P + P], me_lo[slot][:, k, u * P:u * P + P]),
                                              (ow_hi[:, k, 512 * h:512 * h + 512], ow_lo[:, k, 512 * h:512 * h + 512]))
                                             for k in range(KT)], KT)
                    ins.then_inc(s_out, 1)

            with pe.Fori(0, NM // 2) as i:
                for u in range(2):
                    out_tiles(2 * i + u, u)
            out_tiles(NM - 1, 0)
    return nc


def constants():
    c = np.zeros((P, K_ALL), np.float32)
    c[:, K_ID:K_ID + P] = np.eye(P)
    c[:, K_UP:K_UP + P] = np.triu(np.ones((P, P)), 1)
    c[:, K_DW:K_DW + P] = 1 + np.eye(P)
    c[:, K_ONE:K_ONE + P] = 1
    return c


def rope_tables():
    f = DK // 4
    freqs = np.float32(10000.0) ** (-np.arange(f, dtype=np.float32) / f)
    t = np.arange(LAT)
    out = np.zeros((P, 2, TOK), np.float32)
    out[:, 0, LAT:] = 1
    for a, at in enumerate((t // 64, t % 64)):
        ang = freqs[:, None] * at[None].astype(np.float32)
        for half in range(2):
            rows = slice(64 * a + 32 * half, 64 * a + 32 * half + 32)
            out[rows, 0, :LAT] = np.cos(ang)
            out[rows, 1, :LAT] = np.sin(ang) * (1 if half else -1)
    return out


def fourier_tables():
    n = np.arange(P)
    ang = 2 * np.pi * np.outer(n, n) / P
    chan = np.stack([np.cos(ang), -np.sin(ang)], 1)
    k = N1 * n[None, :] + np.arange(N1)[:, None]
    ang = 2 * np.pi * (n[:, None, None] * k[None] % LAT) / LAT
    dft = np.stack([np.cos(ang), np.sin(ang)], 1) / np.sqrt(LAT * P)
    t = np.arange(CTX).reshape(CTX // P, P).T
    ang = 2 * np.pi * (t[:, :, None] * np.arange(CTX) % CTX) / CTX
    dft_c = np.stack([np.cos(ang), np.sin(ang)], 1) / np.sqrt(CTX * P)
    return {"chan": chan.astype(np.float32), "dft": dft.astype(np.float32), "dft_c": dft_c.astype(np.float32)}


def layout(a):
    w_in = a["w_in"][0]
    ranks = 2 * HEADS * DK + 2 * HEADS * DV
    order = np.concatenate([np.arange(ranks, ranks + P), np.arange(ranks), np.arange(ranks + 2 * RANK, w_in.shape[1])])
    tiles = lambda w, c: w.reshape(w.shape[0] // P, P, -1, c).transpose(2, 1, 0, 3)
    return {
        "consts": constants(), "rope": rope_tables(), **fourier_tables(),
        "w_four": a["w_four"][0].transpose(1, 0, 2), "b_gate": a["b_ada"][:, 2 * D:], "final_norm_g": a["final_norm_g"][None],
        "w_proj_a": a["w_proj_a"][0].reshape(KT, P, D), "w_proj_b": a["w_proj_b"][0].reshape(GROUPS, P, D),
        "w_out": a["w_out"][0].reshape(KT, P, D),
        "state_fwd": a["state_gla_fwd"][0, 0], "state_bwd": a["state_gla_bwd"][0, 0],
        "x": np.concatenate([a["x_sample"][0], a["x_prompt"][0]]),
        "c": a["c"].reshape(8, P), "c_ctx": a["c_ctx"].reshape(8, P), "norm_g": a["norm_g"].reshape(8, P),
        "b_ada": a["b_ada"].reshape(24, P), "gla_norm_g": a["gla_norm_g"].reshape(2, P),
        "b_alpha_fwd": a["b_alpha_fwd"].reshape(4, P), "b_alpha_bwd": a["b_alpha_bwd"].reshape(4, P),
        "w_ada": tiles(a["w_ada"][0], 512),
        "w_in": tiles(w_in[:, order], P),
        "w_alpha_fwd": a["w_alpha_fwd"].reshape(RANK, 4, P), "w_alpha_bwd": a["w_alpha_bwd"].reshape(RANK, 4, P),
    }


OUTS = {"y": (TOK, D), "new_fwd": (HEADS, DK, DV), "new_bwd": (HEADS, DK, DV)}


def kernel(**inputs):
    import concourse.bacc as bacc
    from concourse.bass_utils import run_bass_kernel_spmd

    nc = bacc.Bacc("TRN2", target_bir_lowering=False, num_devices=1)
    arrays = {"in_" + k: np.ascontiguousarray(v) for k, v in layout({k: np.asarray(v) for k, v in inputs.items()}).items()}
    io = {k[3:]: nc.dram_tensor(k, v.shape, mybir.dt.from_np(v.dtype), kind="ExternalInput").ap() for k, v in arrays.items()}
    for k, shape in OUTS.items():
        io[k] = nc.dram_tensor(k, shape, F32, kind="ExternalOutput").ap()
    build(nc, io, lambda name, shape: nc.dram_tensor(name, shape, F32, kind="Internal").ap())
    out = run_bass_kernel_spmd(nc, [arrays], core_ids=[0]).results[0]
    y = out["y"]
    return (y[LAT:][None], y[:LAT][None], out["new_fwd"][None, None], out["new_bwd"][None, None])
```

```python
from contextlib import ExitStack

import numpy as np

import concourse.bass as bass
from concourse import mybir

F32 = mybir.dt.float32
F32R = mybir.dt.float32r
BF16 = mybir.dt.bfloat16
U32 = mybir.dt.uint32
ALU = mybir.AluOpType
ACT = mybir.ActivationFunctionType

P = 128
D = 1024
KT = D // P
LAT, CTX = 2048, 256
TOK = LAT + CTX
NT = TOK // P
LT = LAT // P
HEADS, DK, DV = 4, 128, 256
BLOCKS = [(0, 512), (512, 512), (1024, 512), (1536, 512), (2048, 256)]
NB = len(BLOCKS)
RANK = 16
GATE_NORM = 16.0
EPS = 1e-6
GROUPS = 4
N1 = 16
RB = 384
KA = KT + GROUPS
MB = 256
NM = TOK // MB
UNITS = 49

C_COND, C_NG, C_BADA, C_GG, C_BAF, C_BAB, C_ALL = 0, 16, 24, 48, 50, 54, 58
K_ID, K_UP, K_DW, K_ONE, K_ALL = 0, 128, 256, 384, 512


def build(nc, io, scratch):
    q_dram = scratch("qk_dram", [8, P, TOK])
    v_dram = scratch("v_dram", [4, P, NT, DV])
    e_dram = scratch("e_dram", [4, P, 2, 2, TOK])
    qk_dec = scratch("qk_dec", [8, P, 2, TOK])
    ga_dram = scratch("ga_dram", [8, P, TOK])
    u_dram = scratch("u_dram", [4, P, TOK])
    gb_dram = scratch("gb_dram", [4, P, TOK])
    mg_dram = scratch("mg_dram", [16, P, TOK])
    og_dram = scratch("og_dram", [8, P, TOK])
    gate_dram = scratch("gate_dram", [2, D])
    me_dram = scratch("me_dram", [8, P, TOK])

    ctx = ExitStack()
    with ctx:
        base = (nc.sbuf_base + 31) // 32 * 32
        end = nc.sbuf_usable_end

        class Region:

            def __init__(self, start):
                self.at = start

            def __call__(self, name, shape, dt=F32):
                size = int(np.prod(shape[1:])) * (2 if dt == BF16 else 4)
                t = nc.alloc_sbuf_tensor_at(name, shape, dt, offset=self.at)
                self.at += (size + 31) // 32 * 32
                assert self.at <= end, (name, self.at, end)
                return t

        def sem(name):
            return ctx.enter_context(nc.semaphore(name))

        bank = [ctx.enter_context(nc.psum_tensor(f"bank{n}", [P, 512], F32)) for n in range(8)]

        keep = Region(base)
        consts = keep("consts", [P, K_ALL])
        ident = consts[:, K_ID:K_ID + P]
        upper = consts[:, K_UP:K_UP + P].bitcast(U32)
        diag2 = consts[:, K_DW:K_DW + P]
        ones = consts[:, K_ONE:K_ONE + P]
        cols = keep("cols", [P, 64])
        silc = keep("silc", [P, 2, KT])
        modu = keep("modu", [P, 2, 2, KT])
        mid = keep("mid", [P, 8, NT])
        last = keep("last", [P, 8, NT])
        pad = keep("pad", [P, 1])
        kept = keep.at

        act_in = Region(kept)
        h_hi = act_in("h_hi", [P, KT, TOK], F32R)
        adarow = Region(act_in.at)("adarow", [2, 2048])
        h_lo = act_in("h_lo", [P, KT, TOK], F32R)
        after_h = act_in.at
        second = after_h + 2 * KT * 2 * P * 4
        r0 = Region(after_h)
        wada = [r0("wada0", [P, KT, 512]), r0("wada1", [P, KT, 512])]
        x_odd = Region(r0.at - KT * 2048)("x_odd", [P, 4, D])
        x_even = [r0("x_even0", [P, 2, D])]
        h32 = [r0("h32_0", [P, 512])]
        r0.at = second + 16384 + 1056 + TOK * 4
        junk = r0("junk", [P, D], BF16)
        gate_row = r0("gate_row", [2, 512])
        w_raw1_at = r0.at
        r0.at += KT * P * 4
        x_even.append(r0("x_even1", [P, 2, D]))
        h32.append(r0("h32_1", [P, 512]))
        rows = h32[0][0:C_ALL, 0:P]
        sq0 = r0("sq0", [P, 4])
        rs0 = r0("rs0", [P, 4])

        def x_tile(b, s):
            return x_odd[:, s, :] if b % 2 else x_even[s // 2][:, s % 2, :]

        r1 = Region(after_h)
        w_hi = [r1("w_hi0", [P, KT, 2 * P], F32R)]
        w_lo = [r1("w_lo0", [P, KT, 2 * P], F32R)]
        assert second == r1.at
        w_hi.append(r1("w_hi1", [P, KT, 2 * P], F32R))
        w_lo.append(r1("w_lo1", [P, KT, 2 * P], F32R))
        r1.at += 1056
        r_t = r1("r_t", [96, TOK], F32R)
        w_raw = r1("w_raw", [P, 2, KT, P])
        assert r1.at - KT * P * 4 == w_raw1_at
        stage = r1("stage", [P, NB * 512])
        rg = Region(second)
        walp = rg("walp", [96, 8, P], F32R)
        walp_now = rg("walp_now", [96, 2, P], F32R)
        balp_now = rg("balp_now", [P, 2])
        walp_raw = Region(rg.at)("walp_raw", [96, 8, P])
        soft = rg("soft", [P, 512])
        logit = rg("logit", [P, 512])
        cum = rg("cum", [P, 512])
        bcs = rg("bcs", [P, 512])
        decs = rg("decs", [P, 2, 512])
        assert rg.at <= second + 17440
        rp = Region(second)
        x_rot = rp("x_rot", [P, 2, 2, RB])
        rope = rp("rope", [P, 2, 2, RB])
        dec_in = rp("dec_in", [P, 2, 2, RB])

        def stage_b(b):
            return stage[:, 512 * b:512 * b + BLOCKS[b][1]]

        def stage_v(g):
            return stage[:, 768 * g:768 * g + 768].rearrange("p (t c) -> p t c", t=3)

        r2 = Region(kept)
        v_ld, qd, ga_ld = zip(*((r2(f"v_ld{n}", [P, NT, DV]), r2(f"qd{n}", [P, 2, TOK]), r2(f"ga_ld{n}", [P, 2, TOK]))
                                for n in range(2)))
        kk = [None, r2("kk1", [P, 2, TOK])]
        pb = r2("pb", [P, NT, DV])
        pf = r2("pf", [P, 2, DV])
        kin = r2("kin", [P, 2, P])
        comb = r2("comb", [P, 2, P])
        ds_t = r2("ds_t", [P, 2, DV])
        junk2 = r2("junk2", [P, DV], BF16)
        rms = r2("rms", [P, 2])
        on = r2("on", [P, 2, DV])
        tf = r2("tf", [P, 2, HEADS, NT])
        fac = r2("fac", [P, 2, HEADS, NT])
        mid_e = r2("mid_e", [P, 2, HEADS, NT])
        fac_now = r2("fac_now", [P, 2, 2, NT])
        mid_now = r2("mid_now", [P, 2, 2, NT])
        assert r2.at <= second, (r2.at, second)
        r2.at = second
        kk[0] = r2("kk0", [P, 2, TOK])
        og = r2("og", [P, 2, 2, 512])
        first = r2("first", [P, 2, 2, DV])
        after_first = r2.at
        s0 = r2("s0", [P, 2, HEADS, DV])
        fin = r2("fin", [P, 2, 2, DV])

        TERMS = [("b", c) for c in [*range(LT - 1, 0, -1), NT - 1, LT]] + [("f", c) for c in range(NT) if c != LT - 1]
        term = {t: j for j, t in enumerate(TERMS)}
        NTERM = len(TERMS)
        B_TERMS = LT + 1

        r3 = Region(kept)
        uf = r3("uf", [P, GROUPS, TOK])
        dft = r3("dft", [P, 2, N1, P])
        w4 = r3("w4", [P, GROUPS, P])
        assert r3.at <= kept + 4 * 3 * TOK * 2
        at_z = r3.at
        zb = r3("zb", [P, NT, 2, 512])
        at_s = r3.at
        sb = r3("sb", [P, N1, 2, 512])
        r3.at = max(r3.at, after_first)
        chan = r3("chan", [P, 2, P])
        cw = r3("cw", [P, GROUPS, 2, P])
        dft_c = r3("dft_c", [P, 2, CTX // P, CTX])

        u_sum = Region(second)("u_sum", [P, 2, GROUPS, 4 * P])

        r4 = Region(at_z)
        pw_hi = r4("pw_hi", [P, KA, D], F32R)
        pw_raw = Region(r4.at)("pw_raw", [P, 6, D])
        in_hi1, in_lo1 = (r4(f"in_{part}1", [P, KA, MB], F32R) for part in ("hi", "lo"))
        assert r4.at <= at_s
        r4.at = at_s
        pw_lo = r4("pw_lo", [P, KA, D], F32R)
        in_lo0 = r4("in_lo0", [P, KA, MB], F32R)
        mg_ld = r4("mg_ld", [P, 4, 2, MB])
        og_ld = r4("og_ld", [P, KT, MB])
        at_og = r4.at - KT * MB * 4
        r4 = Region(kept + GROUPS * TOK * 4)
        in_hi0 = r4("in_hi0", [P, KA, MB], F32R)
        me_st = r4("me_st", [P, 4, MB])
        assert r4.at <= at_z
        in_hi, in_lo = (in_hi0, in_hi1), (in_lo0, in_lo1)

        ow_raw = Region(kept)("ow_raw", [P, KT, D])
        me_ld = Region(at_og)("me_ld", [P, KT, MB])
        r5 = Region(at_z)
        ow_hi = r5("ow_hi", [P, KT, D], F32R)
        ow_lo = r5("ow_lo", [P, KT, D], F32R)
        me_hi = [r5(f"me_hi{n}", [P, KT, MB], F32R) for n in range(2)]
        me_lo = [r5(f"me_lo{n}", [P, KT, MB], F32R) for n in range(2)]
        x_in = r5("x_in", [P, 2, D])
        yt = r5("yt", [P, 2, D])
        assert r5.at <= at_og
        r5 = Region(at_og + KT * MB * 4)
        rms3 = r5("rms3", [P, 2, 2])
        r5 = Region(kept + KT * D * 4)
        fng = r5("fng", [P, D])
        gate_b = r5("gate_b", [P, D])
        res_gate = r5("res_gate", [P, 2, D])
        junk3 = r5("junk3", [P, D], BF16)
        assert r5.at <= at_z

        s_const, s_rows = sem("s_const"), sem("s_rows")
        s_x = [[sem(f"s_x{m}{n}") for n in range(2)] for m in range(2)]
        s_gr, s_grst = sem("s_gr"), sem("s_grst")
        s_wada = [sem(f"s_wada{n}") for n in range(2)]
        s_rowt, s_cols, s_silc = sem("s_rowt"), sem("s_cols"), sem("s_silc")
        s_ada, s_adar, s_adat, s_mod = sem("s_ada"), sem("s_adar"), sem("s_adat"), sem("s_mod")
        s_ssq, s_root, s_rs, s_xn = sem("s_ssq"), sem("s_root"), sem("s_rs"), sem("s_xn")
        s_xt, s_h32, s_hhi, s_hlo, s_hld = sem("s_xt"), sem("s_h32"), sem("s_hhi"), sem("s_hlo"), sem("s_hld")
        s_wraw = [sem(f"s_wraw{n}") for n in range(2)]
        s_whi, s_wlo = sem("s_whi"), sem("s_wlo")
        s_mm = sem("s_mm")
        s_ev = sem("s_ev")
        s_st = [sem(f"s_st{n}") for n in range(NB)]
        s_vst = [sem(f"s_vst{n}") for n in range(3)]
        s_rlo, s_wsp = sem("s_rlo"), sem("s_wsp")
        s_wal0, s_wal, s_now = sem("s_wal0"), sem("s_wal"), sem("s_now")
        s_g = sem("s_g")
        s_gabs, s_gexp, s_gln = sem("s_gabs"), sem("s_gexp"), sem("s_gln")
        s_gmin, s_glog, s_gcum, s_bc = sem("s_gmin"), sem("s_glog"), sem("s_gcum"), sem("s_bc")
        s_dec, s_est = sem("s_dec"), sem("s_est")
        s_rld = [sem(f"s_rld{n}") for n in range(2)]
        s_rm, s_rotd, s_rprod = sem("s_rm"), sem("s_rotd"), sem("s_rprod")
        s_rst = [sem(f"s_rst{n}") for n in range(2)]

        s_s0 = sem("s_s0")
        s_kl, s_vl, s_ql, s_gl = ([sem(f"{name}{n}") for n in range(2)] for name in ("s_kl", "s_vl", "s_ql", "s_gl"))
        s_v12 = sem("s_v12")
        s_tf, s_fac, s_facn, s_p0 = sem("s_tf"), sem("s_fac"), sem("s_facn"), sem("s_p0")
        s_tr, s_kin, s_ds, s_dt, s_pu = sem("s_tr"), sem("s_kin"), sem("s_ds"), sem("s_dt"), sem("s_pu")
        s_sc, s_cb1, s_cb, s_o = sem("s_sc"), sem("s_cb1"), sem("s_cb"), sem("s_o")
        s_sq2, s_ln2, s_rs2, s_on, s_ot, s_gt = (sem("s_sq2"), sem("s_ln2"), sem("s_rs2"), sem("s_on"), sem("s_ot"),
                                                 sem("s_gt"))
        s_ogst = [sem(f"s_ogst{n}") for n in range(2)]
        s_fst = sem("s_fst")

        s_ctab, s_ftab, s_u, s_gb = sem("s_ctab"), sem("s_ftab"), sem("s_u"), sem("s_gb")
        s_cwm, s_cw, s_zm, s_z = sem("s_cwm"), sem("s_cw"), sem("s_zm"), sem("s_z")
        s_ub = sem("s_ub")
        s_l2, s_l3, s_l4 = sem("s_l2"), sem("s_l3"), sem("s_l4")
        s_p2, s_p3, s_p4 = sem("s_p2"), sem("s_p3"), sem("s_p4")
        s_tw, s_twd, s_cx, s_f, s_fo = sem("s_tw"), sem("s_twd"), sem("s_cx"), sem("s_f"), sem("s_fo")
        s_pwr = [sem(f"s_pwr{n}") for n in range(3)]
        s_pwh, s_pwl, s_pwp = sem("s_pwh"), sem("s_pwl"), sem("s_pwp")
        s_og = [sem(f"s_og{n}") for n in range(2)]
        s_mg = [sem(f"s_mg{n}") for n in range(4)]
        s_mest = [sem(f"s_mest{n}") for n in range(4)]
        s_ih, s_il, s_y, s_yg, s_me = sem("s_ih"), sem("s_il"), sem("s_y"), sem("s_yg"), sem("s_me")
        s_owr = [sem(f"s_owr{n}") for n in range(KT // 2)]
        s_row3 = sem("s_row3")
        s_owh, s_owl, s_gate = sem("s_owh"), sem("s_owl"), sem("s_gate")
        s_mel, s_mh, s_ml, s_out, s_og3 = sem("s_mel"), sem("s_mh"), sem("s_ml"), sem("s_out"), sem("s_og3")
        s_xin = [sem(f"s_xin{n}") for n in range(2)]
        s_yst = [sem(f"s_yst{n}") for n in range(2)]
        s_add, s_rt3, s_yn = sem("s_add"), sem("s_rt3"), sem("s_yn")

        A_QK = NB
        A_V = A_QK + 8 * NB
        A_GA = A_V + 4 * NT
        A_END = A_GA + 32 * NB
        SECTIONS = ((ga_dram, ACT.Silu, 0, 4), (u_dram, ACT.Copy, 8, 2), (gb_dram, ACT.Silu, 12, 2),
                    (mg_dram, ACT.Sigmoid, 16, 8))

        LOW_POOL = range(2, KA, 3)
        LOW_DVE = (2, 5)

        def low_parts(e):
            mine = sum(x % KT in LOW_DVE for x in range(e))
            return e - mine, mine

        R_BANK = (6, 7, 0, 1, 2)

        def state_f(n, c):
            return first[:, n, 0, :] if c == 0 else pb[:, NT - 1, :] if c == LT else pf[:, c % 2, :]

        def state_b(n, c):
            return first[:, n, 1, :] if c == LT - 1 else pb[:, c, :]

        def turn_bank(j):
            return 0 if j < B_TERMS and j % 2 else 6

        Z_ORDER = [0, 1, 2, 3] + [4 * a + n for n in range(4) for a in (2, 3, 1)] + list(range(LT, NT))

        def z_home(t):
            a, n = t // 4, t % 4
            if t >= LT:
                return zb[:, t, :, :]
            if a == 0:
                return sb[:, n, :, :]
            if a == 1:
                return (zb if n else sb)[:, 8 + n, :, :]
            return (sb if n else zb)[:, (4, 12)[a - 2] + n, :, :]

        def combine(eng, n):
            src, dst = (sb, zb) if n else (zb, sb)
            h1, h3 = src[:, 4 + n, :, :], src[:, 12 + n, :, :]
            for c, (first, other) in ((1, (ALU.add, ALU.subtract)), (3, (ALU.subtract, ALU.add))):
                eng.tensor_tensor(dst[:, 4 * c + n, 0, :], h1[:, 0, :], h3[:, 1, :], first)
                ins = eng.tensor_tensor(dst[:, 4 * c + n, 1, :], h1[:, 1, :], h3[:, 0, :], other)
            return ins

        def sums(eng, z, s):
            for n in range(4):
                ins = eng.tensor_tensor(s[n], z[n // 2], z[n // 2 + 2], ALU.subtract if n % 2 else ALU.add)
            return ins

        def turns(eng, s, out):
            eng.tensor_tensor(out[0], s[0], s[2], ALU.add)
            eng.tensor_tensor(out[2], s[0], s[2], ALU.subtract)
            for n, (first, other) in ((1, (ALU.add, ALU.subtract)), (3, (ALU.subtract, ALU.add))):
                eng.tensor_tensor(out[n][:, 0, :], s[1][:, 0, :], s[3][:, 1, :], first)
                ins = eng.tensor_tensor(out[n][:, 1, :], s[1][:, 1, :], s[3][:, 0, :], other)
            return ins

        block = ctx.enter_context(nc.Block())

        @block.sync
        def _(sp):
            sp.dma_start(consts[:, :], io["consts"]).then_inc(s_const, 16)
            at = 0
            for name, n in (("c", 8), ("c_ctx", 8), ("norm_g", 8), ("b_ada", 24), ("gla_norm_g", 2),
                            ("b_alpha_fwd", 4), ("b_alpha_bwd", 4)):
                sp.dma_start(h32[0][at:at + n, 0:P], io[name]).then_inc(s_rows, 16)
                at += n

            def x_block(b):
                for half in range(BLOCKS[b][1] // P // 2):
                    t0 = BLOCKS[b][0] + half * 2 * P
                    tiles = x_odd[:, 2 * half:2 * half + 2, :] if b % 2 else x_even[half][:, :, :]
                    sp.dma_start(tiles, io["x"][t0:t0 + 2 * P, :].rearrange("(s p) d -> p s d", p=P)
                                 ).then_inc(s_x[b % 2][half], 16)

            def ada_columns(n):
                sp.dma_start(wada[n % 2 if n < 4 else 0][:, :, :], io["w_ada"][n]).then_inc(s_wada[n % 2], 16)

            ada_columns(0)
            ada_columns(1)
            x_block(0)
            for n in range(2, 5):
                sp.wait_ge(s_ada, n - 1)
                ada_columns(n)
            sp.wait_ge(s_ada, 4)
            x_block(1)
            sp.wait_ge(s_ada, 5)
            ada_columns(5)
            sp.dma_start(w_raw[:, 1, :, :], io["w_in"][0]).then_inc(s_wraw[1], 16)
            sp.wait_ge(s_xt, KT)
            x_block(2)
            for n in range(2):
                sp.wait_ge(s_gr, n + 1)
                sp.dma_start(gate_dram[:, 512 * n:512 * n + 512], gate_row[:, :]).then_inc(s_grst, 16)
                sp.wait_ge(s_xt, KT * (n + 2))
                x_block(n + 3)
            sp.wait_ge(s_ssq, NT)
            sp.wait_ge(s_grst, 32)
            sp.dma_start(w_raw[:, 0, :, :], io["w_in"][1]).then_inc(s_wraw[0], 16)
            sp.wait_ge(s_xt, KT * NB)
            sp.wait_ge(s_hhi, KT * NB)
            sp.wait_ge(s_hlo, low_parts(KT * NB)[0])
            sp.wait_ge(s_hld, low_parts(KT * NB)[1])
            sp.wait_ge(s_xt, KT * NB)
            sp.wait_ge(s_hhi, KT * NB)
            sp.wait_ge(s_hlo, low_parts(KT * NB)[0])
            sp.wait_ge(s_hld, low_parts(KT * NB)[1])
            sp.wait_ge(s_wal0, 1)
            for copy in range(3):
                p = 2 * RANK * copy
                sp.dma_start(walp_raw[p:p + RANK, 0:4, :], io["w_alpha_fwd"]).then_inc(s_wal, 16)
                sp.dma_start(walp_raw[p + RANK:p + 2 * RANK, 4:8, :], io["w_alpha_bwd"]).then_inc(s_wal, 16)

            def load_after(slot, n):
                sp.wait_ge(s_wlo, n + 1)
                sp.dma_start(w_raw[:, slot, :, :], io["w_in"][bass.ds(n + 2, 1)].rearrange("o p k c -> p (o k) c")
                             ).then_inc(s_wraw[slot], 16)

            load_after(1, 0)
            for sec in range(2):
                with sp.Fori(0, 2) as i:
                    for u in range(2):
                        head = 2 * i + u
                        unit = 4 * sec + head
                        load_after(u, unit + 1)
                        for b, (t0, n) in enumerate(BLOCKS):
                            sp.wait_ge(s_ev, A_QK + NB * unit + b + 1)
                            sp.dma_start(q_dram[bass.ds(unit, 1), :, t0:t0 + n].rearrange("o p n -> p (o n)"),
                                         stage_b(b)).then_inc(s_st[b], 16)
                            sp.wait_ge(s_dec, 2 * (NB * unit + b) + 2)
                            sp.dma_start(e_dram[bass.ds(head, 1), :, :, sec, t0:t0 + n].rearrange("o p s n -> p (o s) n"),
                                         decs[:, :, 0:n]).then_inc(s_est, 16)
            with sp.Fori(0, HEADS) as head:
                for u in range(2):
                    load_after(u, 9 + 2 * head + u)
                for g in range(NT // 3):
                    sp.wait_ge(s_ev, A_V + NT * head + 3 * g + 3)
                    sp.dma_start(v_dram[bass.ds(head, 1), :, 3 * g:3 * g + 3, :].rearrange("o p t c -> p (o t) c"),
                                 stage_v(g % 3)).then_inc(s_vst[g % 3], 16)
            sp.wait_ge(s_est, 16 * 8 * NB)
            for b in range(NB):
                sp.wait_ge(s_st[b], 16 * 8)
            R_STORE = {4: 0, 6: 1, 10: 2, 12: 3, 15: 4, 17: 5}
            R_LOAD = {0: 0, 1: 1, 5: 2, 7: 3, 11: 4, 13: 5}
            for dst, _, m0, pairs in SECTIONS:
                def rotate(i, at):
                    unit = m0 // 4 + i
                    sign = int(m0 >= 16)
                    if at in R_STORE:
                        x = R_STORE[at]
                        sp.wait_ge(s_rprod, 6 * unit + x + 1)
                        sp.dma_start(qk_dec[bass.ds(unit, 1), :, :, x * RB:(x + 1) * RB].rearrange("o p d n -> p (o d) n"),
                                     dec_in[:, x % 2, :, :]).then_inc(s_rst[x % 2], 16)
                    if at in R_LOAD:
                        x = R_LOAD[at]
                        slot, got, tok = x % 2, s_rld[x % 2], slice(x * RB, (x + 1) * RB)
                        src = q_dram[bass.ds(unit, 1), :, tok].rearrange("o p n -> p (o n)")
                        sp.wait_ge(s_rst[slot], 16 * (3 * unit + x // 2))
                        for h in range(2):
                            sp.dma_start(x_rot[64 * h:64 * h + 64, slot, 1, :], src[64 * (1 - h):64 * (1 - h) + 64, :]
                                         ).then_inc(got, 16)
                        sp.dma_start(x_rot[:, slot, 0, :], src).then_inc(got, 16)
                        sp.dma_start(dec_in[:, slot, :, :], e_dram[bass.ds(unit - 4 * sign, 1), :, sign, :, tok]
                                     .rearrange("o p d n -> p (o d) n")).then_inc(got, 16)
                        sp.dma_start(rope[:, slot, :, :], io["rope"][:, :, tok]).then_inc(got, 16)

                def store_four(i, final):
                    for u in range(4):
                        m = m0 + 4 * i + u
                        if not final or u < 2:
                            load_after(u % 2, 17 + m)
                        for b, (t0, n) in enumerate(BLOCKS):
                            sp.wait_ge(s_ev, A_GA + NB * m + b + 1)
                            sp.dma_start(dst[bass.ds(4 * i + u, 1), :, t0:t0 + n].rearrange("o p n -> p (o n)"),
                                         stage_b(b)).then_inc(s_st[b], 16)
                            rotate(i, NB * u + b)

                final = dst is mg_dram
                with sp.Fori(0, pairs // 2 - final) as i:
                    store_four(i, False)
                if final:
                    store_four(pairs // 2 - 1, True)
                    for n in range(2):
                        sp.wait_ge(s_rst[n], 16 * 24)
                    sp.dma_start(kk[0][:, 1, :], qk_dec[4, :, 1]).then_inc(s_kl[0], 16)
            for b in range(NB):
                sp.wait_ge(s_st[b], 16 * 40)
            sp.wait_ge(s_mm, A_END)
            for g in range(3):
                sp.wait_ge(s_vst[g], 16 * 2 * HEADS)

            def load_head(head):
                n = head % 2
                if head:
                    sp.dma_start(kk[n][:, 1, :], qk_dec[4 + head, :, 1]).then_inc(s_kl[n], 16)
                for a, z in (((12, 16), (0, 12), (16, NT)) if n == 0 else ((0, NT),)):
                    sp.dma_start(v_ld[n][:, a:z, :], v_dram[head, :, a:z]).then_inc(s_v12 if a == 12 else s_vl[n], 16)
                    if head == 0 and a == 12:
                        for d, name in enumerate(("state_fwd", "state_bwd")):
                            sp.dma_start(s0[:, d, :, :], io[name].rearrange("h p c -> p h c")).then_inc(s_s0, 16)
                        sp.wait_ge(s_v12, 16)
                        sp.wait_ge(s_s0, 32)
                sp.dma_start(kk[n][:, 0, :], qk_dec[4 + head, :, 0]).then_inc(s_ql[n], 16)
                sp.dma_start(qd[n][:, :, :], qk_dec[head]).then_inc(s_ql[n], 16)
                sp.dma_start(ga_ld[n][:, :, :], ga_dram[2 * head:2 * head + 2].rearrange("e p n -> p e n")).then_inc(s_gl[n], 16)

            load_head(0)
            for head in range(HEADS):
                if head == HEADS - 1:
                    sp.wait_ge(s_gt, NT * head)
                    for g in range(GROUPS):
                        sp.dma_start(uf[:, g, :], u_dram[g]).then_inc(s_u, 16)
                    sp.dma_start(w4[:, :, :], io["w_four"]).then_inc(s_ctab, 16)
                    sp.dma_start(dft[:, :, :, :], io["dft"]).then_inc(s_ftab, 16)
                    sp.wait_ge(s_facn, 2)
                    sp.dma_start(chan[:, :, :], io["chan"]).then_inc(s_ctab, 16)
                if head + 1 < HEADS:
                    if head:
                        sp.wait_ge(s_gt, NT * head)
                    load_head(head + 1)
                for b, (t0, n) in enumerate(BLOCKS):
                    sp.wait_ge(s_gt, NT * head + (t0 + n) // P)
                    sp.dma_start(og_dram[2 * head:2 * head + 2, :, t0:t0 + n].rearrange("e p n -> p e n"),
                                 og[:, b % 2, :, 0:n]).then_inc(s_ogst[b % 2], 16)
                sp.wait_ge(s_pu, NTERM * head + NTERM)
                sp.dma_start(io["new_fwd"][head], fin[:, head % 2, 0, :]).then_inc(s_fst, 16)
                sp.dma_start(io["new_bwd"][head], fin[:, head % 2, 1, :]).then_inc(s_fst, 16)
            sp.wait_ge(s_ogst[0], 16 * 3 * HEADS)
            sp.wait_ge(s_ogst[1], 16 * 2 * HEADS)
            sp.wait_ge(s_fst, 16 * 2 * HEADS)
            sp.dma_start(dft_c[:, :, :, :], io["dft_c"]).then_inc(s_ftab, 16)
            sp.wait_ge(s_zm, NT)
            for g in range(GROUPS):
                sp.dma_start(uf[:, g, :], gb_dram[g]).then_inc(s_gb, 16)

            def load_og(b, half):
                k = slice(4 * half, 4 * half + 4)
                t0 = b * MB if isinstance(b, int) else bass.ds(b * MB, MB)
                src = og_dram[k, :, b * MB:b * MB + MB] if isinstance(b, int) else og_dram[k, :, t0]
                sp.dma_start(og_ld[:, k, :], src.rearrange("k p n -> p k n")).then_inc(s_og[half], 16)

            def load_mg(b, j):
                rows = mg_dram[:, :, :].rearrange("(a j) p n -> j p a n", a=2)[j]
                src = rows[:, :, b * MB:b * MB + MB] if isinstance(b, int) else rows[:, :, bass.ds(b * MB, MB)]
                sp.dma_start(mg_ld[:, j % 4, :, :], src).then_inc(s_mg[j % 4], 16)

            sp.wait_ge(s_l4, 3)
            sp.wait_ge(s_p4, 1)
            sp.wait_ge(s_cx, 1)
            for m in range(KA // 2):
                if m >= 3:
                    done = [k for k in range(2 * m - 4)]
                    sp.wait_ge(s_pwl, sum(k not in LOW_POOL for k in done))
                    sp.wait_ge(s_pwp, sum(k in LOW_POOL for k in done))
                w, k = (io["w_proj_a"], 2 * m) if 2 * m < KT else (io["w_proj_b"], 2 * m - KT)
                sp.dma_start(pw_raw[:, 2 * m % 6:2 * m % 6 + 2, :], w[k:k + 2].rearrange("k p c -> p k c")
                             ).then_inc(s_pwr[m % 3], 16)
                if m == 2:
                    for half in range(2):
                        load_og(0, half)
            sp.wait_ge(s_f, N1)
            for j in range(4):
                load_mg(0, j)

            def merged_block(b, final):
                if not final:
                    for half in range(2):
                        sp.wait_ge(s_il, 3 * b + half + 1)
                        load_og(b + 1, half)
                else:
                    sp.wait_ge(s_il, 3 * NM)
                    for j in range(4):
                        sp.wait_ge(s_mest[j], 16 * 2 * (NM - 1))
                    sp.dma_start(me_ld[:, :, :], me_dram[:, :, 0:MB].rearrange("k p n -> p k n")).then_inc(s_mel, 16)
                    for m in range(KT // 2):
                        sp.dma_start(ow_raw[:, 2 * m:2 * m + 2, :], io["w_out"][2 * m:2 * m + 2].rearrange("k p c -> p k c")
                                     ).then_inc(s_owr[m], 16)
                for j in range(8):
                    sp.wait_ge(s_me, 8 * b + j + 1)
                    sp.dma_start(me_dram[j, :, bass.ds(b * MB, MB)] if not final else me_dram[j, :, b * MB:b * MB + MB],
                                 me_st[:, j % 4, :]).then_inc(s_mest[j % 4], 16)
                    if j < 4:
                        load_mg(b, j + 4)
                    elif not final:
                        load_mg(b + 1, j - 4)

            with sp.Fori(0, NM // 2) as i:
                for u in range(2):
                    merged_block(2 * i + u, False)
            merged_block(NM - 1, True)

            def load_me(b):
                sp.dma_start(me_ld[:, :, :], (me_dram[:, :, 0:MB] if isinstance(b, int) else me_dram[:, :, bass.ds(b * MB, MB)]
                                              ).rearrange("k p n -> p k n")).then_inc(s_mel, 16)

            sp.wait_ge(s_y, 8 * NM)
            sp.dma_start(fng[:, :], io["final_norm_g"].to_broadcast([P, D])).then_inc(s_row3, 16)
            sp.dma_start(gate_b[:, :], io["b_gate"].to_broadcast([P, D])).then_inc(s_row3, 16)
            for r in range(2):
                sp.dma_start(res_gate[:, r, :], gate_dram[r:r + 1].to_broadcast([P, D])).then_inc(s_row3, 16)
            for j in range(4):
                sp.wait_ge(s_mest[j], 16 * 2 * NM)
            for u in range(2):
                sp.dma_start(x_in[:, u, :], io["x"][u * P:u * P + P, :]).then_inc(s_xin[u], 16)

            def out_block(b, final):
                if not final:
                    sp.wait_ge(s_ml, b + 1)
                    load_me(b + 1)
                for u in range(2):
                    if not final:
                        sp.wait_ge(s_add, 2 * b + u + 1)
                        sp.dma_start(x_in[:, u, :], io["x"][bass.ds((2 * b + u + 2) * P, P), :]).then_inc(s_xin[u], 16)
                for u in range(2):
                    sp.wait_ge(s_yn, 2 * b + u + 1)
                    y = io["y"][bass.ds((2 * b + u) * P, P), :] if not final else io["y"][(2 * b + u) * P:(2 * b + u + 1) * P, :]
                    sp.dma_start(y, yt[:, u, :]).then_inc(s_yst[u], 16)

            with sp.Fori(0, NM // 2) as i:
                for u in range(2):
                    out_block(2 * i + u, False)
            out_block(NM - 1, True)
            for u in range(2):
                sp.wait_ge(s_yst[u], 16 * NM)

        @block.gpsimd
        def _(pool):
            for b, (t0, n) in enumerate(BLOCKS):
                for k in range(KT):
                    if k in LOW_DVE:
                        continue
                    e = KT * b + k
                    pool.wait_ge(s_hhi, e + 1)
                    pool.tensor_tensor(h_lo[:, k, t0:t0 + n], h32[e % 2][:, 0:n],
                                       h_hi[:, k, t0:t0 + n].bitcast(F32), ALU.subtract).then_inc(s_hlo, 1)
            with pool.Fori(0, 8) as pair:
                for x in range(6):
                    slot, step = x % 2, 6 * pair + x
                    a, b = x_rot[:, slot, 0, :], x_rot[:, slot, 1, :]
                    pool.wait_ge(s_rld[slot], 16 * 5 * (3 * pair + x // 2 + 1))
                    pool.tensor_tensor(a, a, rope[:, slot, 0, :], ALU.mult)
                    pool.tensor_tensor(b, b, rope[:, slot, 1, :], ALU.mult).then_inc(s_rm, 1)
                    pool.wait_ge(s_rm, step + 1)
                    pool.tensor_tensor(a, a, b, ALU.add).then_inc(s_rotd, 1)
                    pool.wait_ge(s_rotd, step + 1)
                    d = dec_in[:, slot, :, :]
                    pool.tensor_tensor(d, d, a.unsqueeze(1).to_broadcast([P, 2, RB]), ALU.mult).then_inc(s_rprod, 1)
            pool.wait_ge(s_u, 16 * GROUPS)
            pool.wait_ge(s_gt, NT * (HEADS - 1))
            ut = uf[:, :, 0:LAT].rearrange("p g (a n) -> p a g n", a=4)
            for m in range(2):
                pool.tensor_tensor(u_sum[:, m, :, :], ut[:, m], ut[:, m + 2], ALU.add).then_inc(s_ub, 1)
            for m in range(2):
                pool.tensor_tensor(ut[:, m + 2], ut[:, m], ut[:, m + 2], ALU.subtract).then_inc(s_ub, 1)
            pool.wait_ge(s_ub, 4)
            for m, op in enumerate((ALU.add, ALU.subtract)):
                pool.tensor_tensor(ut[:, m], u_sum[:, 0, :, :], u_sum[:, 1, :, :], op).then_inc(s_ub, 1)
            pool.wait_ge(s_z, 6)
            combine(pool, 0).then_inc(s_p2, 1)
            pool.wait_ge(s_p2, 1)
            pool.wait_ge(s_twd, 3)
            sums(pool, [sb[:, 12 + n, :, :] for n in range(4)], [zb[:, 12 + n, :, :] for n in range(4)]).then_inc(s_p3, 1)
            pool.wait_ge(s_p3, 1)
            turns(pool, [zb[:, 12 + n, :, :] for n in range(4)], [sb[:, 12 + n, :, :] for n in range(4)]).then_inc(s_p4, 1)

            for k in LOW_POOL:
                pool.wait_ge(s_f, 4 * (k // 4 + 1))
                pool.wait_ge(s_pwh, k + 1)
                pool.tensor_tensor(pw_lo[:, k, :], pw_raw[:, k % 6, :], pw_hi[:, k, :].bitcast(F32), ALU.subtract
                                   ).then_inc(s_pwp, 1)

            def merge_block(b):
                for j in range(8):
                    pool.wait_ge(s_mest[j % 4], 16 * (2 * b + j // 4))
                    pool.wait_ge(s_yg, 8 + 8 * b + j + 1)
                    pool.tensor_tensor(me_st[:, j % 4, :], mg_ld[:, j % 4, 0, :], mg_ld[:, j % 4, 1, :], ALU.add
                                       ).then_inc(s_me, 1)

            with pool.Fori(0, NM // 2) as i:
                for u in range(2):
                    merge_block(2 * i + u)
            merge_block(NM - 1)

            def add_block(b):
                for u in range(2):
                    pool.wait_ge(s_xin[u], 16 * (b + 1))
                    pool.wait_ge(s_og3, 4 + 2 * b + u + 1)
                    pool.tensor_tensor(yt[:, u, :], yt[:, u, :], x_in[:, u, :], ALU.add).then_inc(s_add, 1)

            with pool.Fori(0, NM // 2) as i:
                for u in range(2):
                    add_block(2 * i + u)
            add_block(NM - 1)

        @block.scalar
        def _(act):
            act.wait_ge(s_cols, 1)
            act.activation(silc[:, :, :], cols[:, C_COND:C_COND + 2 * KT].rearrange("p (s k) -> p s k", s=2),
                           ACT.Silu).then_inc(s_silc, 1)

            def squares(b):
                for s in range(BLOCKS[b][1] // P):
                    act.wait_ge(s_x[b % 2][s // 2], 16 * (b // 2 + 1))
                    if b:
                        act.wait_ge(s_rs, b)
                    act.wait_ge(s_ssq, BLOCKS[b][0] // P + s)
                    act.activation(junk[:, :], x_tile(b, s), ACT.Square, accum_out=sq0[:, s:s + 1]).then_inc(s_ssq, 1)
                tiles = BLOCKS[b][1] // P
                act.wait_ge(s_ssq, BLOCKS[b][0] // P + tiles)
                act.activation(sq0[:, 0:tiles], sq0[:, 0:tiles], ACT.Sqrt, scale=1.0 / D, bias=EPS).then_inc(s_root, 1)

            squares(0)
            for b, (t0, n) in enumerate(BLOCKS):
                for k in range(KT):
                    e = KT * b + k
                    act.wait_ge(s_h32, e + 1)
                    act.activation(h_hi[:, k, t0:t0 + n], h32[e % 2][:, 0:n], ACT.Copy).then_inc(s_hhi, 1)
                if b == 0:
                    squares(1)
                if b + 2 < NB:
                    squares(b + 2)

            for b, (t0, n) in enumerate(BLOCKS):
                act.wait_ge(s_mm, b + 1)
                if b == 0:
                    act.wait_ge(s_xt, KT * NB)
                    act.wait_ge(s_hlo, low_parts(KT * NB)[0])
                    act.wait_ge(s_hld, low_parts(KT * NB)[1])
                act.activation(r_t[:, t0:t0 + n], bank[R_BANK[b]][0:96, 0:n], ACT.Copy).then_inc(s_ev, 1)
            act.preload_act_table_set("natural_log_exp_and_others")
            act.wait_ge(s_wsp, 2)

            def decays(e, n):
                act.wait_ge(s_est, 16 * e)
                act.wait_ge(s_bc, e + 1)
                for sign in range(2):
                    act.activation(decs[:, sign, 0:n], bcs[:, 0:n], ACT.Exp, scale=(1.0, -1.0)[sign] / GATE_NORM
                                   ).then_inc(s_dec, 1)

            for sec in range(2):
                with act.Fori(0, 2) as i:
                    for u in range(2):
                        unit = 4 * sec + 2 * i + u
                        for b, (t0, n) in enumerate(BLOCKS):
                            e = NB * unit + b
                            act.wait_ge(s_now, 2 * sec + i + 1)
                            act.wait_ge(s_glog, e)
                            act.wait_ge(s_g, e + 1)
                            act.activation(soft[:, 0:n], bank[5 + (NB * u + b) % 2][:, 0:n], ACT.Abs,
                                           bias=balp_now[:, u:u + 1]).then_inc(s_gabs, 1)
                            act.wait_ge(s_gabs, e + 1)
                            act.activation(soft[:, 0:n], soft[:, 0:n], ACT.Exp, scale=-1.0).then_inc(s_gexp, 1)
                            act.wait_ge(s_gexp, e + 1)
                            act.activation(soft[:, 0:n], soft[:, 0:n], ACT.Ln, bias=1.0).then_inc(s_gln, 1)
                            if u + b:
                                decays(e - 1, BLOCKS[b - 1][1])
                            act.wait_ge(s_st[b], 16 * unit)
                            act.wait_ge(s_mm, A_QK + e + 1)
                            act.activation(stage_b(b), bank[b][:, 0:n], ACT.Copy,
                                           scale=DK ** -0.5 if sec == 0 else 1.0).then_inc(s_ev, 1)
                    decays(NB * (4 * sec + 2 * i + 2) - 1, BLOCKS[-1][1])
            for b in range(NB):
                act.wait_ge(s_st[b], 16 * 8)
            with act.Fori(0, HEADS) as head:
                for t in range(NT):
                    if t % 3 == 0:
                        act.wait_ge(s_vst[t // 3 % 3], 16 * (2 * head + t // 9))
                    act.wait_ge(s_mm, A_V + NT * head + t + 1)
                    act.activation(stage_v(t // 3 % 3)[:, t % 3, :], bank[5 + t % 3][:, 0:DV], ACT.Copy).then_inc(s_ev, 1)
            for g in range(3):
                act.wait_ge(s_vst[g], 16 * 2 * HEADS)
            for _, func, m0, pairs in SECTIONS:
                with act.Fori(0, pairs) as i:
                    for u in range(2):
                        m = m0 + 2 * i + u
                        for b, (t0, n) in enumerate(BLOCKS):
                            act.wait_ge(s_st[b], 16 * (8 + m))
                            act.wait_ge(s_mm, A_GA + NB * m + b + 1)
                            act.activation(stage_b(b), bank[b][:, 0:n], func).then_inc(s_ev, 1)
            act.preload_act_table_set("natural_log_exp_and_others")
            act.wait_ge(s_tf, 3)
            act.activation(fac[:, :, :, :], tf[:, :, :, :], ACT.Exp, scale=1.0 / GATE_NORM).then_inc(s_fac, 1)
            act.activation(mid_e[:, :, :, :].rearrange("p d h c -> p (d h) c"), mid[:, :, :], ACT.Exp, scale=1.0 / GATE_NORM).then_inc(s_fac, 1)

            def act_head(head, n, i):
                def k_out(j):
                    act.wait_ge(s_ds, NTERM * head + max(j - 1, 0))
                    act.wait_ge(s_tr, NTERM * head + j + 1)
                    act.activation(kin[:, j % 2, :], bank[turn_bank(j)][:, 0:P], ACT.Copy).then_inc(s_kin, 1)

                def term_out(j):
                    way, c = TERMS[j]
                    act.wait_ge(s_pu, NTERM * head + max(j - 1, 0))
                    act.wait_ge(s_ds, NTERM * head + j + 1)
                    act.activation(ds_t[:, j % 2, :], bank[4 + j % 2][:, 0:DV], ACT.Copy,
                                   scale=fac_now[:, 0 if way == "f" else 1, n, c:c + 1]).then_inc(s_dt, 1)

                act.wait_ge(s_facn, i + 1)
                k_out(0)
                for j in range(B_TERMS):
                    if j + 1 < B_TERMS:
                        k_out(j + 1)
                    term_out(j)
                k_out(term["f", 0])
                for c in range(NT):
                    if ("f", c + 1) in term:
                        k_out(term["f", c + 1])
                    if ("f", c) in term:
                        term_out(term["f", c])
                    e, o = NT * head + c, bank[2 + c % 2][:, 0:DV]
                    act.wait_ge(s_on, e)
                    act.wait_ge(s_o, e + 1)
                    act.activation(junk2[:, :], o, ACT.Square, accum_out=rms[:, 0:1]).then_inc(s_sq2, 1)
                    act.wait_ge(s_sq2, e + 1)
                    act.activation(rms[:, 1:2], rms[:, 0:1], ACT.Ln, scale=1.0 / DV, bias=EPS).then_inc(s_ln2, 1)
                    act.wait_ge(s_ln2, e + 1)
                    act.activation(rms[:, 1:2], rms[:, 1:2], ACT.Exp, scale=-0.5).then_inc(s_rs2, 1)
                    act.wait_ge(s_ot, NT * head + max(c - 1, 0))
                    act.wait_ge(s_rs2, e + 1)
                    act.activation(on[:, c % 2, :], o, ACT.Copy, scale=rms[:, 1:2]).then_inc(s_on, 1)

            with act.Fori(0, HEADS // 2) as i:
                for n in range(2):
                    act_head(2 * i + n, n, i)
            for n in range(2):
                act.wait_ge(s_cwm, n + 1)
                act.activation(cw[:, 2 * n:2 * n + 2, :, :], bank[n][:, :].rearrange("p (g r c) -> p g r c", g=2, r=2),
                               ACT.Copy).then_inc(s_cw, 1)
            act.wait_ge(s_gt, NT * HEADS)
            act.wait_ge(s_fst, 32 * HEADS)
            for m, t in enumerate(Z_ORDER):
                act.wait_ge(s_zm, m + 1)
                for h in range(2):
                    ins = act.activation(z_home(t)[:, :, 256 * h:256 * h + 256].rearrange("p r (g c) -> p g r c", g=2),
                                         bank[2 * (m % 3) + h][:, :].rearrange("p (g r c) -> p g r c", g=2, r=2), ACT.Copy)
                ins.then_inc(s_z, 1)
                n = {9: 1, 12: 2, 15: 3}.get(m)
                if n:
                    act.wait_ge(s_l2, n)
                    act.wait_ge(s_z, m + 1)
                    for c in range(1, 4):
                        ins = act.activation(sb[:, 4 * c + n, :, :], zb[:, 4 * c + n, :, :], ACT.Copy,
                                             scale=float(np.cos(2 * np.pi * n * c / N1)))
                    ins.then_inc(s_tw, 1)

            def high(slot, out, src, value, done):
                act.wait_ge(slot, value)
                act.activation(out, src, ACT.Copy).then_inc(done, 1)

            for k in range(KA):
                high(s_pwr[k // 2 % 3], pw_hi[:, k, :], pw_raw[:, k % 6, :], 16 * (k // 6 + 1), s_pwh)

            def high_block(b, slot):
                if not isinstance(b, int):
                    act.wait_ge(s_y, 8 * (b - 1))
                for half in range(2):
                    k = slice(4 * half, 4 * half + 4)
                    high(s_og[half], in_hi[slot][:, k, :], og_ld[:, k, :], 16 * (b + 1), s_ih)
                act.activation(in_hi[slot][:, KT:KA, :], uf[:, :, bass.ds(b * MB, MB)], ACT.Copy).then_inc(s_ih, 1)

            act.wait_ge(s_fo, 17)
            high_block(0, 0)
            act.wait_ge(s_pwl, KA - len(LOW_POOL))
            act.wait_ge(s_pwp, len(LOW_POOL))
            with act.Fori(0, NM // 2) as i:
                for u in range(2):
                    high_block(2 * i + u + 1, 1 - u)

            act.wait_ge(s_y, 8 * NM)
            for k in range(KT):
                high(s_owr[k // 2], ow_hi[:, k, :], ow_raw[:, k, :], 16, s_owh)
                if k == 1:
                    act.wait_ge(s_me, 8 * NM)
                    high(s_mel, me_hi[0][:, :, :], me_ld[:, :, :], 16, s_mh)

            def root_block(b, slot, final):
                if not final:
                    act.wait_ge(s_out, 2 * b)
                    high(s_mel, me_hi[1 - slot][:, :, :], me_ld[:, :, :], 16 * (b + 2), s_mh)
                for u in range(2):
                    e = 2 * b + u
                    act.wait_ge(s_add, e + 1)
                    act.wait_ge(s_rt3, 3 * e)
                    act.wait_ge(s_yn, 2 * b)
                    act.activation(junk3[:, :], yt[:, u, :], ACT.Square, accum_out=rms3[:, u, 0:1]).then_inc(s_rt3, 1)
                    act.wait_ge(s_rt3, 3 * e + 1)
                    act.activation(rms3[:, u, 1:2], rms3[:, u, 0:1], ACT.Ln, scale=1.0 / D, bias=EPS).then_inc(s_rt3, 1)
                    act.wait_ge(s_rt3, 3 * e + 2)
                    act.activation(rms3[:, u, 1:2], rms3[:, u, 1:2], ACT.Exp, scale=-0.5).then_inc(s_rt3, 1)

            with act.Fori(0, NM // 2) as i:
                for u in range(2):
                    root_block(2 * i + u, u, False)
            root_block(NM - 1, 0, True)

        @block.vector
        def _(dve):
            dve.wait_ge(s_rowt, 1)
            dve.tensor_copy(cols[:, 0:C_ALL], bank[7][:, 0:C_ALL]).then_inc(s_cols, 1)

            def roots(b):
                tiles = BLOCKS[b][1] // P
                dve.wait_ge(s_root, b + 1)
                dve.wait_ge(s_xn, BLOCKS[b][0] // P)
                dve.reciprocal(rs0[:, 0:tiles], sq0[:, 0:tiles]).then_inc(s_rs, 1)
                dve.wait_ge(s_rs, b + 1)

            def normalise(b, s):
                x = x_tile(b, s)
                dve.tensor_scalar(x, x, rs0[:, s:s + 1], None, ALU.mult).then_inc(s_xn, 1)

            roots(0)
            for t in range(4):
                normalise(0, t)
            for n in range(4):
                dve.wait_ge(s_ada, n + 1)
                dve.tensor_copy(adarow[:, n * 512:(n + 1) * 512], bank[6 + n % 2][0:2, :]).then_inc(s_adar, 1)
            dve.wait_ge(s_adat, 1)
            dve.wait_ge(s_cols, 1)
            ada = bank[6][:, 0:32].rearrange("p (j k s) -> p j s k", j=2, s=2)
            bada = cols[:, C_BADA:C_BADA + 16].rearrange("p (j k) -> p j k", j=2)
            for s in range(2):
                dve.tensor_tensor(modu[:, 1, s, :], ada[:, 0, s, :], bada[:, 0, :], ALU.add)
                ins = dve.scalar_tensor_tensor(modu[:, 0, s, :], ada[:, 1, s, :], 1.0, bada[:, 1, :], ALU.add, ALU.add)
            ins.then_inc(s_mod, 1)
            dve.wait_ge(s_mod, 1)
            dve.tensor_tensor(modu[:, 0, :, :], modu[:, 0, :, :],
                              cols[:, C_NG:C_NG + KT].unsqueeze(1).to_broadcast([P, 2, KT]), ALU.mult).then_inc(s_mod, 1)
            dve.wait_ge(s_mod, 2)
            for b, (t0, n) in enumerate(BLOCKS):
                s = 0 if t0 < LAT else 1
                for k in range(KT):
                    e = KT * b + k
                    if e >= 2:
                        dve.wait_ge(s_hhi, e - 1)
                        if (e - 2) % KT in LOW_DVE:
                            dve.wait_ge(s_hld, low_parts(e - 1)[1])
                        else:
                            dve.wait_ge(s_hlo, low_parts(e - 1)[0])
                    dve.wait_ge(s_xt, e + 1)
                    dve.tensor_scalar(h32[e % 2][:, 0:n], bank[e % 6][:, 0:n], modu[:, 0, s, k:k + 1],
                                      modu[:, 1, s, k:k + 1], ALU.mult, ALU.add).then_inc(s_h32, 1)
                    if k - 1 in LOW_DVE:
                        dve.wait_ge(s_hhi, e)
                        dve.tensor_tensor(h_lo[:, k - 1, t0:t0 + n], h32[(e - 1) % 2][:, 0:n],
                                          h_hi[:, k - 1, t0:t0 + n].bitcast(F32), ALU.subtract).then_inc(s_hld, 1)
                    if b + 1 < NB and k >= 4 and b:
                        if k == 4:
                            roots(b + 1)
                        if k - 4 < BLOCKS[b + 1][1] // P:
                            normalise(b + 1, k - 4)
                if b < 2:
                    dve.wait_ge(s_ada, 5 + b)
                    if b:
                        dve.wait_ge(s_grst, 16)
                    dve.tensor_copy(gate_row[:, :], bank[7][0:2, :]).then_inc(s_gr, 1)
                if b == 0:
                    roots(1)
                    for t in range(4):
                        normalise(1, t)
                if b == 1:
                    dve.wait_ge(s_wraw[1], 16)
                    dve.tensor_copy(w_hi[0][:, :, P:2 * P], w_raw[:, 1, :, :]).then_inc(s_whi, 1)
                    dve.wait_ge(s_whi, 1)
                    dve.tensor_tensor(w_lo[0][:, :, P:2 * P], w_raw[:, 1, :, :], w_hi[0][:, :, P:2 * P].bitcast(F32),
                                      ALU.subtract).then_inc(s_wlo, 1)

            def split(slot, n, landed, pair=0):
                sl = slice(P * slot, P * slot + P)
                dve.wait_ge(s_wraw[slot], 16 * landed)
                dve.tensor_copy(w_hi[pair][:, :, sl], w_raw[:, slot, :, :]).then_inc(s_whi, 1)
                dve.wait_ge(s_whi, n + 1)
                dve.tensor_tensor(w_lo[pair][:, :, sl], w_raw[:, slot, :, :], w_hi[pair][:, :, sl].bitcast(F32),
                                  ALU.subtract).then_inc(s_wlo, 1)

            dve.wait_ge(s_hhi, KT * NB)
            dve.wait_ge(s_hlo, low_parts(KT * NB)[0])
            dve.memset(walp_raw[:, :, :], 0.0).then_inc(s_wal0, 1)
            split(0, 1, 1)
            for b, (t0, n) in enumerate(BLOCKS):
                dve.wait_ge(s_ev, b + 1)
                lo = r_t[32:64, t0:t0 + n]
                dve.tensor_tensor(lo, bank[R_BANK[b]][32:64, 0:n], lo.bitcast(F32), ALU.subtract).then_inc(s_rlo, 1)
            dve.wait_ge(s_wal, 96)
            dve.tensor_copy(walp[:, :, :], walp_raw[:, :, :]).then_inc(s_wsp, 1)
            dve.wait_ge(s_wsp, 1)
            dve.tensor_tensor(walp[64:96, :, :], walp_raw[64:96, :, :], walp[64:96, :, :].bitcast(F32),
                              ALU.subtract).then_inc(s_wsp, 1)
            dve.wait_ge(s_wsp, 2)
            for sec in range(2):
                with dve.Fori(0, 2) as i:
                    for u in range(2):
                        unit = 4 * sec + 2 * i + u
                        if u == 0:
                            dve.wait_ge(s_g, NB * unit)
                            dve.wait_ge(s_gabs, NB * unit)
                            dve.tensor_copy(walp_now[:, :, :], walp[:, bass.ds(unit, 2), :])
                            dve.tensor_copy(balp_now[:, :], cols[:, bass.ds(C_BAF + unit, 2)]).then_inc(s_now, 1)
                            dve.wait_ge(s_now, 2 * sec + i + 1)
                        dve.wait_ge(s_mm, A_QK + NB * unit)
                        split(1 - u, unit + 2, 2 * sec + i + 2)
                        for b, (t0, n) in enumerate(BLOCKS):
                            e = NB * unit + b
                            par, chunks, t = NB * u + b, n // P, t0 // P
                            dve.wait_ge(s_gabs, e + 1)
                            dve.tensor_scalar(logit[:, 0:n], bank[5 + par % 2][:, 0:n], balp_now[:, u:u + 1], 0.0,
                                              ALU.add, ALU.min).then_inc(s_gmin, 1)
                            dve.wait_ge(s_gmin, e + 1)
                            dve.wait_ge(s_gln, e + 1)
                            dve.tensor_tensor(logit[:, 0:n], logit[:, 0:n], soft[:, 0:n], ALU.subtract).then_inc(s_glog, 1)
                            dve.wait_ge(s_glog, e + 1)
                            for c in range(chunks):
                                x, y = logit[:, c * P:c * P + P], cum[:, c * P:c * P + P]
                                if sec:
                                    x, y = x[:, ::-1], y[:, ::-1]
                                ins = dve.tensor_tensor_scan(y, ones, x, 0.0, ALU.mult, ALU.add)
                            ins.then_inc(s_gcum, 1)
                            dve.wait_ge(s_gcum, e + 1)
                            cc = cum[:, 0:n].rearrange("p (c t) -> p c t", t=P)
                            mt, lt = (64, 0) if sec else (63, 127)
                            dve.tensor_copy(mid[:, bass.ds(unit, 1), t:t + chunks].rearrange("p o c -> p (o c)"), cc[:, :, mt])
                            dve.tensor_copy(last[:, bass.ds(unit, 1), t:t + chunks].rearrange("p o c -> p (o c)"), cc[:, :, lt])
                            dve.wait_ge(s_dec, 2 * e)
                            dve.tensor_tensor(bcs[:, 0:n].rearrange("p (c t) -> p c t", t=P), cc,
                                              cc[:, :, mt:mt + 1].to_broadcast([P, chunks, P]),
                                              ALU.subtract).then_inc(s_bc, 1)
            dve.wait_ge(s_mm, A_V)
            split(1, 10, 6)
            dve.wait_ge(s_est, 16 * 8 * NB)
            for h in range(1, HEADS):
                if h > 1:
                    dve.wait_ge(s_mm, A_V + NT * (h - 1))
                for u in range(2):
                    split(u, 9 + 2 * h + u, 5 + h + u, pair=h % 2)
            dve.wait_ge(s_mm, A_GA - NB)
            split(0, 17, 9)
            for _, _, m0, pairs in SECTIONS:
                def split_pair(i, final):
                    for u in range(2):
                        m = m0 + 2 * i + u
                        if final and u:
                            continue
                        dve.wait_ge(s_mm, A_GA + NB * m)
                        split(1 - u, 18 + m, 10 + m0 // 2 + i)

                final = m0 == 16
                with dve.Fori(0, pairs - final) as i:
                    split_pair(i, False)
                if final:
                    split_pair(pairs - 1, True)
            dve.wait_ge(s_mm, A_END)
            dve.wait_ge(s_ev, A_END)
            md = mid[:, :, :].rearrange("p (d h) c -> p d h c", d=2)
            dve.tensor_tensor(tf[:, :, :, :].rearrange("p d h c -> p (d h) c"), last[:, :, :], mid[:, :, :],
                              ALU.subtract).then_inc(s_tf, 1)
            dve.memset(pb[:, NT - 1, :], 0.0)
            dve.wait_ge(s_tf, 1)
            for n, (d, a, z) in enumerate(((0, 0, LT - 1), (0, LT, NT - 1), (1, 1, LT), (1, LT + 1, NT))):
                step = 1 if d == 0 else -1
                ins = dve.tensor_tensor(tf[:, d, :, a:z], tf[:, d, :, a:z], md[:, d, :, a + step:z + step], ALU.add)
            ins.then_inc(s_tf, 2)
            dve.wait_ge(s_fac, 2)
            dve.wait_ge(s_s0, 32)

            def dve_head(head, n):
                def update(j):
                    way, c = TERMS[j]
                    if way == "b":
                        old, d = state_b(n, c), 1
                        new = fin[:, n, 1, :] if c == LT else pb[:, c - 1, :]
                        if 0 < c < LT:
                            dve.wait_ge(s_o, NT * head)
                    else:
                        old, d = state_f(n, c), 0
                        new = fin[:, n, 0, :] if c == NT - 1 else pf[:, (c + 1) % 2, :]
                        dve.wait_ge(s_o, NT * head + c)
                    dve.wait_ge(s_pu, NTERM * head + j)
                    dve.wait_ge(s_dt, NTERM * head + j + 1)
                    dve.scalar_tensor_tensor(new, old, fac_now[:, d, n, c:c + 1], ds_t[:, j % 2, :],
                                             ALU.mult, ALU.add).then_inc(s_pu, 1)

                def combine_backward(c):
                    dve.wait_ge(s_o, NT * head + max(c - 1, 0))
                    dve.wait_ge(s_sc, NT * head + c + 1)
                    dve.tensor_tensor(comb[:, c % 2, :], bank[c % 2][:, P:2 * P], diag2, ALU.mult).then_inc(s_cb1, 1)

                def backward_in_place(c):
                    dve.wait_ge(s_cb1, NT * head + c + 1)

                def combine_forward(c):
                    dve.copy_predicated(comb[:, c % 2, :], upper, bank[c % 2][:, 0:P]).then_inc(s_cb, 1)

                def gate(c):
                    b = min(c // 4, NB - 1)
                    at = c * P - BLOCKS[b][0]
                    if at == 0:
                        dve.wait_ge(s_ogst[b % 2], 16 * ((2 if b % 2 else 3) * head + b // 2))
                    dve.wait_ge(s_ot, NT * head + c + 1)
                    for e in range(2):
                        ins = dve.scalar_tensor_tensor(og[:, b % 2, e, at:at + P], bank[7][:, e * P:e * P + P],
                                                       cols[:, C_GG + e:C_GG + e + 1], ga_ld[n][:, e, c * P:c * P + P],
                                                       ALU.mult, ALU.mult)
                    ins.then_inc(s_gt, 1)

                for j in range(B_TERMS):
                    update(j)
                combine_backward(0)
                backward_in_place(0)
                dve.memset(pad[:, :], 0.0)
                combine_forward(0)
                for c in range(NT):
                    if c + 1 < NT:
                        combine_backward(c + 1)
                        backward_in_place(c + 1)
                    if ("f", c) in term:
                        update(term["f", c])
                    else:
                        dve.memset(pad[:, :], 0.0)
                    if c + 1 < NT:
                        combine_forward(c + 1)
                    if c == 1:
                        dve.wait_ge(s_gl[n], gate_loads)
                    if c:
                        gate(c - 1)
                gate(NT - 1)

            with dve.Fori(0, HEADS // 2) as i:
                gate_loads = 16 * (i + 1)
                dve.wait_ge(s_o, 2 * NT * i)
                dve.wait_ge(s_pu, 2 * NTERM * i)
                dve.wait_ge(s_fst, 64 * i)
                dve.tensor_copy(fac_now[:, :, :, :], fac[:, :, bass.ds(2 * i, 2), :])
                dve.tensor_copy(mid_now[:, :, :, :], mid_e[:, :, bass.ds(2 * i, 2), :])
                dve.tensor_copy(first[:, :, :, :].rearrange("p n d c -> p d n c"), s0[:, :, bass.ds(2 * i, 2), :]
                                ).then_inc(s_facn, 1)
                dve.wait_ge(s_facn, i + 1)
                for n in range(2):
                    for d, c in ((0, 0), (1, LT - 1)):
                        ins = dve.tensor_scalar(first[:, n, d, :], first[:, n, d, :], mid_now[:, d, n, c:c + 1], None, ALU.mult)
                ins.then_inc(s_p0, 1)
                dve.wait_ge(s_p0, i + 1)
                for n in range(2):
                    dve_head(2 * i + n, n)
            def twiddle(n):
                dve.wait_ge(s_tw, n)
                for c in range(1, 4):
                    sn = float(np.sin(2 * np.pi * n * c / N1))
                    z, o = zb[:, 4 * c + n, :, :], sb[:, 4 * c + n, :, :]
                    dve.scalar_tensor_tensor(o[:, 0, :], z[:, 1, :], sn, o[:, 0, :], ALU.mult, ALU.add)
                    ins = dve.scalar_tensor_tensor(o[:, 1, :], z[:, 0, :], -sn, o[:, 1, :], ALU.mult, ALU.add)
                ins.then_inc(s_twd, 1)

            def second(c):
                sums(dve, [sb[:, 4 * c + n, :, :] for n in range(4)], [zb[:, 4 * c + n, :, :] for n in range(4)]).then_inc(s_l3, 1)
                dve.wait_ge(s_l3, c + 1)
                turns(dve, [zb[:, 4 * c + n, :, :] for n in range(4)], [sb[:, 4 * c + d, :, :] for d in range(4)]).then_inc(s_l4, 1)

            def gate_latents(c):
                for d in range(4):
                    dve.wait_ge(s_f, 4 * c + d + 1)
                    y = uf[:, :, 0:LAT].rearrange("p g (k s) -> p g s k", s=N1)[:, :, c + 4 * d, :]
                    dve.tensor_tensor(y, bank[4 * (c % 2) + d][:, :].rearrange("p (g k) -> p g k", g=4), y, ALU.mult).then_inc(s_fo, 1)

            dve.wait_ge(s_z, 4)
            second(0)
            for n in range(1, 4):
                dve.wait_ge(s_z, 4 + 3 * n + 2)
                combine(dve, n).then_inc(s_l2, 1)
                if n > 1:
                    twiddle(n - 1)
            twiddle(3)
            dve.wait_ge(s_twd, 3)
            dve.wait_ge(s_p2, 1)
            second(1)
            dve.wait_ge(s_gb, 16 * GROUPS)
            dve.wait_ge(s_cx, 1)
            for h in range(2):
                y = uf[:, 2 * h:2 * h + 2, LAT:TOK]
                ins = dve.tensor_tensor(y, bank[6 + h][:, :].rearrange("p (g k) -> p g k", g=2), y, ALU.mult)
            ins.then_inc(s_fo, 1)
            second(2)
            gate_latents(0)

            def low(out, raw, hi, count, value, done):
                dve.wait_ge(count, value)
                return dve.tensor_tensor(out, raw, hi.bitcast(F32), ALU.subtract).then_inc(done, 1)

            for c in range(1, 4):
                gate_latents(c)
                for k in range(4 * c - 4, 4 * c):
                    if k not in LOW_POOL:
                        low(pw_lo[:, k, :], pw_raw[:, k % 6, :], pw_hi[:, k, :], s_pwh, k + 1, s_pwl)

            def low_block(b, slot):
                for half in range(2):
                    k = slice(4 * half, 4 * half + 4)
                    low(in_lo[slot][:, k, :], og_ld[:, k, :], in_hi[slot][:, k, :], s_ih, 3 * b + half + 1, s_il)
                low(in_lo[slot][:, KT:KA, :], uf[:, :, bass.ds(b * MB, MB)], in_hi[slot][:, KT:KA, :], s_ih, 3 * b + 3, s_il)

            def gate_block(b):
                for j in range(8):
                    dve.wait_ge(s_mg[j % 4], 16 * (2 * b + j // 4 + 1))
                    dve.wait_ge(s_y, 8 * b + j + 1)
                    m = mg_ld[:, j % 4, :, :].rearrange("p a n -> p (a n)")
                    dve.tensor_tensor(m, bank[j][:, :], m, ALU.mult).then_inc(s_yg, 1)

            dve.wait_ge(s_fo, 17)
            dve.wait_ge(s_pwl, KA - len(LOW_POOL))
            dve.memset(pad[:, :], 0.0).then_inc(s_yg, 8)
            low_block(0, 0)
            with dve.Fori(0, NM // 2) as i:
                for u in range(2):
                    low_block(2 * i + u + 1, 1 - u)
                    gate_block(2 * i + u)
            gate_block(NM - 1)

            dve.wait_ge(s_me, 8 * NM)
            dve.wait_ge(s_y, 8 * NM)
            for k in range(KT):
                low(ow_lo[:, k, :], ow_raw[:, k, :], ow_hi[:, k, :], s_owh, k + 1, s_owl)
                if k == 1:
                    dve.memset(pad[:, :], 0.0).then_inc(s_og3, 4)
                    low(me_lo[0][:, :, :], me_ld[:, :, :], me_hi[0][:, :, :], s_mh, 1, s_ml)
            dve.wait_ge(s_row3, 64)
            for r in range(2):
                ins = dve.tensor_tensor(res_gate[:, r, :], res_gate[:, r, :], gate_b[:, :], ALU.add)
            ins.then_inc(s_gate, 1)
            dve.wait_ge(s_gate, 1)

            def finish_block(b, slot, final):
                if not final:
                    low(me_lo[1 - slot][:, :, :], me_ld[:, :, :], me_hi[1 - slot][:, :, :], s_mh, b + 2, s_ml)
                for u in range(2):
                    dve.wait_ge(s_yst[u], 16 * b)
                    dve.wait_ge(s_out, 2 * b + u + 1)
                    for h in range(2):
                        sl = slice(512 * h, 512 * h + 512)
                        ins = dve.tensor_tensor(yt[:, u, sl], bank[4 * slot + 2 * u + h][:, :], res_gate[:, int(final), sl], ALU.mult)
                    ins.then_inc(s_og3, 1)
                for u in range(2):
                    dve.wait_ge(s_rt3, 3 * (2 * b + u + 1))
                    dve.scalar_tensor_tensor(yt[:, u, :], yt[:, u, :], rms3[:, u, 1:2], fng[:, :], ALU.mult, ALU.mult
                                             ).then_inc(s_yn, 1)

            with dve.Fori(0, NM // 2) as i:
                for u in range(2):
                    finish_block(2 * i + u, u, False)
            finish_block(NM - 1, 0, True)

        @block.tensor
        def _(pe):
            pe.wait_ge(s_const, 16)
            pe.wait_ge(s_rows, 16 * 7)
            pe.transpose(bank[7][:, 0:C_ALL], rows, ident[0:C_ALL, 0:C_ALL]).then_inc(s_rowt, 1)
            pe.wait_ge(s_silc, 1)
            def ada_row(n):
                pe.wait_ge(s_wada[n % 2], 16 * (n // 2 + 1))
                for k in range(KT):
                    ins = pe.matmul(bank[6 + n % 2 if n < 4 else 7][0:2, :], silc[:, :, k], wada[n % 2 if n < 4 else 0][:, k, :],
                                    start=(k == 0), stop=(k == KT - 1))
                ins.then_inc(s_ada, 1)

            def turn_x(e):
                b, k = e // KT, e % KT
                tiles = BLOCKS[b][1] // P
                if k == 0:
                    pe.wait_ge(s_xn, BLOCKS[b][0] // P + tiles)
                if e >= 6:
                    pe.wait_ge(s_h32, e - 5)
                for s in range(tiles):
                    ins = pe.transpose(bank[e % 6][:, s * P:(s + 1) * P], x_tile(b, s)[:, k * P:(k + 1) * P], ident)
                ins.then_inc(s_xt, 1)

            ada_row(0)
            ada_row(1)
            for e in range(6):
                turn_x(e)
            for n in range(2, 4):
                pe.wait_ge(s_adar, n - 1)
                ada_row(n)
            pe.wait_ge(s_adar, 4)
            for j in range(16):
                ins = pe.transpose(bank[6][:, 2 * j:2 * j + 2], adarow[:, j * P:(j + 1) * P], ident[0:2, 0:2])
            ins.then_inc(s_adat, 1)
            turn_x(6)
            turn_x(7)
            ada_row(4)

            def unit_block(slot, b, a, out):
                t0, n = BLOCKS[b]
                sl = slice(P * slot, P * slot + P)
                for k in range(KT):
                    for w, h in ((w_hi, h_hi), (w_hi, h_lo), (w_lo, h_hi)):
                        ins = pe.matmul(bank[out][:, 0:n], w[0][:, k, sl], h[:, k, t0:t0 + n],
                                        start=(k == 0 and w is w_hi and h is h_hi), stop=(k == KT - 1 and w is w_lo))
                ins.then_inc(s_mm, 1)

            for b in range(NB):
                if b + 1 < NB:
                    for k in range(KT):
                        turn_x(KT * (b + 1) + k)
                if b == 0:
                    pe.wait_ge(s_gr, 1)
                    ada_row(5)
                if b == 1:
                    pe.wait_ge(s_wlo, 1)
                if b == 2:
                    pe.wait_ge(s_gr, 2)
                if b in (1, 2):
                    pe.wait_ge(s_hlo, low_parts(KT * b)[0])
                    pe.wait_ge(s_hld, low_parts(KT * b)[1])
                    unit_block(1, b - 1, b - 1, R_BANK[b - 1])
            pe.wait_ge(s_h32, KT * NB)
            pe.wait_ge(s_hlo, low_parts(KT * NB)[0])
            pe.wait_ge(s_hld, low_parts(KT * NB)[1])
            for b in range(2, NB):
                unit_block(1, b, b, R_BANK[b])
            for sec in range(2):
                with pe.Fori(0, 2) as i:
                    for u in range(2):
                        unit = 4 * sec + 2 * i + u
                        for b, (t0, n) in enumerate(BLOCKS):
                            e = NB * unit + b
                            def logits():
                                pe.wait_ge(s_now, 2 * sec + i + 1)
                                lag = 0 if (sec, u, b) == (0, 0, 0) else 1
                                pe.wait_ge(s_gabs, e - lag)
                                pe.wait_ge(s_gmin, e - lag)
                                pe.matmul(bank[5 + (NB * u + b) % 2][:, 0:n], walp_now[:, u, :], r_t[:, t0:t0 + n],
                                          start=True, stop=True).then_inc(s_g, 1)

                            if (sec, u, b) == (0, 0, 0):
                                pe.wait_ge(s_rlo, NB)
                            if u + b:
                                logits()
                            if b == 0:
                                pe.wait_ge(s_wlo, unit + 2)
                            pe.wait_ge(s_ev, A_QK + e - (NB - 1))
                            unit_block(u, b, A_QK + e, b)
                            if u + b == 0:
                                logits()
            pe.wait_ge(s_gabs, 8 * NB)
            pe.wait_ge(s_gmin, 8 * NB)
            with pe.Fori(0, 2) as i:
                for pair in range(2):
                    head = 2 * i + pair
                    pe.wait_ge(s_wlo, 11 + 2 * head)
                    for t in range(NT):
                        pe.wait_ge(s_ev, A_V + NT * head + t - 2)
                        for k in range(KT):
                            for h, w in ((h_hi, w_hi), (h_hi, w_lo), (h_lo, w_hi)):
                                ins = pe.matmul(bank[5 + t % 3][:, 0:DV], h[:, k, t * P:t * P + P], w[pair][:, k, :],
                                                start=(k == 0 and h is h_hi and w is w_hi), stop=(k == KT - 1 and h is h_lo))
                        ins.then_inc(s_mm, 1)
            with pe.Fori(0, 16) as i:
                for u in range(2):
                    m = 2 * i + u
                    pe.wait_ge(s_wlo, 18 + m)
                    for b in range(NB):
                        pe.wait_ge(s_ev, A_GA + NB * m + b - (NB - 1))
                        unit_block(u, b, A_GA + NB * m + b, b)
            pe.wait_ge(s_ev, A_END)

            def pe_head(head, n, i):
                landed = 16 * (i + 1)

                def turn(j):
                    way, c = TERMS[j]
                    pe.wait_ge(s_kin, NTERM * head + (max(j - 1, 0) if way == "b" else j))
                    pe.transpose(bank[turn_bank(j)][:, 0:P], kk[n][:, 1 if way == "b" else 0, c * P:c * P + P],
                                 ident).then_inc(s_tr, 1)

                def state_term(j):
                    pe.wait_ge(s_dt, NTERM * head + max(j - 1, 0))
                    pe.wait_ge(s_kin, NTERM * head + j + 1)
                    pe.matmul(bank[4 + j % 2][:, 0:DV], kin[:, j % 2, :], v_ld[n][:, TERMS[j][1], :], start=True, stop=True
                              ).then_inc(s_ds, 1)

                def scores(c):
                    pe.wait_ge(s_cb, NT * head + max(c - 1, 0))
                    for d in range(2):
                        ins = pe.matmul(bank[c % 2][:, d * P:d * P + P], kk[n][:, d, c * P:c * P + P],
                                        qd[n][:, d, c * P:c * P + P], start=True, stop=True)
                    ins.then_inc(s_sc, 1)

                def output(c):
                    out = bank[2 + c % 2][:, 0:DV]
                    pe.wait_ge(s_on, NT * head + max(c - 1, 0))
                    pe.wait_ge(s_pu, NTERM * head + (term["f", c - 1] + 1 if ("f", c - 1) in term else
                                                     term["f", c - 2] + 1 if c else B_TERMS))
                    pe.wait_ge(s_cb, NT * head + c + 1)
                    pe.matmul(out, comb[:, c % 2, :], v_ld[n][:, c, :], start=True, stop=False)
                    pe.matmul(out, qd[n][:, 0, c * P:c * P + P], state_f(n, c), start=False, stop=False)
                    pe.matmul(out, qd[n][:, 1, c * P:c * P + P], state_b(n, c), start=False, stop=True).then_inc(s_o, 1)

                def turn_output(c):
                    pe.wait_ge(s_gt, NT * head + c)
                    pe.wait_ge(s_on, NT * head + c + 1)
                    for e in range(2):
                        ins = pe.transpose(bank[7][:, e * P:e * P + P], on[:, c % 2, e * P:e * P + P], ident)
                    ins.then_inc(s_ot, 1)

                pe.wait_ge(s_cb, NT * head)
                pe.wait_ge(s_kl[n], landed)
                turn(0)
                if n == 0:
                    pe.wait_ge(s_v12, landed)
                else:
                    pe.wait_ge(s_vl[n], landed)
                pe.wait_ge(s_p0, i + 1)
                for j in range(B_TERMS):
                    if j + 1 < B_TERMS:
                        turn(j + 1)
                    if j == 4 and n == 0:
                        pe.wait_ge(s_vl[0], 2 * landed)
                    state_term(j)
                pe.wait_ge(s_ql[n], 2 * landed)
                turn(term["f", 0])
                scores(0)
                for c in range(NT):
                    if ("f", c + 1) in term:
                        turn(term["f", c + 1])
                    if c + 1 < NT:
                        scores(c + 1)
                    if ("f", c) in term:
                        state_term(term["f", c])
                    output(c)
                    if c:
                        turn_output(c - 1)
                turn_output(NT - 1)

            with pe.Fori(0, HEADS // 2) as i:
                for n in range(2):
                    pe_head(2 * i + n, n, i)
            pe.wait_ge(s_cb, NT * HEADS)
            pe.wait_ge(s_on, NT * HEADS)
            pe.wait_ge(s_dt, NTERM * HEADS)
            pe.wait_ge(s_ctab, 32)
            for g in range(GROUPS):
                for r in range(2):
                    ins = pe.matmul(bank[g // 2][:, 256 * (g % 2) + P * r:256 * (g % 2) + P * r + P], chan[:, r, :], w4[:, g, :],
                                    start=True, stop=True)
                if g % 2:
                    ins.then_inc(s_cwm, 1)
            pe.wait_ge(s_u, 16 * GROUPS)
            pe.wait_ge(s_ub, 6)
            pe.wait_ge(s_cw, 2)
            for m, t in enumerate(Z_ORDER):
                if m >= 3:
                    pe.wait_ge(s_z, m - 2)
                for g in range(GROUPS):
                    ins = pe.matmul(bank[2 * (m % 3) + g // 2][:, 256 * (g % 2):256 * (g % 2) + 256], uf[:, g, t * P:t * P + P],
                                    cw[:, g, :, :].rearrange("p r c -> p (r c)"), start=True, stop=True)
                ins.then_inc(s_zm, 1)
            pe.wait_ge(s_gt, NT * HEADS)
            pe.wait_ge(s_ftab, 32)
            pe.wait_ge(s_z, NT)
            for g in range(GROUPS):
                for n in range(4):
                    t, r = n // 2, n % 2
                    ins = pe.matmul(bank[6 + g // 2][:, 256 * (g % 2):256 * (g % 2) + 256], zb[:, LT + t, r, g * P:g * P + P],
                                    dft_c[:, r, t, :], start=(n == 0), stop=(n == 3))
            ins.then_inc(s_cx, 1)
            for c in range(4):
                if c < 3:
                    pe.wait_ge(s_l4, c + 1)
                else:
                    pe.wait_ge(s_p4, 1)
                if c:
                    pe.wait_ge(s_fo, 1 if c == 1 else 1 + 4 * (c - 1))
                for d in range(4):
                    for g in range(GROUPS):
                        for r in range(2):
                            ins = pe.matmul(bank[4 * (c % 2) + d][:, g * P:g * P + P], sb[:, 4 * c + d, r, g * P:g * P + P],
                                            dft[:, r, c + 4 * d, :], start=(r == 0), stop=(r == 1))
                    ins.then_inc(s_f, 1)

            def split_product(out, pairs, count, ready=None):
                for k, (st, mv) in enumerate(pairs):
                    if ready:
                        pe.wait_ge(ready, k + 1)
                    for p, (a, b) in enumerate(((0, 0), (0, 1), (1, 0))):
                        ins = pe.matmul(out, st[a], mv[b], start=(k == 0 and p == 0), stop=(k == count - 1 and p == 2))
                return ins

            pe.wait_ge(s_pwp, len(LOW_POOL))

            def branch_block(b, slot):
                pe.wait_ge(s_il, 3 * b + 3)
                for j in range(8):
                    pe.wait_ge(s_yg, 8 * b + j + 1)
                    for a, ks in enumerate((range(0, KT), range(KT, KA))):
                        ins = split_product(bank[j][:, a * MB:a * MB + MB],
                                            [((pw_hi[:, k, j * P:j * P + P], pw_lo[:, k, j * P:j * P + P]),
                                              (in_hi[slot][:, k, :], in_lo[slot][:, k, :])) for k in ks], len(ks))
                    ins.then_inc(s_y, 1)

            with pe.Fori(0, NM // 2) as i:
                for u in range(2):
                    branch_block(2 * i + u, u)
            branch_block(NM - 1, 0)

            pe.wait_ge(s_yg, 8 + 8 * NM)

            def out_tiles(b, slot, first=False):
                pe.wait_ge(s_ml, b + 1)
                for u in range(2):
                    pe.wait_ge(s_og3, 2 * b + u + 1)
                    for h in range(2):
                        ins = split_product(bank[4 * slot + 2 * u + h][:, :],
                                            [((me_hi[slot][:, k, u * P:u * P + P], me_lo[slot][:, k, u * P:u * P + P]),
                                              (ow_hi[:, k, 512 * h:512 * h + 512], ow_lo[:, k, 512 * h:512 * h + 512]))
                                             for k in range(KT)], KT, s_owl if first and u == h == 0 else None)
                    ins.then_inc(s_out, 1)

            out_tiles(0, 0, first=True)
            out_tiles(1, 1)
            with pe.Fori(1, NM // 2) as i:
                for u in range(2):
                    out_tiles(2 * i + u, u)
            out_tiles(NM - 1, 0)
    return nc


def constants():
    c = np.zeros((P, K_ALL), np.float32)
    c[:, K_ID:K_ID + P] = np.eye(P)
    c[:, K_UP:K_UP + P] = np.triu(np.ones((P, P)), 1)
    c[:, K_DW:K_DW + P] = 1 + np.eye(P)
    c[:, K_ONE:K_ONE + P] = 1
    return c


CHANNELS = np.arange(DK).reshape(2, 2, DK // 4).transpose(1, 0, 2).ravel()


def rope_tables():
    f = DK // 4
    freqs = np.float32(10000.0) ** (-np.arange(f, dtype=np.float32) / f)
    t = np.arange(LAT)
    out = np.zeros((P, 2, TOK), np.float32)
    out[:, 0, LAT:] = 1
    for a, at in enumerate((t // 64, t % 64)):
        ang = freqs[:, None] * at[None].astype(np.float32)
        for half in range(2):
            rows = slice(64 * half + 32 * a, 64 * half + 32 * a + 32)
            out[rows, 0, :LAT] = np.cos(ang)
            out[rows, 1, :LAT] = np.sin(ang) * (1 if half else -1)
    return out


def fourier_tables():
    n = np.arange(P)
    ang = 2 * np.pi * np.outer(n, n) / P
    chan = np.stack([np.cos(ang), -np.sin(ang)], 1)
    k = N1 * n[None, :] + np.arange(N1)[:, None]
    ang = 2 * np.pi * (n[:, None, None] * k[None] % LAT) / LAT
    dft = np.stack([np.cos(ang), np.sin(ang)], 1) / np.sqrt(LAT * P)
    t = np.arange(CTX).reshape(CTX // P, P).T
    ang = 2 * np.pi * (t[:, :, None] * np.arange(CTX) % CTX) / CTX
    dft_c = np.stack([np.cos(ang), np.sin(ang)], 1) / np.sqrt(CTX * P)
    return {"chan": chan.astype(np.float32), "dft": dft.astype(np.float32), "dft_c": dft_c.astype(np.float32)}


def layout(a):
    w_in = a["w_in"][0]
    ranks = 2 * HEADS * DK + 2 * HEADS * DV
    order = np.concatenate([ranks + np.arange(P) % (2 * RANK), np.arange(ranks), np.arange(ranks + 2 * RANK, w_in.shape[1])])
    heads = (np.arange(2 * HEADS)[:, None] * DK + CHANNELS).ravel()
    order[P:P + 2 * HEADS * DK] = heads
    tiles = lambda w, c: w.reshape(w.shape[0] // P, P, -1, c).transpose(2, 1, 0, 3)
    return {
        "consts": constants(), "rope": rope_tables(), **fourier_tables(),
        "w_four": a["w_four"][0].transpose(1, 0, 2), "b_gate": a["b_ada"][:, 2 * D:], "final_norm_g": a["final_norm_g"][None],
        "w_proj_a": a["w_proj_a"][0].reshape(KT, P, D), "w_proj_b": a["w_proj_b"][0].reshape(GROUPS, P, D),
        "w_out": a["w_out"][0].reshape(KT, P, D),
        "state_fwd": a["state_gla_fwd"][0, 0][:, CHANNELS], "state_bwd": a["state_gla_bwd"][0, 0][:, CHANNELS],
        "x": np.concatenate([a["x_sample"][0], a["x_prompt"][0]]),
        "c": a["c"].reshape(8, P), "c_ctx": a["c_ctx"].reshape(8, P), "norm_g": a["norm_g"].reshape(8, P),
        "b_ada": a["b_ada"].reshape(24, P), "gla_norm_g": a["gla_norm_g"].reshape(2, P),
        "b_alpha_fwd": a["b_alpha_fwd"].reshape(4, P)[:, CHANNELS], "b_alpha_bwd": a["b_alpha_bwd"].reshape(4, P)[:, CHANNELS],
        "w_ada": tiles(a["w_ada"][0], 512),
        "w_in": tiles(w_in[:, order], P),
        "w_alpha_fwd": a["w_alpha_fwd"].reshape(RANK, 4, P)[:, :, CHANNELS],
        "w_alpha_bwd": a["w_alpha_bwd"].reshape(RANK, 4, P)[:, :, CHANNELS],
    }


OUTS = {"y": (TOK, D), "new_fwd": (HEADS, DK, DV), "new_bwd": (HEADS, DK, DV)}


def kernel(**inputs):
    import concourse.bacc as bacc
    from concourse.bass_utils import run_bass_kernel_spmd

    nc = bacc.Bacc("TRN2", target_bir_lowering=False, num_devices=1)
    arrays = {"in_" + k: np.ascontiguousarray(v) for k, v in layout({k: np.asarray(v) for k, v in inputs.items()}).items()}
    io = {k[3:]: nc.dram_tensor(k, v.shape, mybir.dt.from_np(v.dtype), kind="ExternalInput").ap() for k, v in arrays.items()}
    for k, shape in OUTS.items():
        io[k] = nc.dram_tensor(k, shape, F32, kind="ExternalOutput").ap()
    build(nc, io, lambda name, shape: nc.dram_tensor(name, shape, F32, kind="Internal").ap())
    out = run_bass_kernel_spmd(nc, [arrays], core_ids=[0]).results[0]
    y = out["y"]
    return (y[LAT:][None], y[:LAT][None], out["new_fwd"][:, CHANNELS][None, None], out["new_bwd"][:, CHANNELS][None, None])
```
